# Optimizing a Trainium2 kernel written in Bass

```python
import jax, jax.numpy as jnp
from jax import lax
import numpy as np

D_MODEL = 1024
BATCH = 1
SEQ = 128
DEPTH = 2
DEC_BATCH = 1
DEC_SEQ = 1024
PAST_LEN = 128

GRID_W = 64
EPS = 1e-6
N_BRANCH = 3
FN_WIDTH = D_MODEL // 4
FN_GROUPS = 4
POOL_WINDOWS = (2, 4, 8, 16)
POOL_WIDTH = D_MODEL // 4
POOL_GC = POOL_WIDTH // len(POOL_WINDOWS)
N_HEADS = 8
QK_NOPE = D_MODEL // 16
QK_ROPE = D_MODEL // 32
V_DIM = D_MODEL // 16
Q_RANK = D_MODEL // 4
KV_RANK = D_MODEL // 8
ATT_WIDTH = N_HEADS * V_DIM
ROPE_THETA = 10000.0
Q_BLOCK = 128
IN_SIZES = (FN_WIDTH, FN_WIDTH, POOL_WIDTH, POOL_WIDTH, Q_RANK, KV_RANK, QK_ROPE, ATT_WIDTH, N_BRANCH * D_MODEL)
IN_WIDTH = sum(IN_SIZES)

kernel_name = "hybrid_fourier_pool_mla_diffusion_step"

def _rmsnorm(x, g):
    xf = x.astype(jnp.float32)
    r = lax.rsqrt(jnp.mean(xf * xf, axis=-1, keepdims=True) + EPS)
    return (xf * r).astype(x.dtype) * g

def _split_cols(p):
    parts, off = [], 0
    for s in IN_SIZES:
        parts.append(p[..., off:off + s])
        off += s
    return parts

def _axial_rope(L, dtype):
    rows = L // GRID_W
    t = jnp.arange(L)
    row = jnp.repeat(jnp.arange(rows), GRID_W).astype(jnp.float32)
    col = (t % GRID_W).astype(jnp.float32)
    half = QK_ROPE // 2
    freqs = ROPE_THETA ** (-jnp.arange(0, half, 2, dtype=jnp.float32) / half)
    ar = row[:, None] * freqs
    ac = col[:, None] * freqs
    cos = jnp.concatenate([jnp.cos(ar), jnp.cos(ar), jnp.cos(ac), jnp.cos(ac)], axis=-1)
    sin = jnp.concatenate([jnp.sin(ar), jnp.sin(ar), jnp.sin(ac), jnp.sin(ac)], axis=-1)
    return cos.astype(dtype), sin.astype(dtype)

def _rot_half(x):
    h = x.shape[-1] // 2
    return jnp.concatenate([-x[..., h:], x[..., :h]], axis=-1)

def _apply_rope(x, cos, sin):
    half = QK_ROPE // 2
    rx = jnp.concatenate([_rot_half(x[..., :half]), _rot_half(x[..., half:])], axis=-1)
    return x * cos + rx * sin

def _fourier_mix(u):
    B, L, _ = u.shape
    ug = u.reshape(B, L, FN_GROUPS, FN_WIDTH // FN_GROUPS).astype(jnp.float32)
    f = jnp.fft.fft2(ug, axes=(1, 3), norm="ortho").real
    return f.reshape(B, L, FN_WIDTH).astype(u.dtype)

def _pool_mix(u, pool_w, pool_scale):
    B, L, _ = u.shape
    uf = u.astype(jnp.float32)
    cs = jnp.concatenate([jnp.zeros((B, 1, POOL_WIDTH), jnp.float32), jnp.cumsum(uf, axis=1)], axis=1)
    t = jnp.arange(L)
    outs = []
    for gi, w in enumerate(POOL_WINDOWS):
        left = w // 2
        right = w - 1 - left
        lo = jnp.clip(t - left, 0, L - 1)
        hi = jnp.clip(t + right, 0, L - 1)
        cnt = (hi - lo + 1).astype(jnp.float32)
        csg = cs[..., gi * POOL_GC:(gi + 1) * POOL_GC]
        outs.append((csg[:, hi + 1] - csg[:, lo]) / cnt[None, :, None])
    pooled = (jnp.concatenate(outs, axis=-1) - uf).astype(u.dtype)
    pg = pooled.reshape(B, L, len(POOL_WINDOWS), POOL_GC)
    mixed = jnp.einsum('blgc,gcd->blgd', pg, pool_w).reshape(B, L, POOL_WIDTH)
    return mixed * pool_scale

def _block_attention(q, k, v):
    B, Lq, H, Dq = q.shape
    nb = Lq // Q_BLOCK
    qb = q.reshape(B, nb, Q_BLOCK, H, Dq).transpose(1, 0, 2, 3, 4)
    scale = Dq ** -0.5

    def one(qblk):
        s = jnp.einsum('bqhd,bkhd->bhqk', qblk, k, preferred_element_type=jnp.float32) * scale
        p = jax.nn.softmax(s, axis=-1).astype(v.dtype)
        return jnp.einsum('bhqk,bkhd->bqhd', p, v)

    o = lax.map(one, qb)
    return o.transpose(1, 0, 2, 3, 4).reshape(B, Lq, H, v.shape[-1])

def _layer(h, mod, w, rope, ctx):
    B, L, _ = h.shape
    shift, scale, gate = jnp.split(mod, 3, axis=-1)
    xn = _rmsnorm(h, w['norm_g']) * (1.0 + scale[..., None, :]) + shift[..., None, :]
    a_in, a_z, b_in, b_z, q_lat, kv_lat, k_rope, c_z, g_all = _split_cols(xn @ w['w_in'])

    ya = (_fourier_mix(a_in) * jax.nn.silu(a_z)) @ w['w_br_a']
    yb = (_pool_mix(b_in, w['pool_w'], w['pool_scale']) * jax.nn.silu(b_z)) @ w['w_br_b']

    q = (_rmsnorm(q_lat, w['q_norm_g']) @ w['w_q_up']).reshape(B, L, N_HEADS, QK_NOPE + QK_ROPE)
    q_nope, q_rope = q[..., :QK_NOPE], q[..., QK_NOPE:]
    ckv = _rmsnorm(kv_lat, w['kv_norm_g'])
    if rope is not None:
        cos, sin = rope
        q_rope = _apply_rope(q_rope, cos[:, None, :], sin[:, None, :])
        k_rope_p = _apply_rope(k_rope, cos, sin)
    else:
        k_rope_p = k_rope
    q_full = jnp.concatenate([q_nope, q_rope], axis=-1)
    if ctx is not None:
        ckv_all = jnp.concatenate([ckv, ctx[0]], axis=1)
        kr_all = jnp.concatenate([k_rope_p, ctx[1]], axis=1)
    else:
        ckv_all, kr_all = ckv, k_rope_p
    Lk = ckv_all.shape[1]
    kv = (ckv_all @ w['w_kv_up']).reshape(B, Lk, N_HEADS, QK_NOPE + V_DIM)
    k_nope, v = kv[..., :QK_NOPE], kv[..., QK_NOPE:]
    k = jnp.concatenate([k_nope, jnp.broadcast_to(kr_all[:, :, None, :], (B, Lk, N_HEADS, QK_ROPE))], axis=-1)
    o = _block_attention(q_full, k, v).reshape(B, L, ATT_WIDTH)
    yc = (o * jax.nn.silu(c_z)) @ w['w_br_c']

    g = jax.nn.sigmoid(g_all).reshape(B, L, N_BRANCH, D_MODEL)
    y = g[:, :, 0] * ya + g[:, :, 1] * yb + g[:, :, 2] * yc
    h_new = h + gate[..., None, :] * (y @ w['w_out'])
    return h_new, ckv, k_rope

def setup_inputs(seed: int = 0) -> dict:
    key = jax.random.key(seed)
    ks = jax.random.split(key, 24)
    f32 = jnp.float32

    def nrm(k, shape, s):
        return jax.random.normal(k, shape, f32) * s

    return {
        'x_prompt': nrm(ks[0], (BATCH, SEQ, D_MODEL), 1.0),
        'x_sample': nrm(ks[1], (DEC_BATCH, DEC_SEQ, D_MODEL), 1.0),
        'cache_ckv': nrm(ks[2], (DEC_BATCH, DEPTH, PAST_LEN, KV_RANK), 1.0),
        'cache_krope': nrm(ks[3], (DEC_BATCH, DEPTH, PAST_LEN, QK_ROPE), 1.0),
        'c': nrm(ks[4], (DEC_BATCH, D_MODEL), 1.0),
        'c_ctx': nrm(ks[5], (D_MODEL,), 1.0),
        'norm_g': 1.0 + nrm(ks[6], (DEPTH, D_MODEL), 0.02),
        'w_mod': nrm(ks[7], (DEPTH, D_MODEL, 3 * D_MODEL), 0.5 * D_MODEL ** -0.5),
        'b_mod': nrm(ks[8], (DEPTH, 3 * D_MODEL), 0.01),
        'w_in': nrm(ks[9], (DEPTH, D_MODEL, IN_WIDTH), D_MODEL ** -0.5),
        'pool_w': nrm(ks[10], (DEPTH, len(POOL_WINDOWS), POOL_GC, POOL_GC), POOL_GC ** -0.5),
        'pool_scale': 1.0 + nrm(ks[11], (DEPTH, POOL_WIDTH), 0.02),
        'q_norm_g': 1.0 + nrm(ks[12], (DEPTH, Q_RANK), 0.02),
        'w_q_up': nrm(ks[13], (DEPTH, Q_RANK, N_HEADS * (QK_NOPE + QK_ROPE)), Q_RANK ** -0.5),
        'kv_norm_g': 1.0 + nrm(ks[14], (DEPTH, KV_RANK), 0.02),
        'w_kv_up': nrm(ks[15], (DEPTH, KV_RANK, N_HEADS * (QK_NOPE + V_DIM)), KV_RANK ** -0.5),
        'w_br_a': nrm(ks[16], (DEPTH, FN_WIDTH, D_MODEL), FN_WIDTH ** -0.5),
        'w_br_b': nrm(ks[17], (DEPTH, POOL_WIDTH, D_MODEL), POOL_WIDTH ** -0.5),
        'w_br_c': nrm(ks[18], (DEPTH, ATT_WIDTH, D_MODEL), ATT_WIDTH ** -0.5),
        'w_out': nrm(ks[19], (DEPTH, D_MODEL, D_MODEL), D_MODEL ** -0.5),
        'final_norm_g': 1.0 + nrm(ks[20], (D_MODEL,), 0.02),
    }

def reference(x_prompt, x_sample, cache_ckv, cache_krope, c, c_ctx, norm_g, w_mod, b_mod, w_in, pool_w,
              pool_scale, q_norm_g, w_q_up, kv_norm_g, w_kv_up, w_br_a, w_br_b, w_br_c, w_out, final_norm_g):
    rope = _axial_rope(x_sample.shape[1], x_sample.dtype)
    hp, hs = x_prompt, x_sample
    ckv_list, kr_list = [], []
    for l in range(DEPTH):
        w = {'norm_g': norm_g[l], 'w_in': w_in[l], 'pool_w': pool_w[l], 'pool_scale': pool_scale[l],
             'q_norm_g': q_norm_g[l], 'w_q_up': w_q_up[l], 'kv_norm_g': kv_norm_g[l], 'w_kv_up': w_kv_up[l],
             'w_br_a': w_br_a[l], 'w_br_b': w_br_b[l], 'w_br_c': w_br_c[l], 'w_out': w_out[l]}
        mod_ctx = jax.nn.silu(c_ctx) @ w_mod[l] + b_mod[l]
        mod_lat = jax.nn.silu(c) @ w_mod[l] + b_mod[l]
        hp, ckv_l, kr_l = _layer(hp, mod_ctx, w, None, None)
        ckv_list.append(ckv_l)
        kr_list.append(kr_l)
        hs, _, _ = _layer(hs, mod_lat, w, rope, (cache_ckv[:, l], cache_krope[:, l]))
    y_prompt = _rmsnorm(hp, final_norm_g)
    y_sample = _rmsnorm(hs, final_norm_g)
    new_ckv = jnp.stack(ckv_list, axis=1)
    new_krope = jnp.stack(kr_list, axis=1)
    return (y_prompt, y_sample, new_ckv, new_krope)


_drawn_inputs = setup_inputs


def setup_inputs(seed=0):
    import zlib

    import numpy as np

    out = dict(_drawn_inputs(seed))
    spreads = {}
    factors = {'cache_ckv': 8.0,
     'cache_krope': 8.0,
     'norm_g': 2.944,
     'b_mod': 3.979,
     'pool_scale': 8.0,
     'q_norm_g': 8.0,
     'w_q_up': 2.746,
     'kv_norm_g': 2.918,
     'final_norm_g': 2.947}
    for name, (base, spread) in spreads.items():
        noise = np.random.default_rng([zlib.crc32(name.encode()), seed]).standard_normal(out[name].shape)
        drawn = base * np.exp(spread * noise) if base else spread * noise
        out[name] = __import__('jax').numpy.asarray(drawn.astype(out[name].dtype))
    for name, factor in factors.items():
        out[name] = (out[name] * factor).astype(out[name].dtype)
    return out
```

```python
import numpy as np

from concourse import mybir
from concourse.alu_op_type import AluOpType as ALU

F32 = mybir.dt.float32
F32R = mybir.dt.float32r
ACT = mybir.ActivationFunctionType
AX = mybir.AxisListType

P = 128
D = 1024
DEPTH = 2
SEQ = 128
LAT = 1024
PAST = 128
TOK = LAT + SEQ
TT = TOK // P
KF = D // P
CH = 384
NCH = TOK // CH
CT = CH // P
HEADS = 8
NOPE, ROPE, VDIM = 64, 32, 64
QR, KVR = 256, 128
KEYS = LAT + PAST + SEQ
KS = KEYS // P
EPS = 1e-6
GRID_W = 64
WINDOWS = (2, 4, 8, 16)
COL_AIN, COL_AZ, COL_BIN, COL_BZ, COL_Q, COL_KV, COL_CZ, COL_G = 0, 256, 512, 768, 1024, 1280, 1440, 1952
TOK_COLS = (COL_AIN, COL_Q, COL_CZ - 256)
FEAT_COLS = tuple(COL_BIN + P * i for i in range(2)) + tuple(COL_AZ + P * i for i in range(2)) \
    + tuple(COL_BZ + P * i for i in range(2)) + tuple(COL_CZ + P * i for i in range(4))
PAD = 8
SAMPLE0, PROMPT0, POOLW = PAD, PAD + LAT + 2 * PAD, LAT + SEQ + 4 * PAD
KVW = 224


def make_tables():
    n = np.arange(P)
    def cs(r, length, scale):
        ang = 2 * np.pi * ((n[:, None] * (8 * n[None, :] + r)) % length) / length if length == LAT \
            else 2 * np.pi * ((n[:, None] * n[None, :]) % length) / length
        return np.cos(ang) * scale, np.sin(ang) * scale
    big, small = 1 / np.sqrt(LAT * 64.0), 1 / np.sqrt(SEQ * 64.0)
    dft = []
    for r in (1, 2, 3):
        c, s = cs(r, LAT, big)
        dft.append(np.concatenate([c, -s], 1))
    for r in (1, 2, 3):
        c, s = cs(r, LAT, big)
        dft.append(np.concatenate([s, c], 1))
    for r in (0, 4):
        c, s = cs(r, LAT, big)
        dft.append(np.concatenate([c, -s], 1))
    c, s = cs(0, SEQ, small)
    dft.append(np.concatenate([c, -s], 1))
    seq_dft = np.stack(dft, 1)
    m = np.arange(64)
    ang = 2 * np.pi * ((m[:, None] * m[None, :]) % 64) / 64
    chan = np.zeros((P, 3, P))
    for g in (0, 64):
        chan[g:g + 64, 0, g:g + 64] = np.cos(ang)
        chan[g:g + 64, 1, g:g + 64] = np.sin(ang)
        chan[g:g + 64, 2, g:g + 64] = -np.sin(ang)
    half = ROPE // 2
    freqs = (10000.0 ** (-np.arange(0, half, 2, dtype=np.float32) / half)).astype(np.float32)
    t = np.arange(LAT)
    ar = (t // GRID_W).astype(np.float32)[:, None] * freqs
    ac = (t % GRID_W).astype(np.float32)[:, None] * freqs
    cos = np.concatenate([np.cos(ar), np.cos(ar), np.cos(ac), np.cos(ac)], 1)
    sin = np.concatenate([np.sin(ar), np.sin(ar), np.sin(ac), np.sin(ac)], 1)
    sign = np.tile(np.r_[-np.ones(8), np.ones(8)], 2)
    rope_rows = np.stack([cos.reshape(8, P, ROPE), (sin * sign).reshape(8, P, ROPE)]).transpose(2, 0, 1, 3)
    q_scale = np.zeros((P, TOK))
    q_scale[:NOPE + ROPE] = 1.0
    q_scale[NOPE:NOPE + ROPE, :LAT] = cos.T
    q_scale[NOPE + ROPE:, :LAT] = sin.T
    q_scale *= (NOPE + ROPE) ** -0.5
    edge = np.ones((P, 2, 4, PAD))
    for g, w in enumerate(WINDOWS):
        rows = slice(64 * (g % 2), 64 * (g % 2) + 64)
        for e, (start, length) in enumerate(((0, LAT), (LAT - PAD, LAT), (0, SEQ), (SEQ - PAD, SEQ))):
            pos = start + np.arange(PAD)
            lo = np.clip(pos - w // 2, 0, length - 1)
            hi = np.clip(pos + w - 1 - w // 2, 0, length - 1)
            edge[rows, g // 2, e] = w / (hi - lo + 1.0)
    return {"seq_dft": seq_dft, "chan_dft": chan, "rope_rows": rope_rows, "q_scale": q_scale,
            "edge": edge, "ident": np.eye(P), "vec_zero": np.zeros((P, 2, P))}


def bank_plan():
    phases = []
    def add(layer, name, first, banks, count):
        phases.append(((layer, name), first, banks, count))
    add(0, "vec", 6, 1, 1)
    add(0, "mod", 6, 2, 8)
    add(0, "norm", 6, 2, NCH * KF)
    for l in range(DEPTH):
        add(l, "tok", 0, 3, 3 * TT)
        add(l, "feat", 0, 6, 3 * len(FEAT_COLS))
        add(l, "turn", 6, 2, 14)
        add(l, "val", 6, 2, KS)
        add(l, "pool", 0, 6, 6)
        add(l, "seq", 6, 2, 12)
        add(l, "chan", 0, 6, 6)
        add(l, "attn", 6, 2, HEADS * head_items(l) + 16)
        add(l, "gate", 0, 3, 3 * 3 * KF)
        add(l, "branch", 3, 3, 3 * 3 * KF)
        add(l, "gbc", 6, 2, 4)
        add(l, "out", 0, 6, 4 * TT)
        if l + 1 < DEPTH:
            add(l + 1, "norm", 6, 2, NCH * KF)
    used = [0] * 8
    plan = {}
    for key, first, banks, count in phases:
        plan[key] = (first, banks, [used[first + i] for i in range(banks)])
        for i in range(banks):
            used[first + i] += len(range(i, count, banks))
    return plan


AQ, AK, AT, AM = 0, 3, 6, 31


def head_items(layer):
    return AM + (layer + 1 < DEPTH)


def head_item(layer, pair, u, n):
    return pair * (2 * head_items(layer) + 4) + u * head_items(layer) + n


def hybrid_step(nc, x_prompt, x_sample, cache_ckv, cache_krope, c, c_ctx, norm_g, w_mod, b_mod, w_in,
                pool_w, pool_scale, q_norm_g, w_q_up, kv_norm_g, w_kv_up, w_br_a, w_br_b, w_br_c,
                w_out, final_norm_g, tab, y_prompt, y_sample, new_ckv, new_krope, park_hi, park_lo, rows_mid):
    plan = bank_plan()

    base = 16512
    class Region:
        def __init__(self, start, size):
            self.at, self.end = start, start + size
        def put(self, name, shape, dt=F32):
            t = nc.alloc_sbuf_tensor_at(name, [P] + shape, dt, offset=self.at)
            self.at += (4 * int(np.prod(shape)) + 31) // 32 * 32
            assert self.at <= self.end, name
            return t

    SZ_BR, SZ_RAW, SZ_XY, SZ_R2, SZ_WS, SZ_S = 36864, 16384, 73728, 36864, 16384, 17408
    at = base
    starts = {}
    for name, size in (("br", SZ_BR), ("raw", SZ_RAW), ("xy", SZ_XY), ("r2", SZ_R2), ("ws", SZ_WS), ("s", SZ_S)):
        starts[name] = (at, size)
        at += size
    def region(name):
        return Region(*starts[name])
    const = Region(at, 229344 - at)

    ident = const.put("ident", [P])
    ones = const.put("ones", [P])
    q_scale = const.put("q_scale", [TOK])
    rope = const.put("rope", [2, 8, ROPE])
    edge = const.put("edge", [2, 4, PAD])
    pool_mat = const.put("pool_mat", [2, P])
    modT = const.put("modT", [2, 24, 2])
    scaleT = const.put("scaleT", [KF, 2])
    vecT = const.put("vecT", [84])
    silu_c = const.put("silu_c", [KF, 2])
    gq_rows = const.put("gq_rows", [QR])
    gkv_rows = const.put("gkv_rows", [KVR])
    ssq = const.put("ssq", [CT])
    root = const.put("root", [CT])
    rinv = const.put("rinv", [CT])
    lat_ssq = const.put("lat_ssq", [2 * TT])
    lat_root = const.put("lat_root", [2 * TT])
    lat_rinv = const.put("lat_rinv", [2 * TT])
    negmax = const.put("negmax", [2])
    rowsum = const.put("rowsum", [2])
    rsinv = const.put("rsinv", [2])
    rot_tmp = const.put("rot_tmp", [8, ROPE])

    BR = region("br").put("branch", [KF, TOK])
    bs = region("br").put("split_br", [4, 2, KF, P], F32R)
    raw = region("raw").put("raw", [4, KF, P])
    r = region("xy")
    XH = r.put("xn_high", [KF, TOK], F32R)
    XL = r.put("xn_low", [KF, TOK], F32R)
    r = region("xy")
    qhatT = r.put("qhatT", [2, TOK])
    V = r.put("values", [KS, HEADS * VDIM])
    kT = r.put("kT", [2, KEYS])
    qT = r.put("qT", [2, TOK])
    seq_dft = r.put("seq_dft", [9, 2 * P])
    chan_dft = r.put("chan_dft", [3, P])
    win_at = r.at
    XR = r.put("spectrum", [2, 2, 6, P])
    r = Region(win_at, 2 * 4 * POOLW)
    winA = r.put("winA", [POOLW])
    winB = r.put("winB", [POOLW])
    H = region("r2").put("rows", [TT, D])
    Y = region("r2").put("merged", [KF, TOK])
    r = region("r2")
    atok = r.put("fourier_in", [TT, 256])
    qlat = r.put("qlat", [TT, QR])
    kvk = r.put("kvk", [KS, KVW])
    binp = r.put("pool_in", [2, POOLW])
    r = region("r2")
    probs = r.put("probs", [2, TOK])
    probsT = r.put("probsT", [2, TT, P])
    O = r.put("heads_out", [2, TT, P])
    ws = region("ws").put("split_ws", [2, 2, KF, P], F32R)
    r = region("ws")
    dft_sd = r.put("dft_sd", [8, 256])
    U = r.put("dft_u", [8, 256])
    r = region("ws")
    gateB = r.put("gate_rows", [2, D])
    finalB = r.put("final_rows", [D])
    tmpw = r.put("tmpw", [2, 256])
    r = region("s")
    wq_raw = r.put("wq_raw", [2, HEADS * (NOPE + ROPE)])
    wkv = r.put("wkv", [HEADS * P])
    ckvT = r.put("ckvT", [KEYS])
    wq = r.put("wq_head", [2, 2, P])
    r = region("s")
    xhat = r.put("xhat", [CT, D])
    vtmp = r.put("xn_value", [3, CH])
    r = region("s")
    sig = r.put("sigmoids", [3, CH])
    prod = r.put("products", [2, CH])
    r = region("s")
    diag = r.put("diag", [2, 4, P])
    vec_rows = region("br").put("vec_rows", [P])

    PS = nc.alloc_psum_tensor("ps", [P, 8, 512], F32)

    sems = {}
    def S(name):
        if name not in sems:
            sems[name] = nc.alloc_semaphore(name)
        return sems[name]
    bank_full = [S(f"bank_full{b}") for b in range(8)]
    bank_free = [S(f"bank_free{b}") for b in range(8)]
    raw_in = [S(f"raw_in{s}") for s in range(4)]

    def item(l, phase, n):
        first, banks, start = plan[(l, phase)]
        return first + n % banks, start[n % banks] + n // banks

    def pe_takes(pe, l, phase, n):
        b, use = item(l, phase, n)
        if use:
            pe.wait_ge(bank_free[b], use)
        return b

    def filled(eng, l, phase, n):
        b, use = item(l, phase, n)
        eng.wait_ge(bank_full[b], use + 1)
        return b

    def read_out(eng, l, phase, n):
        b, use = item(l, phase, n)
        eng.wait_ge(bank_free[b], use + 1)

    units = []
    unit_at = {}
    def unit(key, srcs, split, release):
        unit_at[key] = len(units)
        units.append((srcs, split, release))
    n_split = 0
    split_plan = []
    last_in = {}
    def split_unit(key, srcs, dest, release):
        nonlocal n_split
        unit(key, srcs, n_split, None)
        split_plan.append((unit_at[key], dest, last_in.get(dest)))
        last_in[dest] = release
        n_split += 1
    def wcols(w, l, c0):
        return w[l].rearrange("(k p) n -> p k n", p=P)[:, :, c0:c0 + P]
    WS0, WS1 = 0, 1
    for m in range(24):
        unit(("mod", 0, m), [(0, KF, wcols(w_mod, 0, m * P))], None, (0, "mod", m // 3))
    for l in range(DEPTH):
        for p in range(3):
            for u in range(2):
                split_unit(("tok", l, 2 * p + u), [(0, KF, wcols(w_in, l, TOK_COLS[p] + u * P))],
                           2 * p + u, (l, "tok", p * TT + TT - 1))
        for u, c0 in enumerate(FEAT_COLS):
            split_unit(("feat", l, u), [(0, KF, wcols(w_in, l, c0))], u % 2, (l, "feat", 3 * u + 2))
        if l + 1 < DEPTH:
            for m in range(24):
                h = m // 3
                unit(("mod", l + 1, m), [(0, KF, wcols(w_mod, l + 1, m * P))], None,
                     (l, "attn", head_item(l, h // 2, h % 2, AM)))
        for j in range(KF):
            for b in range(3):
                split_unit(("gate", l, 3 * j + b), [(0, KF, wcols(w_in, l, COL_G + b * D + j * P))],
                           (3 * j + b) % 2, (l, "gate", (3 * j + b) * 3 + 2))
            unit(("branch", l, j), [(0, 2, wcols(w_br_a, l, j * P)), (2, 4, wcols(w_br_b, l, j * P)),
                                    (4, 8, wcols(w_br_c, l, j * P))], None, (l, "branch", (3 * j + 2) * 3 + 2))
        for u in range(8):
            split_unit(("out", l, u), [(0, KF, wcols(w_out, l, u * P))], 2 + u % 4,
                       (l, "out", (u // 2) * TT + TT - 1))
    arrivals = [0] * 4
    arrived_at = []
    for n, (srcs, _, _) in enumerate(units):
        arrivals[n % 4] += 16 * len(srcs)
        arrived_at.append(arrivals[n % 4])
    def split_dest(d):
        return ws[:, d] if d < 2 else bs[:, d - 2]
    split_no = {u: k for k, (u, _, _) in enumerate(split_plan)}
    split_k = {key: split_no[n] for key, n in unit_at.items() if n in split_no}

    def arrived(eng, n):
        eng.wait_ge(raw_in[n % 4], arrived_at[n])

    def load_units(sp, lo, hi):
        for n in range(lo, hi):
            srcs = units[n][0]
            if n >= 4:
                _, k, release = units[n - 4]
                if k is not None:
                    sp.wait_ge(S("split_low"), k + 1)
                else:
                    filled(sp, *release)
            for k0, k1, src in srcs:
                sp.dma_start(raw[:, n % 4, k0:k1, :], src).then_inc(raw_in[n % 4], 16)

    def cond_parts(c):
        return [(0, 0, CH)] if (c + 1) * CH <= LAT else [(0, 0, LAT - c * CH), (1, LAT - c * CH, CH)]

    block_cm = nc.Block()
    block = block_cm.__enter__()

    @block.sync
    def _(sp):
        for dst, src in ((ident, "ident"), (q_scale, "q_scale"), (rope, "rope_rows"), (edge, "edge"),
                         (pool_mat, "vec_zero")):
            sp.dma_start(dst[:], tab[src]).then_inc(S("const_in"), 16)
        for row, src in ((0, b_mod[0].rearrange("(r p) -> r p", p=P)), (24, b_mod[1].rearrange("(r p) -> r p", p=P)),
                         (48, norm_g.rearrange("l (r p) -> (l r) p", p=P)),
                         (64, pool_scale.rearrange("l (r p) -> (l r) p", p=P)),
                         (68, c.rearrange("a (r p) -> (a r) p", p=P)),
                         (76, c_ctx.rearrange("(r p) -> r p", p=P))):
            sp.dma_start(vec_rows[row:row + src.shape[0], :], src).then_inc(S("vec_in"), 16)
        load_units(sp, 0, 4)
        xs = x_sample[0].rearrange("(t p) d -> p t d", p=P)
        for t in range(TT):
            sp.dma_start(H[:, t, :], xs[:, t, :] if t < 8 else x_prompt[0]).then_inc(S("rows_in"), 16)
        load_units(sp, 4, unit_at[("tok", 0, 4)])
        for l in range(DEPTH):
            for ch in range(NCH):
                sp.wait_ge(S("xn_low"), KF * ((l * NCH) + ch + 1))
                sl = slice(ch * CH, (ch + 1) * CH)
                sp.dma_start(park_hi[:, :, sl], XH[:, :, sl].bitcast(F32)).then_inc(S("parked"), 16)
                sp.dma_start(park_lo[:, :, sl], XL[:, :, sl].bitcast(F32)).then_inc(S("parked"), 16)
            sp.dma_start(gq_rows[:], q_norm_g[l:l + 1, :].broadcast_to([P, QR])).then_inc(S("small_in"), 16)
            sp.dma_start(gkv_rows[:], kv_norm_g[l:l + 1, :].broadcast_to([P, KVR])).then_inc(S("small_in"), 16)
            sp.dma_start(wq_raw[:], w_q_up[l].rearrange("(k p) n -> p k n", p=P)).then_inc(S("small_in"), 16)
            sp.dma_start(wkv[:], w_kv_up[l]).then_inc(S("small_in"), 16)
            sp.dma_start(kvk[:, 8, 0:KVR], cache_ckv[0, l]).then_inc(S("small_in"), 16)
            for off in (128, 160, 192):
                sp.dma_start(kvk[:, 8, off:off + ROPE], cache_krope[0, l]).then_inc(S("small_in"), 16)
            if l:
                filled(sp, l - 1, "pool", 5)
            else:
                sp.wait_ge(S("const_in"), 80)
            for g in range(4):
                o = 64 * (g % 2)
                sp.dma_start(pool_mat[o:o + 64, g // 2, o:o + 64], pool_w[l, g]).then_inc(S("small_in"), 16)
            load_units(sp, unit_at[("tok", l, 4)], unit_at[("feat", l, 9)] + 1)
            sp.wait_ge(S("lat_ready"), l + 1)
            sp.dma_start(new_ckv[0, l], kvk[:, 9, 0:KVR]).then_inc(S("stored"), 16)
            sp.dma_start(new_krope[0, l], kvk[:, 9, KVR:KVR + ROPE]).then_inc(S("stored"), 16)
            sp.wait_ge(S("parked"), 16 * 6 * (l + 1))
            filled(sp, l, "feat", 29)
            sp.dma_start(seq_dft[:], tab["seq_dft"]).then_inc(S("dft_in"), 16)
            sp.dma_start(chan_dft[:], tab["chan_dft"]).then_inc(S("dft_in"), 16)
            if l + 1 < DEPTH:
                load_units(sp, unit_at[("mod", l + 1, 0)], unit_at[("mod", l + 1, 23)] + 1)
            load_units(sp, unit_at[("gate", l, 0)], unit_at[("gate", l, 0)] + 4)
            filled(sp, l, "attn", head_item(l, 3, 2, 3))
            for ch in range(NCH):
                sl = slice(ch * CH, (ch + 1) * CH)
                sp.dma_start(XH[:, :, sl].bitcast(F32), park_hi[:, :, sl]).then_inc(S(f"xn_back{ch}"), 16)
                sp.dma_start(XL[:, :, sl].bitcast(F32), park_lo[:, :, sl]).then_inc(S(f"xn_back{ch}"), 16)
            load_units(sp, unit_at[("gate", l, 0)] + 4, unit_at[("out", l, 3)] + 1)
            sp.wait_ge(S("y_low"), NCH * KF * (l + 1))
            for t in range(TT):
                if l == 0:
                    src = xs[:, t, :] if t < 8 else x_prompt[0]
                else:
                    src = rows_mid[:, t, :]
                sp.dma_start(H[:, t, :], src).then_inc(S("rows_in"), 16)
            if l + 1 == DEPTH:
                sp.dma_start(finalB[:], final_norm_g.rearrange("(a d) -> a d", a=1).broadcast_to([P, D])).then_inc(S("final_in"), 16)
            hi = unit_at[("tok", l + 1, 3)] + 1 if l + 1 < DEPTH else len(units)
            load_units(sp, unit_at[("out", l, 4)], unit_at[("out", l, 7)] + 1)
            if l + 1 < DEPTH:
                for t in range(TT):
                    sp.wait_ge(S("rows_added"), 4 * TT * l + 3 * TT + t + 1)
                    sp.dma_start(rows_mid[:, t, :], H[:, t, :]).then_inc(S("mid_out"), 16)
                load_units(sp, unit_at[("out", l, 7)] + 1, hi)
            else:
                ys = y_sample[0].rearrange("(t p) d -> p t d", p=P)
                for t in range(TT):
                    sp.wait_ge(S("y_rows"), t + 1)
                    sp.dma_start(ys[:, t, :] if t < 8 else y_prompt[0], xhat[:, t % CT, :]).then_inc(S("y_out"), 16)
        sp.wait_ge(S("stored"), 16 * 2 * DEPTH)
        sp.wait_ge(S("y_out"), 16 * TT)

    @block.scalar
    def _(act):
        a = nc.scalar

        def split_high(key):
            k = split_k[key]
            n, dest, free_after = split_plan[k]
            arrived(act, n)
            if free_after:
                filled(act, *free_after)
            a.activation(split_dest(dest)[:, 0], raw[:, n % 4], ACT.Copy).then_inc(S("split_high"), 1)

        def squares(l, ch):
            for tt in range(CT):
                t = ch * CT + tt
                if l == 0:
                    act.wait_ge(S("rows_in"), 16 * TT)
                else:
                    act.wait_ge(S("rows_added"), 4 * TT * (l - 1) + 3 * TT + t + 1)
                a.activation(xhat[:, tt, :], H[:, t, :], ACT.Square, accum_out=ssq[:, tt:tt + 1])\
                    .then_inc(S("squares"), 1)

        def norm_act(l, ch):
            g = l * NCH + ch
            if ch:
                filled(act, l, "norm", ch * KF - 1)
            squares(l, ch)
            act.wait_ge(S("mean_sq"), g + 1)
            a.activation(root[:], ssq[:], ACT.Sqrt).then_inc(S("roots"), 1)
            for f in range(KF):
                n = ch * KF + f
                b = filled(act, l, "norm", n)
                if n + l * NCH * KF >= 3:
                    act.wait_ge(S("xn_low"), l * NCH * KF + n - 2)
                if f == 0:
                    act.wait_ge(S("scale_ready"), l + 1)
                parts = cond_parts(ch)
                for i, (cond, c0, c1) in enumerate(parts):
                    ins = a.activation(vtmp[:, n % 3, c0:c1], PS[:, b, c0:c1], ACT.Identity,
                                       bias=modT[:, l % 2, f, cond:cond + 1], scale=scaleT[:, f, cond:cond + 1])
                    if i == len(parts) - 1:
                        ins.then_inc(bank_free[b], 1)

        read_out(act, 0, "vec", 0)
        for cond in range(2):
            a.activation(silu_c[:, :, cond], vecT[:, 68 + 8 * cond:76 + 8 * cond], ACT.Silu).then_inc(S("silu_c"), 1)
        for ch in range(NCH):
            norm_act(0, ch)

        for l in range(DEPTH):
            for u in range(6):
                if u == 2 and l == 0:
                    read_out(act, 0, "vec", 0)
                split_high(("tok", l, u))
            for p in range(3):
                for t in range(TT):
                    b = filled(act, l, "tok", p * TT + t)
                    if t == 0:
                        act.wait_ge(S("xhat"), 9 * l + 3 * (p + 1))
                        if l:
                            act.wait_ge(S("mid_out"), 16 * TT)
                    if p == 0:
                        ins = a.activation(atok[:, t, :], PS[:, b, 0:256], ACT.Copy)
                    elif p == 1:
                        ins = a.activation(qlat[:, t, :], PS[:, b, 0:256], ACT.Copy)
                    else:
                        s = t if t < 8 else 9
                        ins = a.activation(kvk[:, s, 0:160], PS[:, b, 96:256], ACT.Copy)
                    ins.then_inc(bank_free[b], 1)
                if p == 0:
                    split_high(("feat", l, 0))
                    split_high(("feat", l, 1))
            for u in range(10):
                if u == 1:
                    act.wait_ge(S("lat_mean"), l + 1)
                    a.activation(lat_root[:], lat_ssq[:], ACT.Sqrt).then_inc(S("lat_root"), 1)
                if 1 <= u < 9:
                    split_high(("feat", l, u + 1))
                for ch in range(NCH):
                    b = filled(act, l, "feat", 3 * u + ch)
                    if u < 2:
                        if ch == 0:
                            act.wait_ge(S("pads"), l + 1)
                        for cond, c0, c1 in cond_parts(ch):
                            o = SAMPLE0 + ch * CH if cond == 0 else PROMPT0 - c0
                            ins = a.activation(binp[:, u, o + c0:o + c1], PS[:, b, c0:c1], ACT.Copy)
                    else:
                        i = u - 2
                        ins = a.activation(BR[:, i, ch * CH:(ch + 1) * CH], PS[:, b, 0:CH], ACT.Silu)
                    ins.then_inc(bank_free[b], 1)
            act.wait_ge(S("parked"), 16 * 6 * (l + 1))
            for s in range(KS):
                b = filled(act, l, "val", s)
                a.activation(V[:, s, :], PS[:, b, :], ACT.Copy).then_inc(bank_free[b], 1)
            filled(act, l, "pool", 5)
            for n in range(12):
                b = filled(act, l, "seq", n)
                a.activation(XR[:, n % 2, :, n // 2, :], PS[:, b, 0:256].rearrange("p (c m) -> p c m", c=2),
                             ACT.Copy).then_inc(bank_free[b], 1)
            def exps(i, u, j):
                m = u * 9 + j
                g = (l * 4 + i) * 18 + m
                buf = m % 2
                act.wait_ge(S("negmax"), g + 1)
                if m >= 2 or i:
                    prev = m - 2 if m >= 2 else m + 16
                    pi = i if m >= 2 else i - 1
                    pj = prev % 9
                    filled(act, l, "attn", head_item(l, pi, prev // 9, AT + (3 * pj + 2 if pj < 8 else 24)))
                b0 = 3 * buf
                if j < 8:
                    src = PS[:, b0:b0 + 3, 0:CH]
                    dst = probs[:, buf, :].rearrange("p (k c) -> p k c", k=3)
                else:
                    src = PS[:, b0, 0:P]
                    dst = probs[:, buf, 0:P]
                a.activation(dst, src, ACT.Exp, bias=negmax[:, buf:buf + 1],
                             accum_out=rowsum[:, buf:buf + 1]).then_inc(S("exped"), 1)

            def turned(i, u, j):
                m = u * 9 + j
                buf = m % 2
                if j < 8:
                    n = head_item(l, i, u, AT + 3 * j)
                    b = filled(act, l, "attn", n)
                    g = (l * 4 + i) * 9 + m // 2
                    if g:
                        act.wait_ge(S(f"mixed{buf}"), g)
                    a.activation(probsT[:, buf, 0:3, :], PS[:, b, 0:CH].rearrange("p (k c) -> p k c", k=3),
                                 ACT.Copy).then_inc(bank_free[b], 1)

            for i in range(4):
                for u in range(2):
                    for n in range(3):
                        nn = head_item(l, i, u, AK + n)
                        b = filled(act, l, "attn", nn)
                        w = min(512, KEYS - 512 * n)
                        a.activation(kT[0:NOPE, u, 512 * n:512 * n + w], PS[0:NOPE, b, 0:w], ACT.Copy)\
                            .then_inc(bank_free[b], 1)
                    exps(i, u, 0)
                    for j in range(9):
                        if j < 8:
                            exps(i, u, j + 1)
                        turned(i, u, j)
            split_high(("gate", l, 0))
            split_high(("gate", l, 1))
            for n in range(24):
                for ch in range(NCH):
                    b = filled(act, l, "gate", 3 * n + ch)
                    if 3 * n + ch >= 3:
                        read_out(act, l, "branch", 3 * n + ch - 3)
                    a.activation(sig[:, ch, :], PS[:, b, 0:CH], ACT.Sigmoid).then_inc(bank_free[b], 1)
                if n + 2 < 24:
                    split_high(("gate", l, n + 2))
            for u in range(4):
                if u == 0:
                    filled(act, l, "branch", 71)
                split_high(("out", l, u))
            filled(act, l, "gate", 71)
            for ch in range(NCH):
                for j in range(KF):
                    if ch == 0:
                        act.wait_ge(S("y_sum"), 48 * l + 6 * j + 6)
                    sl = slice(ch * CH, (ch + 1) * CH)
                    a.activation(XH[:, j, sl], Y[:, j, sl], ACT.Copy).then_inc(S("y_high"), 1)
            for u in range(4, 8):
                split_high(("out", l, u))
            if l + 1 < DEPTH:
                for ch in range(NCH):
                    norm_act(l + 1, ch)
            else:
                for ch in range(NCH):
                    if ch:
                        act.wait_ge(S("y_out"), 16 * CT * ch)
                    squares(DEPTH, ch)
                    act.wait_ge(S("mean_sq"), DEPTH * NCH + ch + 1)
                    a.activation(root[:], ssq[:], ACT.Sqrt).then_inc(S("roots"), 1)

    @block.gpsimd
    def _(pool):
        g = nc.gpsimd

        def split_low(key):
            k = split_k[key]
            n, dest, _ = split_plan[k]
            pool.wait_ge(S("split_high"), k + 1)
            d = split_dest(dest)
            g.tensor_tensor(d[:, 1], raw[:, n % 4], d[:, 0].bitcast(F32), ALU.subtract).then_inc(S("split_low"), 1)

        def norm_low(l, ch):
            for f in range(KF):
                n = l * NCH * KF + ch * KF + f
                pool.wait_ge(S("xn_high"), n + 1)
                sl = slice(ch * CH, (ch + 1) * CH)
                g.tensor_tensor(XL[:, f, sl], vtmp[:, (ch * KF + f) % 3, :], XH[:, f, sl].bitcast(F32),
                                ALU.subtract).then_inc(S("xn_low"), 1)

        g.memset(ones[:], 1.0).then_inc(S("ones"), 1)
        for ch in range(NCH):
            norm_low(0, ch)
        for l in range(DEPTH):
            for u in range(6):
                split_low(("tok", l, u))
            split_low(("feat", l, 0))
            split_low(("feat", l, 1))
            for i, (o, w) in enumerate(((0, PAD), (SAMPLE0 + LAT, 2 * PAD), (PROMPT0 + SEQ, PAD))):
                ins = g.memset(binp[:, :, o:o + w], 0.0)
            ins.then_inc(S("pads"), 1)
            for u in range(2, 10):
                split_low(("feat", l, u))
            filled(pool, l, "feat", 29)
            pool.wait_ge(S("parked"), 16 * 6 * (l + 1))
            for kt in range(2):
                read_out(pool, l, "feat", 3 * kt + 2)
                if kt:
                    pool.wait_ge(S("pooled"), 4 * l + 2)
                w = POOLW
                x = binp[:, kt, :]
                nw = l * 6 + (0 if kt == 0 else 2)
                g.tensor_tensor(winA[:, 1:w], x[:, 0:w - 1], x[:, 1:w], ALU.add).then_inc(S("window"), 1)
                pool.wait_ge(S("window"), nw + 1)
                lo = 64 if kt == 0 else 0
                g.tensor_tensor(winB[lo:, 2:w - 1], winA[lo:, 1:w - 2], winA[lo:, 3:w], ALU.add).then_inc(S("window"), 1)
                if kt:
                    pool.wait_ge(S("window"), nw + 2)
                    g.tensor_tensor(winA[:, 4:w - 3], winB[:, 2:w - 5], winB[:, 6:w - 1], ALU.add).then_inc(S("window"), 1)
                    pool.wait_ge(S("window"), nw + 3)
                    g.tensor_tensor(winB[64:, 8:w - 7], winA[64:, 4:w - 11], winA[64:, 12:w - 3], ALU.add)\
                        .then_inc(S("window"), 1)
            split_low(("gate", l, 0))
            split_low(("gate", l, 1))
            for j in range(KF):
                for b in range(3):
                    if b:
                        for ch in range(NCH):
                            q = 6 * j + (b - 1) * 3 + ch
                            sl = slice(ch * CH, (ch + 1) * CH)
                            read_out(pool, l, "branch", (3 * j + b) * 3 + ch)
                            if b == 1:
                                read_out(pool, l, "branch", 3 * j * 3 + ch)
                            else:
                                pool.wait_ge(S("y_sum"), 48 * l + q - 2)
                            g.tensor_tensor(Y[:, j, sl], Y[:, j, sl], prod[:, q % 2, :], ALU.add)\
                                .then_inc(S("y_sum"), 1)
                    n = 3 * j + b
                    if n + 2 < 24:
                        split_low(("gate", l, n + 2))
            for u in range(4):
                split_low(("out", l, u))
            for ch in range(NCH):
                for j in range(KF):
                    n = l * NCH * KF + ch * KF + j
                    pool.wait_ge(S("y_high"), n + 1)
                    sl = slice(ch * CH, (ch + 1) * CH)
                    g.tensor_tensor(XL[:, j, sl], Y[:, j, sl], XH[:, j, sl].bitcast(F32), ALU.subtract)\
                        .then_inc(S("y_low"), 1)
            for p in range(4):
                for t in range(TT):
                    n = p * TT + t
                    if t == 5 and p in (0, 1):
                        split_low(("out", l, 4 + 2 * p))
                        split_low(("out", l, 5 + 2 * p))
                    read_out(pool, l, "out", n)
                    if p == 0:
                        pool.wait_ge(S("rows_in"), 16 * TT * (l + 2))
                    dst = H[:, t, p * 256:(p + 1) * 256]
                    g.tensor_tensor(dst, dst, tmpw[:, n % 2, :], ALU.add).then_inc(S("rows_added"), 1)
            if l + 1 < DEPTH:
                for ch in range(NCH):
                    norm_low(l + 1, ch)

    @block.vector
    def _(dve):
        v = nc.vector

        def norm_scale(l, ch, final=False):
            gch = l * NCH + ch
            dve.wait_ge(S("squares"), CT * (gch + 1))
            v.tensor_scalar(ssq[:], ssq[:], 1.0 / D, EPS, ALU.mult, ALU.add).then_inc(S("mean_sq"), 1)
            dve.wait_ge(S("roots"), gch + 1)
            v.reciprocal(rinv[:], root[:]).then_inc(S("rinv"), 1)
            dve.wait_ge(S("rinv"), gch + 1)
            if final and ch == 0:
                dve.wait_ge(S("final_in"), 16)
            for tt in range(CT):
                t = ch * CT + tt
                if final:
                    v.scalar_tensor_tensor(xhat[:, tt, :], H[:, t, :], rinv[:, tt:tt + 1], finalB[:], ALU.mult,
                                           ALU.mult).then_inc(S("y_rows"), 1)
                else:
                    v.tensor_scalar(xhat[:, tt, :], H[:, t, :], rinv[:, tt:tt + 1], None, ALU.mult)\
                        .then_inc(S("xhat"), 1)

        def norm_dve(l, ch):
            norm_scale(l, ch)
            for f in range(KF):
                n = ch * KF + f
                read_out(dve, l, "norm", n)
                if l and f == 0:
                    filled(dve, l - 1, "out", 3 * TT + ch * CT + CT - 1)
                sl = slice(ch * CH, (ch + 1) * CH)
                v.tensor_copy(XH[:, f, sl], vtmp[:, n % 3, :]).then_inc(S("xn_high"), 1)

        def modulation(l, h, b):
            bias = vecT[:, 24 * l + 3 * h:24 * l + 3 * h + 3].unsqueeze(2).broadcast_to([P, 3, 2])
            v.tensor_tensor(modT[:, l % 2, 3 * h:3 * h + 3, :], PS[:, b, 0:6].rearrange("p (m c) -> p m c", c=2),
                            bias, ALU.add).then_inc(bank_free[b], 1)

        def scales(l):
            for cond in range(2):
                ins = v.scalar_tensor_tensor(scaleT[:, :, cond], modT[:, l % 2, 8:16, cond], 1.0,
                                             vecT[:, 48 + 8 * l:56 + 8 * l], ALU.add, ALU.mult)
            ins.then_inc(S("scale_ready"), 1)

        filled(dve, 0, "vec", 0)
        v.tensor_copy(vecT[:], PS[:, 6, 0:84]).then_inc(bank_free[6], 1)
        read_out(dve, 0, "vec", 0)
        for h in range(8):
            b = filled(dve, 0, "mod", h)
            modulation(0, h, b)
        read_out(dve, 0, "mod", 6)
        read_out(dve, 0, "mod", 7)
        scales(0)
        for ch in range(NCH):
            norm_dve(0, ch)

        for l in range(DEPTH):
            dve.wait_ge(S("small_in"), 16 * 12 * (l + 1))
            for t in range(TT):
                read_out(dve, l, "tok", TT + t)
                v.tensor_tensor_reduce(rot_tmp[:].rearrange("p a b -> p (a b)"), qlat[:, t, :], qlat[:, t, :], 1.0, 0.0, ALU.mult, ALU.add,
                                       lat_ssq[:, t:t + 1]).then_inc(S("lat_ssq"), 1)
                dve.wait_ge(S("lat_ssq"), 18 * l + t + 1)
            for t in range(TT):
                s = t if t < 8 else 9
                read_out(dve, l, "tok", 2 * TT + t)
                v.tensor_tensor_reduce(rot_tmp[:].rearrange("p a b -> p (a b)")[:, 0:KVR], kvk[:, s, 0:KVR],
                                       kvk[:, s, 0:KVR], 1.0, 0.0, ALU.mult, ALU.add,
                                       lat_ssq[:, TT + t:TT + t + 1]).then_inc(S("lat_ssq"), 1)
                dve.wait_ge(S("lat_ssq"), 18 * l + TT + t + 1)
            v.tensor_scalar(lat_ssq[:, 0:TT], lat_ssq[:, 0:TT], 1.0 / QR, EPS, ALU.mult, ALU.add)
            v.tensor_scalar(lat_ssq[:, TT:2 * TT], lat_ssq[:, TT:2 * TT], 1.0 / KVR, EPS, ALU.mult, ALU.add)\
                .then_inc(S("lat_mean"), 1)
            kr = kvk[:, 0:8, KVR:KVR + ROPE]
            kr1 = kvk[:, 0:8, KVR + ROPE:KVR + 2 * ROPE]
            for hf in range(2):
                for a2 in range(2):
                    o = 16 * a2 + 8 * hf
                    oo = 16 * a2 + 8 * (1 - hf)
                    v.tensor_tensor(rot_tmp[:, :, o:o + 8], kr[:, :, oo:oo + 8], rope[:, 1, :, o:o + 8], ALU.mult)\
                        .then_inc(S("rope_rot"), 1)
            v.tensor_tensor(kr1, kr, rope[:, 0], ALU.mult).then_inc(S("rope_rot"), 1)
            dve.wait_ge(S("rope_rot"), 6 * l + 5)
            v.tensor_tensor(kr1, kr1, rot_tmp[:], ALU.add).then_inc(S("rope_rot"), 1)
            dve.wait_ge(S("rope_rot"), 6 * l + 6)
            v.tensor_copy(kvk[:, 0:8, KVR + 2 * ROPE:KVW], kr1)
            for o in (160, 192):
                v.tensor_copy(kvk[:, 9, o:o + ROPE], kvk[:, 9, KVR:KVR + ROPE])
            dve.wait_ge(S("lat_root"), l + 1)
            v.reciprocal(lat_rinv[:], lat_root[:]).then_inc(S("lat_rinv"), 1)
            dve.wait_ge(S("lat_rinv"), l + 1)
            for t in range(TT):
                v.scalar_tensor_tensor(qlat[:, t, :], qlat[:, t, :], lat_rinv[:, t:t + 1], gq_rows[:], ALU.mult, ALU.mult)
            for t in range(TT):
                s = t if t < 8 else 9
                ins = v.scalar_tensor_tensor(kvk[:, s, 0:KVR], kvk[:, s, 0:KVR], lat_rinv[:, TT + t:TT + t + 1],
                                             gkv_rows[:], ALU.mult, ALU.mult)
            ins.then_inc(S("lat_ready"), 1)
            filled(dve, l, "feat", 29)
            dve.wait_ge(S("parked"), 16 * 6 * (l + 1))
            for n in range(6):
                b = filled(dve, l, "turn", n)
                kt, ch = n // 3, n % 3
                v.tensor_copy(qhatT[:, kt, ch * CH:(ch + 1) * CH], PS[:, b, 0:CH]).then_inc(bank_free[b], 1)
            for n in range(4):
                b = filled(dve, l, "turn", 6 + n)
                w = min(CH, KEYS - CH * n)
                v.tensor_copy(ckvT[:, CH * n:CH * n + w], PS[:, b, 0:w]).then_inc(bank_free[b], 1)
            for n in range(4):
                b = filled(dve, l, "turn", 10 + n)
                w = min(CH, KEYS - CH * n)
                v.tensor_copy(kT[NOPE:, 0, CH * n:CH * n + w], PS[NOPE:, b, 0:w])
                v.tensor_copy(kT[NOPE:, 1, CH * n:CH * n + w], PS[NOPE:, b, 0:w]).then_inc(bank_free[b], 1)
            ss, dd = dft_sd[:, 0:4, :], dft_sd[:, 4:8, :]
            half = 0.5 ** 0.5
            v.tensor_tensor(ss, atok[:, 0:4, :], atok[:, 4:8, :], ALU.add).then_inc(S("dft8"), 1)
            v.tensor_tensor(dd, atok[:, 0:4, :], atok[:, 4:8, :], ALU.subtract).then_inc(S("dft8"), 1)
            dve.wait_ge(S("dft8"), 8 * l + 2)
            v.tensor_tensor(atok[:, 0:2, :], ss[:, 0:2], ss[:, 2:4], ALU.add).then_inc(S("dft8"), 1)
            v.tensor_tensor(U[:, 4], ss[:, 0], ss[:, 2], ALU.subtract)
            v.tensor_tensor(U[:, 5], ss[:, 3], ss[:, 1], ALU.subtract)
            v.tensor_tensor(atok[:, 2], dd[:, 1], dd[:, 3], ALU.subtract).then_inc(S("dft8"), 1)
            v.tensor_tensor(atok[:, 3], dd[:, 1], dd[:, 3], ALU.add).then_inc(S("dft8"), 1)
            dve.wait_ge(S("dft8"), 8 * l + 5)
            v.tensor_tensor(U[:, 0], atok[:, 0], atok[:, 1], ALU.add)
            v.tensor_tensor(U[:, 1], atok[:, 0], atok[:, 1], ALU.subtract)
            v.scalar_tensor_tensor(U[:, 2], atok[:, 2], half, dd[:, 0], ALU.mult, ALU.add)
            v.scalar_tensor_tensor(U[:, 6], atok[:, 2], -half, dd[:, 0], ALU.mult, ALU.add).then_inc(S("dft8"), 1)
            v.scalar_tensor_tensor(U[:, 3], atok[:, 3], -half, dd[:, 2], ALU.mult, ALU.subtract).then_inc(S("dft8"), 1)
            v.scalar_tensor_tensor(U[:, 7], atok[:, 3], -half, dd[:, 2], ALU.mult, ALU.add).then_inc(S("dft8"), 1)
            for kt in range(2):
                dve.wait_ge(S("window"), 6 * l + (2 if kt == 0 else 6))
                for hf, wn in ((0, winA), (1, winB)):
                    rows = slice(64 * hf, 64 * hf + 64)
                    for e, o in enumerate((SAMPLE0, SAMPLE0 + LAT - PAD, PROMPT0, PROMPT0 + SEQ - PAD)):
                        ins = v.tensor_tensor(wn[rows, o:o + PAD], wn[rows, o:o + PAD], edge[rows, kt, e, :], ALU.mult)
                    ins.then_inc(S("edges"), 1)
                dve.wait_ge(S("edges"), 4 * l + 2 * kt + 2)
                for hf, wn in ((0, winA), (1, winB)):
                    rows = slice(64 * hf, 64 * hf + 64)
                    x = binp[rows, kt, PAD:POOLW - PAD]
                    v.scalar_tensor_tensor(x, wn[rows, PAD:POOLW - PAD], 1.0 / WINDOWS[2 * kt + hf], x, ALU.mult,
                                           ALU.subtract).then_inc(S("pooled"), 1)
            for n in range(6):
                kt, ch = n // 3, n % 3
                b = filled(dve, l, "pool", n)
                if n == 0:
                    read_out(dve, l, "feat", 6 * 3 - 1)
                x = BR[:, 2 + kt, ch * CH:(ch + 1) * CH]
                v.scalar_tensor_tensor(x, PS[:, b, 0:CH], vecT[:, 64 + 2 * l + kt:65 + 2 * l + kt], x, ALU.mult, ALU.mult)\
                    .then_inc(bank_free[b], 1)
            for n in range(6):
                kt, part = n // 3, n % 3
                b = filled(dve, l, "chan", n)
                z = BR[:, kt, 0:LAT].rearrange("p (m r) -> p r m", r=8)
                pb = PS[:, b, :].rearrange("p (r m) -> p r m", r=4)
                if part == 0:
                    ins = v.tensor_tensor(z[:, 0:4, :], pb, z[:, 0:4, :], ALU.mult)
                elif part == 1:
                    v.tensor_tensor(z[:, 4, :], pb[:, 0, :], z[:, 4, :], ALU.mult)
                    for r3 in range(3):
                        ins = v.tensor_tensor(z[:, 5 + r3, :], pb[:, 1 + r3, ::-1], z[:, 5 + r3, :], ALU.mult)
                else:
                    zp = BR[:, kt, LAT:TOK]
                    ins = v.tensor_tensor(zp, PS[:, b, 0:P], zp, ALU.mult)
                ins.then_inc(bank_free[b], 1)

            def head_weights(i, u):
                h = 2 * i + u
                g = l * 8 + h
                if h >= 2:
                    filled(dve, l, "attn", head_item(l, i - 1, u, AQ + 2))
                c0 = h * (NOPE + ROPE)
                v.tensor_copy(wq[:, u, :, 0:96], wq_raw[:, :, c0:c0 + 96])
                for a2 in range(2):
                    for hf in range(2):
                        dst = wq[:, u, :, 96 + 16 * a2 + 8 * hf:104 + 16 * a2 + 8 * hf]
                        so = c0 + NOPE + 16 * a2 + 8 * (1 - hf)
                        ins = v.tensor_scalar(dst, wq_raw[:, :, so:so + 8], 1.0 if hf else -1.0, None, ALU.mult)
                ins.then_inc(S("wq_ready"), 1)

            def negmaxes(i, u, j):
                m = u * 9 + j
                buf = m % 2
                b0 = 3 * buf
                dve.wait_ge(S(f"scores{buf}"), (l * 4 + i) * 9 + m // 2 + 1)
                src = PS[:, b0:b0 + 3, 0:CH] if j < 8 else PS[:, b0, 0:P]
                v.tensor_reduce(negmax[:, buf:buf + 1], src, AX.XY if j < 8 else AX.X, ALU.max, negate=True)\
                    .then_inc(S("negmax"), 1)

            def turned(i, u, j):
                m = u * 9 + j
                buf = m % 2
                for gg in ((1, 2) if j < 8 else (0,)):
                    n = head_item(l, i, u, AT + 3 * j + gg)
                    b = filled(dve, l, "attn", n)
                    if m >= 2 or i or l:
                        dve.wait_ge(S(f"mixed{buf}"), (l * 4 + i) * 9 + m // 2)
                    if j < 8:
                        ins = v.tensor_copy(probsT[:, buf, 3 * gg:3 * gg + 3, :],
                                            PS[:, b, 0:CH].rearrange("p (k c) -> p k c", k=3))
                    else:
                        ins = v.tensor_copy(probsT[:, buf, 0, :], PS[:, b, 0:P])
                    ins.then_inc(bank_free[b], 1)

            def normalise(i, u, j):
                m = u * 9 + j
                buf = m % 2
                g = (l * 4 + i) * 18 + m
                dve.wait_ge(S("exped"), g + 1)
                v.reciprocal(rsinv[:, buf:buf + 1], rowsum[:, buf:buf + 1]).then_inc(S("rsinv"), 1)
                dve.wait_ge(S("rsinv"), g + 1)
                dve.wait_ge(S(f"mixed{buf}"), (l * 4 + i) * 9 + m // 2 + 1)
                if u == 0 and j == 0 and i == 0:
                    dve.wait_ge(S("stored"), 32 * (l + 1))
                if u == 0 and j == 0 and i >= 2:
                    filled(dve, l, "attn", head_item(l, i - 2, 2, 3))
                v.tensor_scalar(O[:, i % 2, j, VDIM * u:VDIM * u + VDIM], PS[:, 3 * buf, CH:CH + VDIM],
                                rsinv[:, buf:buf + 1], None, ALU.mult).then_inc(S(f"head_rows{buf}"), 1)

            for i in range(4):
                for u in range(2):
                    head_weights(i, u)
                    for ch in range(3):
                        b = filled(dve, l, "attn", head_item(l, i, u, AQ + ch))
                        sl = slice(ch * CH, (ch + 1) * CH)
                        v.tensor_tensor(qT[:, u, sl], PS[:, b, 0:CH], q_scale[:, sl], ALU.mult).then_inc(bank_free[b], 1)
                    negmaxes(i, u, 0)
                    for j in range(9):
                        if j < 8:
                            negmaxes(i, u, j + 1)
                        turned(i, u, j)
                        normalise(i, u, j)
                    if l + 1 < DEPTH:
                        b = filled(dve, l, "attn", head_item(l, i, u, AM))
                        modulation(l + 1, 2 * i + u, b)
                for n in range(4):
                    b = filled(dve, l, "attn", head_item(l, i, 2, n))
                    t0, t1 = ((0, 3), (3, 6), (6, 8), (8, 9))[n]
                    x = BR[:, 4 + i, t0 * P:t1 * P]
                    v.tensor_tensor(x, PS[:, b, 0:(t1 - t0) * P], x, ALU.mult).then_inc(bank_free[b], 1)
            if l + 1 < DEPTH:
                for h in (6, 7):
                    read_out(dve, l, "attn", head_item(l, 3, h - 6, AM))
                scales(l + 1)
            for j in range(KF):
                for b3 in range(3):
                    for ch in range(NCH):
                        n = (3 * j + b3) * 3 + ch
                        read_out(dve, l, "gate", n)
                        b = filled(dve, l, "branch", n)
                        sl = slice(ch * CH, (ch + 1) * CH)
                        if b3 == 0:
                            dst = Y[:, j, sl]
                        else:
                            q = 6 * j + (b3 - 1) * 3 + ch
                            if q >= 2:
                                dve.wait_ge(S("y_sum"), 48 * l + q - 1)
                            dst = prod[:, q % 2, :]
                        v.tensor_tensor(dst, PS[:, b, 0:CH], sig[:, ch, :], ALU.mult).then_inc(bank_free[b], 1)
            filled(dve, l, "gate", 71)
            for n in range(4):
                cond, hf = n // 2, n % 2
                if n >= 2:
                    filled(dve, l, "gbc", n - 2)
                else:
                    dve.wait_ge(S("y_sum"), 48 * (l + 1))
                for q in range(4):
                    f = 16 + 4 * hf + q
                    ins = v.tensor_scalar(diag[:, n % 2, q, :], ident[:], modT[:, l % 2, f, cond:cond + 1], None, ALU.mult)
                ins.then_inc(S("diag"), 1)
            for n in range(4):
                cond, hf = n // 2, n % 2
                b = filled(dve, l, "gbc", n)
                v.tensor_copy(gateB[:, cond, hf * 512:hf * 512 + 512], PS[:, b, :]).then_inc(bank_free[b], 1)
            for n in range(4):
                read_out(dve, l, "gbc", n)
            for p in range(4):
                for t in range(TT):
                    n = p * TT + t
                    b = filled(dve, l, "out", n)
                    if n >= 2:
                        dve.wait_ge(S("rows_added"), 4 * TT * l + n - 1)
                    v.tensor_tensor(tmpw[:, n % 2, :], PS[:, b, 0:256], gateB[:, int(t == 8), p * 256:(p + 1) * 256],
                                    ALU.mult).then_inc(bank_free[b], 1)
            if l + 1 < DEPTH:
                for ch in range(NCH):
                    norm_dve(l + 1, ch)
            else:
                for ch in range(NCH):
                    norm_scale(DEPTH, ch, final=True)

    @block.tensor
    def _(pe):
        mm = nc.tensor.matmul

        def three_pass(out, wh, wl, xh, xl, first, last):
            mm(out, wh, xh, start=first, stop=False)
            mm(out, wh, xl, start=False, stop=False)
            return mm(out, wl, xh, start=False, stop=last)

        def mod_item(l, ph, n, layer, h):
            b = pe_takes(pe, ph[0], ph[1], n)
            for q in range(3):
                m = 3 * h + q
                arrived(pe, unit_at[("mod", layer, m)])
                for k in range(KF):
                    ins = mm(PS[:, b, 2 * q:2 * q + 2], raw[:, unit_at[("mod", layer, m)] % 4, k, :], silu_c[:, k, :],
                             start=(k == 0), stop=(k == KF - 1))
            ins.then_inc(bank_full[b], 1)

        def norm_turn(l, ch):
            pe.wait_ge(S("xhat"), 9 * l + CT * (ch + 1))
            for f in range(KF):
                b = pe_takes(pe, l, "norm", ch * KF + f)
                for tt in range(CT):
                    ins = nc.tensor.transpose(PS[:, b, tt * P:(tt + 1) * P], xhat[:, tt, f * P:(f + 1) * P], ident[:])
                ins.then_inc(bank_full[b], 1)

        pe.wait_ge(S("const_in"), 80)
        pe.wait_ge(S("ones"), 1)
        pe.wait_ge(S("vec_in"), 16 * 6)
        nc.tensor.transpose(PS[:, 6, 0:84], vec_rows[0:84, :], ident[0:84, 0:84]).then_inc(bank_full[6], 1)
        pe.wait_ge(S("silu_c"), 2)
        for h in range(8):
            mod_item(0, (0, "mod"), h, 0, h)
        for ch in range(NCH):
            norm_turn(0, ch)

        for l in range(DEPTH):
            for p in range(3):
                pe.wait_ge(S("split_low"), split_k[("tok", l, 2 * p + 1)] + 1)
                w = ws[:] if p == 0 else bs[:, 2 * (p - 1):2 * p]
                for t in range(TT):
                    if p == 0 and t % CT == 0:
                        pe.wait_ge(S("xn_low"), KF * (l * NCH + t // CT + 1))
                    b = pe_takes(pe, l, "tok", p * TT + t)
                    sl = slice(t * P, (t + 1) * P)
                    out = PS[:, b, 0:256]
                    for k in range(KF):
                        ins = three_pass(out, XH[:, k, sl], XL[:, k, sl], w[:, :, 0, k, :], w[:, :, 1, k, :],
                                         k == 0, k == KF - 1)
                    ins.then_inc(bank_full[b], 1)
            def columns(phase, l, u, ch, n):
                b = pe_takes(pe, l, phase, n)
                sl = slice(ch * CH, (ch + 1) * CH)
                for k in range(KF):
                    ins = three_pass(PS[:, b, 0:CH], ws[:, u % 2, 0, k, :], ws[:, u % 2, 1, k, :], XH[:, k, sl],
                                     XL[:, k, sl], k == 0, k == KF - 1)
                ins.then_inc(bank_full[b], 1)
            for u in range(10):
                pe.wait_ge(S("split_low"), split_k[("feat", l, u)] + 1)
                for ch in range(NCH):
                    columns("feat", l, u, ch, 3 * u + ch)
            pe.wait_ge(S("lat_ready"), l + 1)
            for n in range(6):
                kt, ch = n // 3, n % 3
                b = pe_takes(pe, l, "turn", n)
                for tt in range(CT):
                    ins = nc.tensor.transpose(PS[:, b, tt * P:(tt + 1) * P], qlat[:, ch * CT + tt, kt * P:(kt + 1) * P], ident[:])
                ins.then_inc(bank_full[b], 1)
            for kind in range(2):
                for n in range(4):
                    b = pe_takes(pe, l, "turn", 6 + 4 * kind + n)
                    for s in range(3 * n, min(3 * n + 3, KS)):
                        src = kvk[:, s, 0:P] if kind == 0 else kvk[:, s, KVW - P:KVW]
                        ins = nc.tensor.transpose(PS[:, b, (s - 3 * n) * P:(s - 3 * n + 1) * P], src, ident[:])
                    ins.then_inc(bank_full[b], 1)
            for n in range(4):
                read_out(pe, l, "turn", 6 + n)
            wv = wkv[:].rearrange("p (h c) -> p h c", c=P)[:, :, NOPE:P]
            for s in range(KS):
                b = pe_takes(pe, l, "val", s)
                mm(PS[:, b, :], ckvT[:, s * P:(s + 1) * P], wv, start=True, stop=True).then_inc(bank_full[b], 1)
            pe.wait_ge(S("small_in"), 16 * 12 * (l + 1))
            for n in range(6):
                kt, ch = n // 3, n % 3
                pe.wait_ge(S("pooled"), 4 * l + 2 * kt + 2)
                b = pe_takes(pe, l, "pool", n)
                for cond, c0, c1 in cond_parts(ch):
                    o = SAMPLE0 + ch * CH if cond == 0 else PROMPT0 - c0
                    ins = mm(PS[:, b, c0:c1], pool_mat[:, kt, :], binp[:, kt, o + c0:o + c1], start=True, stop=True)
                ins.then_inc(bank_full[b], 1)
            pe.wait_ge(S("dft_in"), 32 * (l + 1))
            pe.wait_ge(S("dft8"), 8 * (l + 1))
            for n in range(12):
                r, kt = n // 2, n % 2
                ks = slice(kt * P, (kt + 1) * P)
                b = pe_takes(pe, l, "seq", n)
                out = PS[:, b, 0:256]
                if r in (0, 4):
                    ins = mm(out, U[:, r // 4, ks], seq_dft[:, 6 + r // 4, :], start=True, stop=True)
                elif r == 5:
                    ins = mm(out, atok[:, 8, ks], seq_dft[:, 8, :], start=True, stop=True)
                else:
                    mm(out, U[:, 2 * r, ks], seq_dft[:, r - 1, :], start=True, stop=False)
                    ins = mm(out, U[:, 2 * r + 1, ks], seq_dft[:, r + 2, :], start=False, stop=True)
                ins.then_inc(bank_full[b], 1)
            for n in range(10, 12):
                read_out(pe, l, "seq", n)
            cd, sd, nsd = chan_dft[:, 0, :], chan_dft[:, 1, :], chan_dft[:, 2, :]
            for n in range(6):
                kt, part = n // 3, n % 3
                b = pe_takes(pe, l, "chan", n)
                if part == 0:
                    mm(PS[:, b, :], cd, XR[:, kt, 0, 0:4, :], start=True, stop=False)
                    ins = mm(PS[:, b, :], sd, XR[:, kt, 1, 0:4, :], start=False, stop=True)
                elif part == 1:
                    for q in range(4):
                        out = PS[:, b, q * P:(q + 1) * P]
                        mm(out, cd, XR[:, kt, 0, 4 - q, :], start=True, stop=False)
                        ins = mm(out, nsd if q else sd, XR[:, kt, 1, 4 - q, :], start=False, stop=True)
                else:
                    mm(PS[:, b, 0:P], cd, XR[:, kt, 0, 5, :], start=True, stop=False)
                    ins = mm(PS[:, b, 0:P], sd, XR[:, kt, 1, 5, :], start=False, stop=True)
                ins.then_inc(bank_full[b], 1)
            for n in range(6):
                read_out(pe, l, "chan", n)
            def project(i, u):
                pe.wait_ge(S("wq_ready"), l * 8 + 2 * i + u + 1)
                for ch in range(3):
                    b = pe_takes(pe, l, "attn", head_item(l, i, u, AQ + ch))
                    sl = slice(ch * CH, (ch + 1) * CH)
                    for k in range(2):
                        ins = mm(PS[:, b, 0:CH], wq[:, u, k, :], qhatT[:, k, sl], start=(k == 0), stop=(k == 1))
                    ins.then_inc(bank_full[b], 1)
                h = 2 * i + u
                for n in range(3):
                    b = pe_takes(pe, l, "attn", head_item(l, i, u, AK + n))
                    w = min(512, KEYS - 512 * n)
                    mm(PS[0:NOPE, b, 0:w], wkv[:, h * P:h * P + NOPE], ckvT[:, 512 * n:512 * n + w],
                       start=True, stop=True).then_inc(bank_full[b], 1)

            def scores(i, u, j):
                m = u * 9 + j
                buf = m % 2
                g = (l * 4 + i) * 9 + m // 2
                if g:
                    pe.wait_ge(S(f"head_rows{buf}"), g)
                if j == 0:
                    read_out(pe, l, "attn", head_item(l, i, u, AQ + 2))
                    read_out(pe, l, "attn", head_item(l, i, u, AQ + 1))
                    read_out(pe, l, "attn", head_item(l, i, u, AK + 2))
                    read_out(pe, l, "attn", head_item(l, i, u, AK + 1))
                lhs = qT[:, u, j * P:(j + 1) * P]
                if j < 8:
                    for kc in range(3):
                        ins = mm(PS[:, 3 * buf + kc, 0:CH], lhs, kT[:, u, kc * CH:(kc + 1) * CH], start=True, stop=True)
                else:
                    ins = mm(PS[:, 3 * buf, 0:P], lhs, kT[:, u, 9 * P:10 * P], start=True, stop=True)
                ins.then_inc(S(f"scores{buf}"), 1)

            def turn(i, u, j):
                m = u * 9 + j
                buf = m % 2
                pe.wait_ge(S("exped"), (l * 4 + i) * 18 + m + 1)
                for gg in range(3 if j < 8 else 1):
                    n = head_item(l, i, u, AT + 3 * j + gg)
                    b = pe_takes(pe, l, "attn", n)
                    for q in range(3 if j < 8 else 1):
                        ins = nc.tensor.transpose(PS[:, b, q * P:(q + 1) * P],
                                                  probs[:, buf, (3 * gg + q) * P:(3 * gg + q + 1) * P], ident[:])
                    ins.then_inc(bank_full[b], 1)

            def mix(i, u, j):
                m = u * 9 + j
                buf = m % 2
                h = 2 * i + u
                out = PS[:, 3 * buf, CH:CH + VDIM]
                if j < 8:
                    for kt in range(9):
                        if kt % 3 == 0:
                            read_out(pe, l, "attn", head_item(l, i, u, AT + 3 * j + kt // 3))
                        ins = mm(out, probsT[:, buf, kt, :], V[:, kt, h * VDIM:(h + 1) * VDIM], start=(kt == 0), stop=(kt == 8))
                else:
                    read_out(pe, l, "attn", head_item(l, i, u, AT + 24))
                    ins = mm(out, probsT[:, buf, 0, :], V[:, 9, h * VDIM:(h + 1) * VDIM], start=True, stop=True)
                ins.then_inc(S(f"mixed{buf}"), 1)

            for i in range(4):
                for u in range(2):
                    project(i, u)
                    scores(i, u, 0)
                    for j in range(9):
                        if j < 8:
                            scores(i, u, j + 1)
                        turn(i, u, j)
                        mix(i, u, j)
                    if l + 1 < DEPTH:
                        mod_item(l, (l, "attn"), head_item(l, i, u, AM), l + 1, 2 * i + u)
                for buf in range(2):
                    pe.wait_ge(S(f"head_rows{buf}"), (l * 4 + i + 1) * 9)
                for n in range(4):
                    b = pe_takes(pe, l, "attn", head_item(l, i, 2, n))
                    t0, t1 = ((0, 3), (3, 6), (6, 8), (8, 9))[n]
                    for t in range(t0, t1):
                        ins = nc.tensor.transpose(PS[:, b, (t - t0) * P:(t - t0 + 1) * P], O[:, i % 2, t, :], ident[:])
                    ins.then_inc(bank_full[b], 1)
            for j in range(KF):
                for b3 in range(3):
                    u = 3 * j + b3
                    pe.wait_ge(S("split_low"), split_k[("gate", l, u)] + 1)
                    for ch in range(NCH):
                        if u == 0:
                            pe.wait_ge(S(f"xn_back{ch}"), 32 * (l + 1))
                        columns("gate", l, u, ch, 3 * u + ch)
                    nu = unit_at[("branch", l, j)]
                    arrived(pe, nu)
                    k0, k1 = ((0, 2), (2, 4), (4, 8))[b3]
                    if j == 0 and b3 == 2:
                        for n in range(4):
                            read_out(pe, l, "attn", head_item(l, 3, 2, n))
                    for ch in range(NCH):
                        b = pe_takes(pe, l, "branch", 3 * u + ch)
                        for k in range(k0, k1):
                            ins = mm(PS[:, b, 0:CH], raw[:, nu % 4, k, :], BR[:, k, ch * CH:(ch + 1) * CH],
                                     start=(k == k0), stop=(k == k1 - 1))
                        ins.then_inc(bank_full[b], 1)
            for n in range(4):
                pe.wait_ge(S("diag"), 4 * l + n + 1)
                b = pe_takes(pe, l, "gbc", n)
                mm(PS[:, b, :], ones[:], diag[:, n % 2].rearrange("p q m -> p (q m)"), start=True, stop=True)\
                    .then_inc(bank_full[b], 1)
            for p in range(4):
                pe.wait_ge(S("split_low"), split_k[("out", l, 2 * p + 1)] + 1)
                w = bs[:, 2 * (p % 2):2 * (p % 2) + 2]
                for t in range(TT):
                    if p == 0 and t % CT == 0:
                        pe.wait_ge(S("y_low"), KF * (l * NCH + t // CT + 1))
                    b = pe_takes(pe, l, "out", p * TT + t)
                    sl = slice(t * P, (t + 1) * P)
                    for k in range(KF):
                        ins = three_pass(PS[:, b, 0:256], XH[:, k, sl], XL[:, k, sl], w[:, :, 0, k, :], w[:, :, 1, k, :],
                                         k == 0, k == KF - 1)
                    ins.then_inc(bank_full[b], 1)
            if l + 1 < DEPTH:
                for ch in range(NCH):
                    norm_turn(l + 1, ch)

    block_cm.__exit__(None, None, None)


_INS = ["x_prompt", "x_sample", "cache_ckv", "cache_krope", "c", "c_ctx", "norm_g", "w_mod", "b_mod", "w_in",
        "pool_w", "pool_scale", "q_norm_g", "w_q_up", "kv_norm_g", "w_kv_up", "w_br_a", "w_br_b", "w_br_c",
        "w_out", "final_norm_g"]
_OUTS = [(1, SEQ, D), (1, LAT, D), (1, DEPTH, SEQ, KVR), (1, DEPTH, SEQ, ROPE)]


def kernel(**inputs):
    import numpy as _np
    import concourse.bacc as _bacc
    from concourse import mybir as _mybir
    from concourse.bass_utils import run_bass_kernel_spmd as _run

    nc = _bacc.Bacc("TRN2", target_bir_lowering=False, num_devices=1)
    arrays, args, tab = {}, [], {}
    for name in _INS:
        a = _np.ascontiguousarray(inputs[name])
        arrays[f"in_{name}"] = a
        args.append(nc.dram_tensor(f"in_{name}", a.shape, _mybir.dt.from_np(a.dtype), kind="ExternalInput").ap())
    for name, a in make_tables().items():
        a = _np.ascontiguousarray(a, dtype=_np.float32)
        arrays[f"tab_{name}"] = a
        tab[name] = nc.dram_tensor(f"tab_{name}", a.shape, _mybir.dt.float32, kind="ExternalInput").ap()
    outs = [nc.dram_tensor(f"out_{i}", s, _mybir.dt.float32, kind="ExternalOutput").ap() for i, s in enumerate(_OUTS)]
    park = [nc.dram_tensor(n, s, _mybir.dt.float32).ap()
            for n, s in (("park_high", (P, KF, TOK)), ("park_low", (P, KF, TOK)), ("rows_mid", (P, TT, D)))]
    hybrid_step(nc, *args, tab, *outs, *park)
    r = _run(nc, [arrays], core_ids=[0])
    return tuple(r.results[0][f"out_{i}"] for i in range(len(_OUTS)))
```

```python
import numpy as np

from concourse import mybir
from concourse.alu_op_type import AluOpType as ALU

F32 = mybir.dt.float32
F32R = mybir.dt.float32r
ACT = mybir.ActivationFunctionType
AX = mybir.AxisListType

P = 128
D = 1024
DEPTH = 2
SEQ = 128
LAT = 1024
PAST = 128
TOK = LAT + SEQ
TT = TOK // P
KF = D // P
CH = 384
NCH = TOK // CH
CT = CH // P
HEADS = 8
NOPE, ROPE, VDIM = 64, 32, 64
QR, KVR = 256, 128
KEYS = LAT + PAST + SEQ
KS = KEYS // P
EPS = 1e-6
GRID_W = 64
WINDOWS = (2, 4, 8, 16)
COL_AIN, COL_AZ, COL_BIN, COL_BZ, COL_Q, COL_KV, COL_CZ, COL_G = 0, 256, 512, 768, 1024, 1280, 1440, 1952
TOK_COLS = (COL_AIN, COL_Q, COL_CZ - 256)
FEAT_COLS = tuple(COL_BIN + P * i for i in range(2)) + tuple(COL_AZ + P * i for i in range(2)) \
    + tuple(COL_BZ + P * i for i in range(2)) + tuple(COL_CZ + P * i for i in range(4))
PAD = 8
SAMPLE0, PROMPT0, POOLW = PAD, PAD + LAT + 2 * PAD, LAT + SEQ + 4 * PAD
KVW = 224


def make_tables():
    n = np.arange(P)
    def cs(r, length, scale):
        ang = 2 * np.pi * ((n[:, None] * (8 * n[None, :] + r)) % length) / length if length == LAT \
            else 2 * np.pi * ((n[:, None] * n[None, :]) % length) / length
        return np.cos(ang) * scale, np.sin(ang) * scale
    big, small = 1 / np.sqrt(LAT * 64.0), 1 / np.sqrt(SEQ * 64.0)
    dft = []
    for r in (1, 2, 3):
        c, s = cs(r, LAT, big)
        dft.append(np.concatenate([c, -s], 1))
    for r in (1, 2, 3):
        c, s = cs(r, LAT, big)
        dft.append(np.concatenate([s, c], 1))
    for r in (0, 4):
        c, s = cs(r, LAT, big)
        dft.append(np.concatenate([c, -s], 1))
    c, s = cs(0, SEQ, small)
    dft.append(np.concatenate([c, -s], 1))
    seq_dft = np.stack(dft, 1)
    m = np.arange(64)
    ang = 2 * np.pi * ((m[:, None] * m[None, :]) % 64) / 64
    chan = np.zeros((P, 3, P))
    for g in (0, 64):
        chan[g:g + 64, 0, g:g + 64] = np.cos(ang)
        chan[g:g + 64, 1, g:g + 64] = np.sin(ang)
        chan[g:g + 64, 2, g:g + 64] = -np.sin(ang)
    half = ROPE // 2
    freqs = (10000.0 ** (-np.arange(0, half, 2, dtype=np.float32) / half)).astype(np.float32)
    t = np.arange(LAT)
    ar = (t // GRID_W).astype(np.float32)[:, None] * freqs
    ac = (t % GRID_W).astype(np.float32)[:, None] * freqs
    cos = np.concatenate([np.cos(ar), np.cos(ar), np.cos(ac), np.cos(ac)], 1)
    sin = np.concatenate([np.sin(ar), np.sin(ar), np.sin(ac), np.sin(ac)], 1)
    sign = np.tile(np.r_[-np.ones(8), np.ones(8)], 2)
    rope_rows = np.stack([cos.reshape(8, P, ROPE), (sin * sign).reshape(8, P, ROPE)]).transpose(2, 0, 1, 3)
    q_scale = np.zeros((P, TOK))
    q_scale[:NOPE + ROPE] = 1.0
    q_scale[NOPE:NOPE + ROPE, :LAT] = cos.T
    q_scale[NOPE + ROPE:, :LAT] = sin.T
    q_scale *= (NOPE + ROPE) ** -0.5
    edge = np.ones((P, 2, 4, PAD))
    for g, w in enumerate(WINDOWS):
        rows = slice(64 * (g % 2), 64 * (g % 2) + 64)
        for e, (start, length) in enumerate(((0, LAT), (LAT - PAD, LAT), (0, SEQ), (SEQ - PAD, SEQ))):
            pos = start + np.arange(PAD)
            lo = np.clip(pos - w // 2, 0, length - 1)
            hi = np.clip(pos + w - 1 - w // 2, 0, length - 1)
            edge[rows, g // 2, e] = w / (hi - lo + 1.0)
    return {"seq_dft": seq_dft, "chan_dft": chan, "rope_rows": rope_rows, "q_scale": q_scale,
            "edge": edge, "ident": np.eye(P), "vec_zero": np.zeros((P, 2, P))}


def bank_plan():
    phases = []
    def add(layer, name, first, banks, count):
        phases.append(((layer, name), first, banks, count))
    add(0, "vec", 6, 1, 1)
    add(0, "mod", 6, 2, 8)
    add(0, "norm", 6, 2, NCH * KF)
    for l in range(DEPTH):
        add(l, "tok", 0, 3, 3 * TT)
        add(l, "feat", 0, 6, 3 * len(FEAT_COLS))
        add(l, "turn", 6, 2, 14)
        add(l, "val", 6, 2, KS)
        add(l, "pool", 0, 6, 6)
        add(l, "seq", 6, 2, 12)
        add(l, "chan", 0, 6, 6)
        add(l, "attn", 6, 2, len(attention_items(l)))
        add(l, "score", 0, 5, HEADS * (3 * TT - 2))
        add(l, "mixed", 5, 1, HEADS * GROUPS)
        add(l, "gate", 0, 3, 3 * 3 * KF)
        add(l, "branch", 3, 3, 3 * 3 * KF)
        add(l, "gbc", 6, 2, 4)
        add(l, "out", 0, 6, 4 * TT)
        if l + 1 < DEPTH:
            add(l + 1, "norm", 6, 2, NCH * KF)
    used = [0] * 8
    plan = {}
    for key, first, banks, count in phases:
        plan[key] = (first, banks, [used[first + i] for i in range(banks)])
        for i in range(banks):
            used[first + i] += len(range(i, count, banks))
    return plan


TILES = HEADS * TT
GROUPS = 5
K_CHUNKS = ((0, 512), (512, 1024), (1024, 1280))


def parts(m):
    return 1 if m % TT == 8 else 3


def score_item(m, c):
    h, j = divmod(m, TT)
    return h * (3 * TT - 2) + 3 * j + c


STEPS = TILES + 3


def mix_slots(s):
    slots = [None, None, None]
    h, j = divmod(s, TT)
    if j in (3, 5, 7) and h < HEADS:
        slots[1], slots[2] = (h, (j - 3) // 2, (0, 1)), (h, (j - 3) // 2, (2, 3, 4))
    if j in (4, 6, 8) and h < HEADS:
        slots = [(h, (j - 4) // 2, (5,)), (h, (j - 4) // 2, (6, 7)), (h, (j - 4) // 2, (8,))]
    if h and j == 0:
        slots[1], slots[2] = (h - 1, 3, (0, 1)), (h - 1, 3, (2, 3, 4))
    if h and j == 1:
        slots = [(h - 1, 3, (5,)), (h - 1, 3, (6, 7)), (h - 1, 3, (8,))]
    if h and j == 2:
        slots[1] = (h - 1, 4, (0,))
    return slots


def mixed_in(s):
    for slot in mix_slots(s):
        if slot and (slot[2][-1] == 8 or slot[1] == 4):
            return slot[:2]
    return None


def beside(layer, s):
    h, j = divmod(s, TT)
    if 1 <= j <= 6 and h + 1 < HEADS:
        return [("qk"[(j - 1) // 3], h + 1, (j - 1) % 3)]
    if j == 0 and layer + 1 < DEPTH and h < HEADS:
        return [("m", h, 0)]
    return []


def attention_items(layer):
    order = [(kind, 0, i) for kind in "qk" for i in range(3)]
    for s in range(STEPS):
        if 1 <= s <= TILES:
            order += [("t", s - 1, g) for g in range(parts(s - 1))]
        order += beside(layer, s)
    return {key: n for n, key in enumerate(order)}


def hybrid_step(nc, x_prompt, x_sample, cache_ckv, cache_krope, c, c_ctx, norm_g, w_mod, b_mod, w_in,
                pool_w, pool_scale, q_norm_g, w_q_up, kv_norm_g, w_kv_up, w_br_a, w_br_b, w_br_c,
                w_out, final_norm_g, tab, y_prompt, y_sample, new_ckv, new_krope, park_hi, park_lo, rows_mid):
    plan = bank_plan()

    base = 16512
    class Region:
        def __init__(self, start, size):
            self.at, self.end = start, start + size
        def put(self, name, shape, dt=F32):
            t = nc.alloc_sbuf_tensor_at(name, [P] + shape, dt, offset=self.at)
            self.at += (4 * int(np.prod(shape)) + 31) // 32 * 32
            assert self.at <= self.end, name
            return t

    SZ_BR, SZ_RAW, SZ_XY, SZ_R2, SZ_WS, SZ_S = 36864, 16384, 73728, 36864, 16384, 17408
    at = base
    starts = {}
    for name, size in (("br", SZ_BR), ("raw", SZ_RAW), ("xy", SZ_XY), ("r2", SZ_R2), ("ws", SZ_WS), ("s", SZ_S)):
        starts[name] = (at, size)
        at += size
    def region(name):
        return Region(*starts[name])
    const = Region(at, 229344 - at)

    ident = const.put("ident", [P])
    ones = const.put("ones", [P])
    q_scale = const.put("q_scale", [TOK])
    rope_at = const.at
    rope = const.put("rope", [2, 8, ROPE])
    rot_tmp = const.put("rot_tmp", [8, ROPE])
    r = Region(rope_at, 3072)
    rinvT = r.put("sum_inv_rows", [2, 2 * P])
    mixed_out = r.put("mixed_out", [2 * P])
    rinvTp = const.put("sum_inv_prompt", [P])
    edge = const.put("edge", [2, 4, PAD])
    pool_mat = const.put("pool_mat", [2, P])
    modT = const.put("modT", [2, 24, 2])
    scaleT = const.put("scaleT", [KF, 2])
    vecT = const.put("vecT", [84])
    silu_c = const.put("silu_c", [KF, 2])
    ssq = const.put("ssq", [CT])
    root = const.put("root", [CT])
    rinv = const.put("rinv", [CT])
    lat_ssq = const.put("lat_ssq", [2 * TT])
    lat_root = const.put("lat_root", [2 * TT])
    lat_rinv = const.put("lat_rinv", [2 * TT])
    negmax = const.put("negmax", [2])
    partmax = const.put("partmax", [2, 4])
    partsum = const.put("partsum", [2, 4])
    rowsum = const.put("rowsum", [2])
    sum_inv = const.put("sum_inv", [2])
    qtmp_at = const.at
    qtmp = const.put("q_value", [2, CH])
    r = Region(qtmp_at, 1536)
    gq_rows = r.put("gq_rows", [QR])
    gkv_rows = r.put("gkv_rows", [KVR])

    BR = region("br").put("branch", [KF, TOK])
    bs = region("br").put("split_br", [4, 2, KF, P], F32R)
    raw = region("raw").put("raw", [4, KF, P])
    r = region("xy")
    XH = r.put("xn_high", [KF, TOK], F32R)
    XL = r.put("xn_low", [KF, TOK], F32R)
    r = region("xy")
    qhatT = r.put("qhatT", [2, TOK])
    V = r.put("values", [KS, HEADS * VDIM])
    kT = r.put("kT", [2, 2, KEYS], F32R)
    dft_at = r.at
    qT = r.put("qT", [2, 2, TOK], F32R)
    P0 = r.put("probs0", [TOK])
    r = Region(dft_at, starts["xy"][0] + SZ_XY - dft_at)
    seq_dft = r.put("seq_dft", [9, 2 * P])
    chan_dft = r.put("chan_dft", [3, P])
    win_at = r.at
    XR = r.put("spectrum", [2, 2, 6, P])
    r = Region(win_at, 2 * 4 * POOLW)
    winA = r.put("winA", [POOLW])
    winB = r.put("winB", [POOLW])
    H = region("r2").put("rows", [TT, D])
    Y = region("r2").put("merged", [KF, TOK])
    r = region("r2")
    atok = r.put("fourier_in", [TT, 256])
    qlat = r.put("qlat", [TT, QR])
    kvk = r.put("kvk", [KS, KVW])
    binp = r.put("pool_in", [2, POOLW])
    r = region("r2")
    PT = r.put("probsT", [2, 2, 9, 2 * P], F32R)
    ws = region("ws").put("split_ws", [2, 2, KF, P], F32R)
    r = region("ws")
    dft_sd = r.put("dft_sd", [8, 256])
    U = r.put("dft_u", [8, 256])
    r = region("ws")
    P1 = r.put("probs1", [TOK])
    vh = r.put("head_values", [2, KS, P], F32R)
    PTp = r.put("probsT_prompt", [2, P], F32R)
    r = region("ws")
    gateB = r.put("gate_rows", [2, D])
    finalB = r.put("final_rows", [D])
    tmpw = r.put("tmpw", [2, 256])
    r = region("s")
    wq_raw = r.put("wq_raw", [2, HEADS * (NOPE + ROPE)])
    wkv = r.put("wkv", [HEADS * P])
    ckvT = r.put("ckvT", [KEYS])
    wq = r.put("wq_head", [2, 2, P])
    r = region("s")
    xhat = r.put("xhat", [CT, D])
    vtmp = r.put("xn_value", [3, CH])
    r = region("s")
    sig = r.put("sigmoids", [3, CH])
    prod = r.put("products", [2, CH])
    r = region("s")
    diag = r.put("diag", [2, 4, P])
    vec_rows = region("br").put("vec_rows", [P])

    PS = nc.alloc_psum_tensor("ps", [P, 8, 512], F32)

    sems = {}
    def S(name):
        if name not in sems:
            sems[name] = nc.alloc_semaphore(name)
        return sems[name]
    bank_full = [S(f"bank_full{b}") for b in range(8)]
    bank_free = [S(f"bank_free{b}") for b in range(8)]
    raw_in = [S(f"raw_in{s}") for s in range(4)]

    SMALL = 16 * 13
    attn = [attention_items(l) for l in range(DEPTH)]

    def item(l, phase, n):
        first, banks, start = plan[(l, phase)]
        return first + n % banks, start[n % banks] + n // banks

    def pe_takes(pe, l, phase, n):
        b, use = item(l, phase, n)
        if use:
            pe.wait_ge(bank_free[b], use)
        return b

    def filled(eng, l, phase, n):
        b, use = item(l, phase, n)
        eng.wait_ge(bank_full[b], use + 1)
        return b

    def read_out(eng, l, phase, n):
        b, use = item(l, phase, n)
        eng.wait_ge(bank_free[b], use + 1)

    units = []
    unit_at = {}
    def unit(key, srcs, split, release):
        unit_at[key] = len(units)
        units.append((srcs, split, release))
    n_split = 0
    split_plan = []
    last_in = {}
    def split_unit(key, srcs, dest, release):
        nonlocal n_split
        unit(key, srcs, n_split, None)
        split_plan.append((unit_at[key], dest, last_in.get(dest)))
        last_in[dest] = release
        n_split += 1
    def wcols(w, l, c0):
        return w[l].rearrange("(k p) n -> p k n", p=P)[:, :, c0:c0 + P]
    WS0, WS1 = 0, 1
    for m in range(24):
        unit(("mod", 0, m), [(0, KF, wcols(w_mod, 0, m * P))], None, (0, "mod", m // 3))
    for l in range(DEPTH):
        for p in range(3):
            for u in range(2):
                split_unit(("tok", l, 2 * p + u), [(0, KF, wcols(w_in, l, TOK_COLS[p] + u * P))],
                           2 * p + u, (l, "tok", p * TT + TT - 1))
        for u, c0 in enumerate(FEAT_COLS):
            split_unit(("feat", l, u), [(0, KF, wcols(w_in, l, c0))], u % 2, (l, "feat", 3 * u + 2))
        if l + 1 < DEPTH:
            for m in range(24):
                h = m // 3
                unit(("mod", l + 1, m), [(0, KF, wcols(w_mod, l + 1, m * P))], None,
                     (l, "attn", attention_items(l)[("m", h, 0)]))
        for j in range(KF):
            for b in range(3):
                split_unit(("gate", l, 3 * j + b), [(0, KF, wcols(w_in, l, COL_G + b * D + j * P))],
                           (3 * j + b) % 2, (l, "gate", (3 * j + b) * 3 + 2))
            unit(("branch", l, j), [(0, 2, wcols(w_br_a, l, j * P)), (2, 4, wcols(w_br_b, l, j * P)),
                                    (4, 8, wcols(w_br_c, l, j * P))], None, (l, "branch", (3 * j + 2) * 3 + 2))
        for u in range(8):
            split_unit(("out", l, u), [(0, KF, wcols(w_out, l, u * P))], 2 + u % 4,
                       (l, "out", (u // 2) * TT + TT - 1))
    arrivals = [0] * 4
    arrived_at = []
    for n, (srcs, _, _) in enumerate(units):
        arrivals[n % 4] += 16 * len(srcs)
        arrived_at.append(arrivals[n % 4])
    def split_dest(d):
        return ws[:, d] if d < 2 else bs[:, d - 2]
    split_no = {u: k for k, (u, _, _) in enumerate(split_plan)}
    split_k = {key: split_no[n] for key, n in unit_at.items() if n in split_no}

    def turned_place(m, gg, part):
        h, j = divmod(m, TT)
        if j == 8:
            return PTp[:, part:part + 1, :]
        return PT[:, (j // 2) % 2, part, 3 * gg:3 * gg + 3, (j % 2) * P:(j % 2) * P + P]

    def sums_place(m):
        j = m % TT
        return rinvTp[:] if j == 8 else rinvT[:, (j // 2) % 2, (j % 2) * P:(j % 2) * P + P]

    def arrived(eng, n):
        eng.wait_ge(raw_in[n % 4], arrived_at[n])

    def load_units(sp, lo, hi):
        for n in range(lo, hi):
            srcs = units[n][0]
            if n >= 4:
                _, k, release = units[n - 4]
                if k is not None:
                    sp.wait_ge(S("split_low"), k + 1)
                else:
                    filled(sp, *release)
            for k0, k1, src in srcs:
                sp.dma_start(raw[:, n % 4, k0:k1, :], src).then_inc(raw_in[n % 4], 16)

    def cond_parts(c):
        return [(0, 0, CH)] if (c + 1) * CH <= LAT else [(0, 0, LAT - c * CH), (1, LAT - c * CH, CH)]

    block_cm = nc.Block()
    block = block_cm.__enter__()

    @block.sync
    def _(sp):
        for dst, src in ((ident, "ident"), (q_scale, "q_scale"), (edge, "edge"),
                         (pool_mat, "vec_zero")):
            sp.dma_start(dst[:], tab[src]).then_inc(S("const_in"), 16)
        for row, src in ((0, b_mod[0].rearrange("(r p) -> r p", p=P)), (24, b_mod[1].rearrange("(r p) -> r p", p=P)),
                         (48, norm_g.rearrange("l (r p) -> (l r) p", p=P)),
                         (64, pool_scale.rearrange("l (r p) -> (l r) p", p=P)),
                         (68, c.rearrange("a (r p) -> (a r) p", p=P)),
                         (76, c_ctx.rearrange("(r p) -> r p", p=P))):
            sp.dma_start(vec_rows[row:row + src.shape[0], :], src).then_inc(S("vec_in"), 16)
        load_units(sp, 0, 4)
        xs = x_sample[0].rearrange("(t p) d -> p t d", p=P)
        for t in range(TT):
            sp.dma_start(H[:, t, :], xs[:, t, :] if t < 8 else x_prompt[0]).then_inc(S("rows_in"), 16)
        load_units(sp, 4, unit_at[("tok", 0, 4)])
        for l in range(DEPTH):
            for ch in range(NCH):
                sp.wait_ge(S("xn_low"), KF * ((l * NCH) + ch + 1))
                sl = slice(ch * CH, (ch + 1) * CH)
                sp.dma_start(park_hi[:, :, sl], XH[:, :, sl].bitcast(F32)).then_inc(S("parked"), 16)
                sp.dma_start(park_lo[:, :, sl], XL[:, :, sl].bitcast(F32)).then_inc(S("parked"), 16)
            sp.dma_start(gq_rows[:], q_norm_g[l:l + 1, :].broadcast_to([P, QR])).then_inc(S("small_in"), 16)
            sp.dma_start(gkv_rows[:], kv_norm_g[l:l + 1, :].broadcast_to([P, KVR])).then_inc(S("small_in"), 16)
            sp.dma_start(wq_raw[:], w_q_up[l].rearrange("(k p) n -> p k n", p=P)).then_inc(S("small_in"), 16)
            sp.dma_start(wkv[:], w_kv_up[l]).then_inc(S("small_in"), 16)
            sp.dma_start(rope[:], tab["rope_rows"]).then_inc(S("small_in"), 16)
            sp.dma_start(kvk[:, 8, 0:KVR], cache_ckv[0, l]).then_inc(S("small_in"), 16)
            for off in (128, 160, 192):
                sp.dma_start(kvk[:, 8, off:off + ROPE], cache_krope[0, l]).then_inc(S("small_in"), 16)
            if l:
                filled(sp, l - 1, "pool", 5)
            else:
                sp.wait_ge(S("const_in"), 64)
            for g in range(4):
                o = 64 * (g % 2)
                sp.dma_start(pool_mat[o:o + 64, g // 2, o:o + 64], pool_w[l, g]).then_inc(S("small_in"), 16)
            load_units(sp, unit_at[("tok", l, 4)], unit_at[("feat", l, 9)] + 1)
            sp.wait_ge(S("lat_ready"), l + 1)
            sp.dma_start(new_ckv[0, l], kvk[:, 9, 0:KVR]).then_inc(S("stored"), 16)
            sp.dma_start(new_krope[0, l], kvk[:, 9, KVR:KVR + ROPE]).then_inc(S("stored"), 16)
            sp.wait_ge(S("parked"), 16 * 6 * (l + 1))
            filled(sp, l, "feat", 29)
            sp.dma_start(seq_dft[:], tab["seq_dft"]).then_inc(S("dft_in"), 16)
            sp.dma_start(chan_dft[:], tab["chan_dft"]).then_inc(S("dft_in"), 16)
            if l + 1 < DEPTH:
                load_units(sp, unit_at[("mod", l + 1, 0)], unit_at[("mod", l + 1, 23)] + 1)
            load_units(sp, unit_at[("gate", l, 0)], unit_at[("gate", l, 0)] + 4)
            filled(sp, l, "mixed", HEADS * GROUPS - 1)
            for ch in range(NCH):
                sl = slice(ch * CH, (ch + 1) * CH)
                sp.dma_start(XH[:, :, sl].bitcast(F32), park_hi[:, :, sl]).then_inc(S(f"xn_back{ch}"), 16)
                sp.dma_start(XL[:, :, sl].bitcast(F32), park_lo[:, :, sl]).then_inc(S(f"xn_back{ch}"), 16)
            load_units(sp, unit_at[("gate", l, 0)] + 4, unit_at[("out", l, 3)] + 1)
            sp.wait_ge(S("y_low"), NCH * KF * (l + 1))
            for t in range(TT):
                if l == 0:
                    src = xs[:, t, :] if t < 8 else x_prompt[0]
                else:
                    src = rows_mid[:, t, :]
                sp.dma_start(H[:, t, :], src).then_inc(S("rows_in"), 16)
            if l + 1 == DEPTH:
                sp.dma_start(finalB[:], final_norm_g.rearrange("(a d) -> a d", a=1).broadcast_to([P, D])).then_inc(S("final_in"), 16)
            hi = unit_at[("tok", l + 1, 3)] + 1 if l + 1 < DEPTH else len(units)
            load_units(sp, unit_at[("out", l, 4)], unit_at[("out", l, 7)] + 1)
            if l + 1 < DEPTH:
                for t in range(TT):
                    sp.wait_ge(S("rows_added"), 4 * TT * l + 3 * TT + t + 1)
                    sp.dma_start(rows_mid[:, t, :], H[:, t, :]).then_inc(S("mid_out"), 16)
                load_units(sp, unit_at[("out", l, 7)] + 1, hi)
            else:
                ys = y_sample[0].rearrange("(t p) d -> p t d", p=P)
                for t in range(TT):
                    sp.wait_ge(S("y_rows"), t + 1)
                    sp.dma_start(ys[:, t, :] if t < 8 else y_prompt[0], xhat[:, t % CT, :]).then_inc(S("y_out"), 16)
        sp.wait_ge(S("stored"), 16 * 2 * DEPTH)
        sp.wait_ge(S("y_out"), 16 * TT)

    @block.scalar
    def _(act):
        a = nc.scalar

        def split_high(key):
            k = split_k[key]
            n, dest, free_after = split_plan[k]
            arrived(act, n)
            if free_after:
                filled(act, *free_after)
            a.activation(split_dest(dest)[:, 0], raw[:, n % 4], ACT.Copy).then_inc(S("split_high"), 1)

        def squares(l, ch):
            for tt in range(CT):
                t = ch * CT + tt
                if l == 0:
                    act.wait_ge(S("rows_in"), 16 * TT)
                else:
                    act.wait_ge(S("rows_added"), 4 * TT * (l - 1) + 3 * TT + t + 1)
                a.activation(xhat[:, tt, :], H[:, t, :], ACT.Square, accum_out=ssq[:, tt:tt + 1])\
                    .then_inc(S("squares"), 1)

        def norm_act(l, ch):
            g = l * NCH + ch
            if ch:
                filled(act, l, "norm", ch * KF - 1)
            squares(l, ch)
            act.wait_ge(S("mean_sq"), g + 1)
            a.activation(root[:], ssq[:], ACT.Sqrt).then_inc(S("roots"), 1)
            for f in range(KF):
                n = ch * KF + f
                b = filled(act, l, "norm", n)
                if n + l * NCH * KF >= 3:
                    act.wait_ge(S("xn_low"), l * NCH * KF + n - 2)
                if f == 0:
                    act.wait_ge(S("scale_ready"), l + 1)
                parts = cond_parts(ch)
                for i, (cond, c0, c1) in enumerate(parts):
                    ins = a.activation(vtmp[:, n % 3, c0:c1], PS[:, b, c0:c1], ACT.Identity,
                                       bias=modT[:, l % 2, f, cond:cond + 1], scale=scaleT[:, f, cond:cond + 1])
                    if i == len(parts) - 1:
                        ins.then_inc(bank_free[b], 1)

        read_out(act, 0, "vec", 0)
        for cond in range(2):
            a.activation(silu_c[:, :, cond], vecT[:, 68 + 8 * cond:76 + 8 * cond], ACT.Silu).then_inc(S("silu_c"), 1)
        for ch in range(NCH):
            norm_act(0, ch)

        for l in range(DEPTH):
            for u in range(6):
                if u == 2 and l == 0:
                    read_out(act, 0, "vec", 0)
                split_high(("tok", l, u))
            for p in range(3):
                for t in range(TT):
                    b = filled(act, l, "tok", p * TT + t)
                    if t == 0:
                        act.wait_ge(S("xhat"), 9 * l + 3 * (p + 1))
                        if l:
                            act.wait_ge(S("mid_out"), 16 * TT)
                    if p == 0:
                        ins = a.activation(atok[:, t, :], PS[:, b, 0:256], ACT.Copy)
                    elif p == 1:
                        ins = a.activation(qlat[:, t, :], PS[:, b, 0:256], ACT.Copy)
                    else:
                        s = t if t < 8 else 9
                        ins = a.activation(kvk[:, s, 0:160], PS[:, b, 96:256], ACT.Copy)
                    ins.then_inc(bank_free[b], 1)
                if p == 0:
                    split_high(("feat", l, 0))
                    split_high(("feat", l, 1))
            for u in range(10):
                if u == 1:
                    act.wait_ge(S("lat_mean"), l + 1)
                    a.activation(lat_root[:], lat_ssq[:], ACT.Sqrt).then_inc(S("lat_root"), 1)
                if 1 <= u < 9:
                    split_high(("feat", l, u + 1))
                for ch in range(NCH):
                    b = filled(act, l, "feat", 3 * u + ch)
                    if u < 2:
                        if ch == 0:
                            act.wait_ge(S("pads"), l + 1)
                        for cond, c0, c1 in cond_parts(ch):
                            o = SAMPLE0 + ch * CH if cond == 0 else PROMPT0 - c0
                            ins = a.activation(binp[:, u, o + c0:o + c1], PS[:, b, c0:c1], ACT.Copy)
                    else:
                        i = u - 2
                        ins = a.activation(BR[:, i, ch * CH:(ch + 1) * CH], PS[:, b, 0:CH], ACT.Silu)
                    ins.then_inc(bank_free[b], 1)
            act.wait_ge(S("parked"), 16 * 6 * (l + 1))
            for s in range(KS):
                b = filled(act, l, "val", s)
                a.activation(V[:, s, :], PS[:, b, :], ACT.Copy).then_inc(bank_free[b], 1)
            filled(act, l, "pool", 5)
            for n in range(12):
                b = filled(act, l, "seq", n)
                a.activation(XR[:, n % 2, :, n // 2, :], PS[:, b, 0:256].rearrange("p (c m) -> p c m", c=2),
                             ACT.Copy).then_inc(bank_free[b], 1)
            def exps(m, c):
                if c == 0:
                    act.wait_ge(S("negmax"), l * TILES + m + 1)
                    if m >= 2:
                        filled(act, l, "attn", attn[l][("t", m - 2, parts(m - 2) - 1)])
                n = score_item(m, c)
                b = filled(act, l, "score", n)
                w = CH if parts(m) == 3 else P
                a.activation((P0, P1)[m % 2][:, c * CH:c * CH + w], PS[:, b, 0:w], ACT.Exp,
                             bias=negmax[:, m % 2:m % 2 + 1], accum_out=partsum[:, m % 2, c:c + 1])\
                    .then_inc(bank_free[b], 1)

            def turned_high(m, gg):
                h, j = divmod(m, TT)
                b = filled(act, l, "attn", attn[l][("t", m, gg)])
                if m == 0 and gg == 0:
                    act.wait_ge(S("stored"), 32 * (l + 1))
                if gg == 0:
                    if j < 8 and h * 4 + j // 2 >= 2:
                        hh, gr = divmod(h * 4 + j // 2 - 2, 4)
                        filled(act, l, "mixed", hh * GROUPS + gr)
                    if j == 8 and h:
                        filled(act, l, "mixed", h * GROUPS - 1)
                n = parts(m)
                ins = a.activation(turned_place(m, gg, 0), PS[:, b, 0:n * P].rearrange("p (k c) -> p k c", k=n), ACT.Copy)
                if gg == n - 1:
                    ins = a.activation(sums_place(m), PS[:, b, CH:CH + P], ACT.Copy)
                ins.then_inc(S("pt_high"), 1)

            def beside_high(kind, h, i):
                if kind == "q":
                    sl = slice(i * CH, (i + 1) * CH)
                    read_out(act, l, "attn", attn[l][(kind, h, i)])
                    if h >= 2 and i == 0:
                        filled(act, l, "score", (h - 1) * (3 * TT - 2) - 1)
                    a.activation(qT[:, h % 2, 0, sl], qtmp[:, i % 2, :], ACT.Copy).then_inc(S("q_high"), 1)
                elif kind == "k":
                    b = filled(act, l, "attn", attn[l][(kind, h, i)])
                    c0, c1 = K_CHUNKS[i]
                    a.activation(kT[0:NOPE, h % 2, 0, c0:c1], PS[0:NOPE, b, 0:c1 - c0], ACT.Copy)\
                        .then_inc(S("k_high"), 1)

            for kind in "qk":
                for i in range(3):
                    beside_high(kind, 0, i)
            for s in range(STEPS):
                for c in range(3):
                    if c < 2 and 1 <= s <= TILES and c < parts(s - 1):
                        turned_high(s - 1, c)
                    if s < TILES and c < parts(s):
                        exps(s, c)
                if 1 <= s <= TILES and parts(s - 1) == 3:
                    turned_high(s - 1, 2)
                for it in beside(l, s):
                    beside_high(*it)
            filled(act, l, "mixed", HEADS * GROUPS - 1)
            split_high(("gate", l, 0))
            split_high(("gate", l, 1))
            for n in range(24):
                for ch in range(NCH):
                    b = filled(act, l, "gate", 3 * n + ch)
                    if 3 * n + ch >= 3:
                        read_out(act, l, "branch", 3 * n + ch - 3)
                    a.activation(sig[:, ch, :], PS[:, b, 0:CH], ACT.Sigmoid).then_inc(bank_free[b], 1)
                if n + 2 < 24:
                    split_high(("gate", l, n + 2))
            for u in range(4):
                if u == 0:
                    filled(act, l, "branch", 71)
                split_high(("out", l, u))
            filled(act, l, "gate", 71)
            for ch in range(NCH):
                for j in range(KF):
                    if ch == 0:
                        act.wait_ge(S("y_sum"), 48 * l + 6 * j + 6)
                    sl = slice(ch * CH, (ch + 1) * CH)
                    a.activation(XH[:, j, sl], Y[:, j, sl], ACT.Copy).then_inc(S("y_high"), 1)
            for u in range(4, 8):
                split_high(("out", l, u))
            if l + 1 < DEPTH:
                for ch in range(NCH):
                    norm_act(l + 1, ch)
            else:
                for ch in range(NCH):
                    if ch:
                        act.wait_ge(S("y_out"), 16 * CT * ch)
                    squares(DEPTH, ch)
                    act.wait_ge(S("mean_sq"), DEPTH * NCH + ch + 1)
                    a.activation(root[:], ssq[:], ACT.Sqrt).then_inc(S("roots"), 1)

    @block.gpsimd
    def _(pool):
        g = nc.gpsimd

        def split_low(key):
            k = split_k[key]
            n, dest, _ = split_plan[k]
            pool.wait_ge(S("split_high"), k + 1)
            d = split_dest(dest)
            g.tensor_tensor(d[:, 1], raw[:, n % 4], d[:, 0].bitcast(F32), ALU.subtract).then_inc(S("split_low"), 1)

        def norm_low(l, ch):
            for f in range(KF):
                n = l * NCH * KF + ch * KF + f
                pool.wait_ge(S("xn_high"), n + 1)
                sl = slice(ch * CH, (ch + 1) * CH)
                g.tensor_tensor(XL[:, f, sl], vtmp[:, (ch * KF + f) % 3, :], XH[:, f, sl].bitcast(F32),
                                ALU.subtract).then_inc(S("xn_low"), 1)

        g.memset(ones[:], 1.0).then_inc(S("ones"), 1)
        for ch in range(NCH):
            norm_low(0, ch)
        for l in range(DEPTH):
            for u in range(6):
                split_low(("tok", l, u))
            split_low(("feat", l, 0))
            split_low(("feat", l, 1))
            for i, (o, w) in enumerate(((0, PAD), (SAMPLE0 + LAT, 2 * PAD), (PROMPT0 + SEQ, PAD))):
                ins = g.memset(binp[:, :, o:o + w], 0.0)
            ins.then_inc(S("pads"), 1)
            for u in range(2, 10):
                split_low(("feat", l, u))
            filled(pool, l, "feat", 29)
            pool.wait_ge(S("parked"), 16 * 6 * (l + 1))
            for kt in range(2):
                read_out(pool, l, "feat", 3 * kt + 2)
                if kt:
                    pool.wait_ge(S("pooled"), 4 * l + 2)
                w = POOLW
                x = binp[:, kt, :]
                nw = l * 6 + (0 if kt == 0 else 2)
                g.tensor_tensor(winA[:, 1:w], x[:, 0:w - 1], x[:, 1:w], ALU.add).then_inc(S("window"), 1)
                pool.wait_ge(S("window"), nw + 1)
                lo = 64 if kt == 0 else 0
                g.tensor_tensor(winB[lo:, 2:w - 1], winA[lo:, 1:w - 2], winA[lo:, 3:w], ALU.add).then_inc(S("window"), 1)
                if kt:
                    pool.wait_ge(S("window"), nw + 2)
                    g.tensor_tensor(winA[:, 4:w - 3], winB[:, 2:w - 5], winB[:, 6:w - 1], ALU.add).then_inc(S("window"), 1)
                    pool.wait_ge(S("window"), nw + 3)
                    g.tensor_tensor(winB[64:, 8:w - 7], winA[64:, 4:w - 11], winA[64:, 12:w - 3], ALU.add)\
                        .then_inc(S("window"), 1)
            done = {"q_low": l * HEADS * 3, "v_ready": l * 4, "gated": l * HEADS * GROUPS}

            def own_done():
                for name, value in done.items():
                    if value:
                        pool.wait_ge(S(name), value)

            def head_values(pair):
                own_done()
                done["v_ready"] += 1
                if pair:
                    filled(pool, l, "mixed", 2 * pair * GROUPS - 1)
                src = V[:, :, pair * P:(pair + 1) * P]
                g.tensor_copy(vh[:, 0], src).then_inc(S("v_high"), 1)
                pool.wait_ge(S("v_high"), l * 4 + pair + 1)
                g.tensor_tensor(vh[:, 1], src, vh[:, 0].bitcast(F32), ALU.subtract).then_inc(S("v_ready"), 1)

            def q_low(h, i):
                own_done()
                done["q_low"] += 1
                pool.wait_ge(S("q_high"), (l * HEADS + h) * 3 + i + 1)
                sl = slice(i * CH, (i + 1) * CH)
                g.tensor_tensor(qT[:, h % 2, 1, sl], qtmp[:, i % 2, :], qT[:, h % 2, 0, sl].bitcast(F32), ALU.subtract)\
                    .then_inc(S("q_low"), 1)

            def gated(hh, gr):
                own_done()
                done["gated"] += 1
                G = hh * GROUPS + gr
                w = 2 * P if gr < 4 else P
                read_out(pool, l, "mixed", G)
                rows = slice(VDIM * (hh % 2), VDIM * (hh % 2) + VDIM)
                x = BR[rows, 4 + hh // 2, gr * 2 * P:gr * 2 * P + w]
                g.tensor_tensor(x, mixed_out[rows, 0:w], x, ALU.mult).then_inc(S("gated"), 1)

            read_out(pool, l, "feat", 29)
            read_out(pool, l, "val", KS - 1)
            read_out(pool, l, "val", KS - 2)
            filled(pool, l, "seq", 11)
            head_values(0)
            for i in range(3):
                q_low(0, i)
            for s in range(STEPS):
                group = mixed_in(s)
                if group:
                    gated(*group)
                    if group[1] == 4 and group[0] % 2 and group[0] + 1 < HEADS:
                        head_values(group[0] // 2 + 1)
                for kind, hh, i in beside(l, s):
                    if kind == "q":
                        q_low(hh, i)
            own_done()
            split_low(("gate", l, 0))
            split_low(("gate", l, 1))
            for j in range(KF):
                for b in range(3):
                    if b:
                        for ch in range(NCH):
                            q = 6 * j + (b - 1) * 3 + ch
                            sl = slice(ch * CH, (ch + 1) * CH)
                            read_out(pool, l, "branch", (3 * j + b) * 3 + ch)
                            if b == 1:
                                read_out(pool, l, "branch", 3 * j * 3 + ch)
                            else:
                                pool.wait_ge(S("y_sum"), 48 * l + q - 2)
                            g.tensor_tensor(Y[:, j, sl], Y[:, j, sl], prod[:, q % 2, :], ALU.add)\
                                .then_inc(S("y_sum"), 1)
                    n = 3 * j + b
                    if n + 2 < 24:
                        split_low(("gate", l, n + 2))
            for u in range(4):
                split_low(("out", l, u))
            for ch in range(NCH):
                for j in range(KF):
                    n = l * NCH * KF + ch * KF + j
                    pool.wait_ge(S("y_high"), n + 1)
                    sl = slice(ch * CH, (ch + 1) * CH)
                    g.tensor_tensor(XL[:, j, sl], Y[:, j, sl], XH[:, j, sl].bitcast(F32), ALU.subtract)\
                        .then_inc(S("y_low"), 1)
            for p in range(4):
                for t in range(TT):
                    n = p * TT + t
                    if t == 5 and p in (0, 1):
                        split_low(("out", l, 4 + 2 * p))
                        split_low(("out", l, 5 + 2 * p))
                    read_out(pool, l, "out", n)
                    if p == 0:
                        pool.wait_ge(S("rows_in"), 16 * TT * (l + 2))
                    dst = H[:, t, p * 256:(p + 1) * 256]
                    g.tensor_tensor(dst, dst, tmpw[:, n % 2, :], ALU.add).then_inc(S("rows_added"), 1)
            if l + 1 < DEPTH:
                for ch in range(NCH):
                    norm_low(l + 1, ch)

    @block.vector
    def _(dve):
        v = nc.vector

        def norm_scale(l, ch, final=False):
            gch = l * NCH + ch
            dve.wait_ge(S("squares"), CT * (gch + 1))
            v.tensor_scalar(ssq[:], ssq[:], 1.0 / D, EPS, ALU.mult, ALU.add).then_inc(S("mean_sq"), 1)
            dve.wait_ge(S("roots"), gch + 1)
            v.reciprocal(rinv[:], root[:]).then_inc(S("rinv"), 1)
            dve.wait_ge(S("rinv"), gch + 1)
            if final and ch == 0:
                dve.wait_ge(S("final_in"), 16)
            for tt in range(CT):
                t = ch * CT + tt
                if final:
                    v.scalar_tensor_tensor(xhat[:, tt, :], H[:, t, :], rinv[:, tt:tt + 1], finalB[:], ALU.mult,
                                           ALU.mult).then_inc(S("y_rows"), 1)
                else:
                    v.tensor_scalar(xhat[:, tt, :], H[:, t, :], rinv[:, tt:tt + 1], None, ALU.mult)\
                        .then_inc(S("xhat"), 1)

        def norm_dve(l, ch):
            norm_scale(l, ch)
            for f in range(KF):
                n = ch * KF + f
                read_out(dve, l, "norm", n)
                if l and f == 0:
                    filled(dve, l - 1, "out", 3 * TT + ch * CT + CT - 1)
                sl = slice(ch * CH, (ch + 1) * CH)
                v.tensor_copy(XH[:, f, sl], vtmp[:, n % 3, :]).then_inc(S("xn_high"), 1)

        def modulation(l, h, b):
            bias = vecT[:, 24 * l + 3 * h:24 * l + 3 * h + 3].unsqueeze(2).broadcast_to([P, 3, 2])
            v.tensor_tensor(modT[:, l % 2, 3 * h:3 * h + 3, :], PS[:, b, 0:6].rearrange("p (m c) -> p m c", c=2),
                            bias, ALU.add).then_inc(bank_free[b], 1)

        def scales(l):
            for cond in range(2):
                ins = v.scalar_tensor_tensor(scaleT[:, :, cond], modT[:, l % 2, 8:16, cond], 1.0,
                                             vecT[:, 48 + 8 * l:56 + 8 * l], ALU.add, ALU.mult)
            ins.then_inc(S("scale_ready"), 1)

        filled(dve, 0, "vec", 0)
        v.tensor_copy(vecT[:], PS[:, 6, 0:84]).then_inc(bank_free[6], 1)
        read_out(dve, 0, "vec", 0)
        for h in range(8):
            b = filled(dve, 0, "mod", h)
            modulation(0, h, b)
        read_out(dve, 0, "mod", 6)
        read_out(dve, 0, "mod", 7)
        scales(0)
        for ch in range(NCH):
            norm_dve(0, ch)

        for l in range(DEPTH):
            dve.wait_ge(S("small_in"), SMALL * (l + 1))
            for t in range(TT):
                read_out(dve, l, "tok", TT + t)
                v.tensor_tensor_reduce(rot_tmp[:].rearrange("p a b -> p (a b)"), qlat[:, t, :], qlat[:, t, :], 1.0, 0.0, ALU.mult, ALU.add,
                                       lat_ssq[:, t:t + 1]).then_inc(S("lat_ssq"), 1)
                dve.wait_ge(S("lat_ssq"), 18 * l + t + 1)
            for t in range(TT):
                s = t if t < 8 else 9
                read_out(dve, l, "tok", 2 * TT + t)
                v.tensor_tensor_reduce(rot_tmp[:].rearrange("p a b -> p (a b)")[:, 0:KVR], kvk[:, s, 0:KVR],
                                       kvk[:, s, 0:KVR], 1.0, 0.0, ALU.mult, ALU.add,
                                       lat_ssq[:, TT + t:TT + t + 1]).then_inc(S("lat_ssq"), 1)
                dve.wait_ge(S("lat_ssq"), 18 * l + TT + t + 1)
            v.tensor_scalar(lat_ssq[:, 0:TT], lat_ssq[:, 0:TT], 1.0 / QR, EPS, ALU.mult, ALU.add)
            v.tensor_scalar(lat_ssq[:, TT:2 * TT], lat_ssq[:, TT:2 * TT], 1.0 / KVR, EPS, ALU.mult, ALU.add)\
                .then_inc(S("lat_mean"), 1)
            kr = kvk[:, 0:8, KVR:KVR + ROPE]
            kr1 = kvk[:, 0:8, KVR + ROPE:KVR + 2 * ROPE]
            for hf in range(2):
                for a2 in range(2):
                    o = 16 * a2 + 8 * hf
                    oo = 16 * a2 + 8 * (1 - hf)
                    v.tensor_tensor(rot_tmp[:, :, o:o + 8], kr[:, :, oo:oo + 8], rope[:, 1, :, o:o + 8], ALU.mult)\
                        .then_inc(S("rope_rot"), 1)
            v.tensor_tensor(kr1, kr, rope[:, 0], ALU.mult).then_inc(S("rope_rot"), 1)
            dve.wait_ge(S("rope_rot"), 6 * l + 5)
            v.tensor_tensor(kr1, kr1, rot_tmp[:], ALU.add).then_inc(S("rope_rot"), 1)
            dve.wait_ge(S("rope_rot"), 6 * l + 6)
            v.tensor_copy(kvk[:, 0:8, KVR + 2 * ROPE:KVW], kr1)
            for o in (160, 192):
                v.tensor_copy(kvk[:, 9, o:o + ROPE], kvk[:, 9, KVR:KVR + ROPE])
            dve.wait_ge(S("lat_root"), l + 1)
            v.reciprocal(lat_rinv[:], lat_root[:]).then_inc(S("lat_rinv"), 1)
            dve.wait_ge(S("lat_rinv"), l + 1)
            for t in range(TT):
                v.scalar_tensor_tensor(qlat[:, t, :], qlat[:, t, :], lat_rinv[:, t:t + 1], gq_rows[:], ALU.mult, ALU.mult)
            for t in range(TT):
                s = t if t < 8 else 9
                ins = v.scalar_tensor_tensor(kvk[:, s, 0:KVR], kvk[:, s, 0:KVR], lat_rinv[:, TT + t:TT + t + 1],
                                             gkv_rows[:], ALU.mult, ALU.mult)
            ins.then_inc(S("lat_ready"), 1)
            filled(dve, l, "feat", 29)
            dve.wait_ge(S("parked"), 16 * 6 * (l + 1))
            for n in range(6):
                b = filled(dve, l, "turn", n)
                kt, ch = n // 3, n % 3
                v.tensor_copy(qhatT[:, kt, ch * CH:(ch + 1) * CH], PS[:, b, 0:CH]).then_inc(bank_free[b], 1)
            for n in range(4):
                b = filled(dve, l, "turn", 6 + n)
                w = min(CH, KEYS - CH * n)
                v.tensor_copy(ckvT[:, CH * n:CH * n + w], PS[:, b, 0:w]).then_inc(bank_free[b], 1)
            for n in range(4):
                b = filled(dve, l, "turn", 10 + n)
                w = min(CH, KEYS - CH * n)
                sl = slice(CH * n, CH * n + w)
                v.tensor_copy(kT[NOPE:, 0, 0, sl], PS[NOPE:, b, 0:w])
                v.tensor_copy(kT[NOPE:, 1, 0, sl], PS[NOPE:, b, 0:w]).then_inc(S("kr_high"), 1)
                dve.wait_ge(S("kr_high"), 4 * l + n + 1)
                for u in range(2):
                    ins = v.tensor_tensor(kT[NOPE:, u, 1, sl], PS[NOPE:, b, 0:w], kT[NOPE:, u, 0, sl].bitcast(F32),
                                          ALU.subtract)
                ins.then_inc(bank_free[b], 1)
            ss, dd = dft_sd[:, 0:4, :], dft_sd[:, 4:8, :]
            half = 0.5 ** 0.5
            v.tensor_tensor(ss, atok[:, 0:4, :], atok[:, 4:8, :], ALU.add).then_inc(S("dft8"), 1)
            v.tensor_tensor(dd, atok[:, 0:4, :], atok[:, 4:8, :], ALU.subtract).then_inc(S("dft8"), 1)
            dve.wait_ge(S("dft8"), 8 * l + 2)
            v.tensor_tensor(atok[:, 0:2, :], ss[:, 0:2], ss[:, 2:4], ALU.add).then_inc(S("dft8"), 1)
            v.tensor_tensor(U[:, 4], ss[:, 0], ss[:, 2], ALU.subtract)
            v.tensor_tensor(U[:, 5], ss[:, 3], ss[:, 1], ALU.subtract)
            v.tensor_tensor(atok[:, 2], dd[:, 1], dd[:, 3], ALU.subtract).then_inc(S("dft8"), 1)
            v.tensor_tensor(atok[:, 3], dd[:, 1], dd[:, 3], ALU.add).then_inc(S("dft8"), 1)
            dve.wait_ge(S("dft8"), 8 * l + 5)
            v.tensor_tensor(U[:, 0], atok[:, 0], atok[:, 1], ALU.add)
            v.tensor_tensor(U[:, 1], atok[:, 0], atok[:, 1], ALU.subtract)
            v.scalar_tensor_tensor(U[:, 2], atok[:, 2], half, dd[:, 0], ALU.mult, ALU.add)
            v.scalar_tensor_tensor(U[:, 6], atok[:, 2], -half, dd[:, 0], ALU.mult, ALU.add).then_inc(S("dft8"), 1)
            v.scalar_tensor_tensor(U[:, 3], atok[:, 3], -half, dd[:, 2], ALU.mult, ALU.subtract).then_inc(S("dft8"), 1)
            v.scalar_tensor_tensor(U[:, 7], atok[:, 3], -half, dd[:, 2], ALU.mult, ALU.add).then_inc(S("dft8"), 1)
            for kt in range(2):
                dve.wait_ge(S("window"), 6 * l + (2 if kt == 0 else 6))
                for hf, wn in ((0, winA), (1, winB)):
                    rows = slice(64 * hf, 64 * hf + 64)
                    for e, o in enumerate((SAMPLE0, SAMPLE0 + LAT - PAD, PROMPT0, PROMPT0 + SEQ - PAD)):
                        ins = v.tensor_tensor(wn[rows, o:o + PAD], wn[rows, o:o + PAD], edge[rows, kt, e, :], ALU.mult)
                    ins.then_inc(S("edges"), 1)
                dve.wait_ge(S("edges"), 4 * l + 2 * kt + 2)
                for hf, wn in ((0, winA), (1, winB)):
                    rows = slice(64 * hf, 64 * hf + 64)
                    x = binp[rows, kt, PAD:POOLW - PAD]
                    v.scalar_tensor_tensor(x, wn[rows, PAD:POOLW - PAD], 1.0 / WINDOWS[2 * kt + hf], x, ALU.mult,
                                           ALU.subtract).then_inc(S("pooled"), 1)
            for n in range(6):
                kt, ch = n // 3, n % 3
                b = filled(dve, l, "pool", n)
                if n == 0:
                    read_out(dve, l, "feat", 6 * 3 - 1)
                x = BR[:, 2 + kt, ch * CH:(ch + 1) * CH]
                v.scalar_tensor_tensor(x, PS[:, b, 0:CH], vecT[:, 64 + 2 * l + kt:65 + 2 * l + kt], x, ALU.mult, ALU.mult)\
                    .then_inc(bank_free[b], 1)
            for n in range(6):
                kt, part = n // 3, n % 3
                b = filled(dve, l, "chan", n)
                z = BR[:, kt, 0:LAT].rearrange("p (m r) -> p r m", r=8)
                pb = PS[:, b, :].rearrange("p (r m) -> p r m", r=4)
                if part == 0:
                    ins = v.tensor_tensor(z[:, 0:4, :], pb, z[:, 0:4, :], ALU.mult)
                elif part == 1:
                    v.tensor_tensor(z[:, 4, :], pb[:, 0, :], z[:, 4, :], ALU.mult)
                    for r3 in range(3):
                        ins = v.tensor_tensor(z[:, 5 + r3, :], pb[:, 1 + r3, ::-1], z[:, 5 + r3, :], ALU.mult)
                else:
                    zp = BR[:, kt, LAT:TOK]
                    ins = v.tensor_tensor(zp, PS[:, b, 0:P], zp, ALU.mult)
                ins.then_inc(bank_free[b], 1)

            def head_weights(h):
                u = h % 2
                if h >= 2:
                    filled(dve, l, "attn", attn[l][("q", h - 2, 2)])
                c0 = h * (NOPE + ROPE)
                v.tensor_copy(wq[:, u, :, 0:96], wq_raw[:, :, c0:c0 + 96])
                for a2 in range(2):
                    for hf in range(2):
                        dst = wq[:, u, :, 96 + 16 * a2 + 8 * hf:104 + 16 * a2 + 8 * hf]
                        so = c0 + NOPE + 16 * a2 + 8 * (1 - hf)
                        ins = v.tensor_scalar(dst, wq_raw[:, :, so:so + 8], 1.0 if hf else -1.0, None, ALU.mult)
                ins.then_inc(S("wq_ready"), 1)

            def beside_dve(kind, h, i):
                b = filled(dve, l, "attn", attn[l][(kind, h, i)])
                if kind == "q":
                    n = (l * HEADS + h) * 3 + i
                    if n >= 2:
                        dve.wait_ge(S("q_low"), n - 1)
                    sl = slice(i * CH, (i + 1) * CH)
                    v.tensor_tensor(qtmp[:, i % 2, :], PS[:, b, 0:CH], q_scale[:, sl], ALU.mult).then_inc(bank_free[b], 1)
                elif kind == "k":
                    c0, c1 = K_CHUNKS[i]
                    dve.wait_ge(S("k_high"), (l * HEADS + h) * 3 + i + 1)
                    v.tensor_tensor(kT[0:NOPE, h % 2, 1, c0:c1], PS[0:NOPE, b, 0:c1 - c0],
                                    kT[0:NOPE, h % 2, 0, c0:c1].bitcast(F32), ALU.subtract).then_inc(bank_free[b], 1)
                else:
                    modulation(l + 1, h, b)

            def maxes(m, c):
                b = filled(dve, l, "score", score_item(m, c))
                w = CH if parts(m) == 3 else P
                v.tensor_reduce(partmax[:, m % 2, c:c + 1], PS[:, b, 0:w], AX.X, ALU.max).then_inc(S("partmax"), 1)

            def negmaxes(m):
                dve.wait_ge(S("partmax"), l * HEADS * (3 * TT - 2) + score_item(m, parts(m) - 1) + 1)
                if m >= 2:
                    read_out(dve, l, "score", score_item(m - 2, parts(m - 2) - 1))
                v.tensor_reduce(negmax[:, m % 2:m % 2 + 1], partmax[:, m % 2, 0:parts(m)], AX.X, ALU.max, negate=True)\
                    .then_inc(S("negmax"), 1)

            def turned_low(m, gg):
                b = filled(dve, l, "attn", attn[l][("t", m, gg)])
                dve.wait_ge(S("pt_high"), l * HEADS * (3 * TT - 2) + score_item(m, gg) + 1)
                n = parts(m)
                v.tensor_tensor(turned_place(m, gg, 1), PS[:, b, 0:n * P].rearrange("p (k c) -> p k c", k=n),
                                turned_place(m, gg, 0).bitcast(F32), ALU.subtract).then_inc(bank_free[b], 1)

            def sum_inverses(m):
                read_out(dve, l, "score", score_item(m, parts(m) - 1))
                g = l * TILES + m
                v.tensor_reduce(rowsum[:, m % 2:m % 2 + 1], partsum[:, m % 2, 0:parts(m)], AX.X, ALU.add)\
                    .then_inc(S("rowsum"), 1)
                dve.wait_ge(S("rowsum"), g + 1)
                if m >= 2:
                    filled(dve, l, "attn", attn[l][("t", m - 2, parts(m - 2) - 1)])
                v.reciprocal(sum_inv[:, m % 2:m % 2 + 1], rowsum[:, m % 2:m % 2 + 1]).then_inc(S("sum_inv"), 1)

            def unmix(hh, gr):
                G = hh * GROUPS + gr
                g = l * HEADS * GROUPS + G
                w = 2 * P if gr < 4 else P
                b = filled(dve, l, "mixed", G)
                if g:
                    dve.wait_ge(S("gated"), g)
                rows = slice(VDIM * (hh % 2), VDIM * (hh % 2) + VDIM)
                sums = rinvT[rows, gr % 2, :] if gr < 4 else rinvTp[rows, :]
                v.tensor_tensor(mixed_out[rows, 0:w], PS[rows, b, 0:w], sums, ALU.mult).then_inc(bank_free[b], 1)

            head_weights(0)
            head_weights(1)
            for kind in "qk":
                for i in range(3):
                    beside_dve(kind, 0, i)
            maxes(0, 0)
            maxes(0, 1)
            for s in range(STEPS):
                if s < TILES:
                    maxes(s, parts(s) - 1)
                    negmaxes(s)
                if 1 <= s <= TILES:
                    sum_inverses(s - 1)
                if s and mixed_in(s - 1):
                    unmix(*mixed_in(s - 1))
                for c in range(3):
                    if s + 1 < TILES and c < parts(s + 1) - 1:
                        maxes(s + 1, c)
                    if 1 <= s <= TILES and c < parts(s - 1):
                        turned_low(s - 1, c)
                for it in beside(l, s):
                    beside_dve(*it)
                h, j = divmod(s, TT)
                if j == 7 and h + 2 < HEADS:
                    head_weights(h + 2)
            unmix(*mixed_in(STEPS - 1))
            if l + 1 < DEPTH:
                for h in (6, 7):
                    read_out(dve, l, "attn", attn[l][("m", h, 0)])
                scales(l + 1)
            for j in range(KF):
                for b3 in range(3):
                    for ch in range(NCH):
                        n = (3 * j + b3) * 3 + ch
                        read_out(dve, l, "gate", n)
                        b = filled(dve, l, "branch", n)
                        sl = slice(ch * CH, (ch + 1) * CH)
                        if b3 == 0:
                            dst = Y[:, j, sl]
                        else:
                            q = 6 * j + (b3 - 1) * 3 + ch
                            if q >= 2:
                                dve.wait_ge(S("y_sum"), 48 * l + q - 1)
                            dst = prod[:, q % 2, :]
                        v.tensor_tensor(dst, PS[:, b, 0:CH], sig[:, ch, :], ALU.mult).then_inc(bank_free[b], 1)
            filled(dve, l, "gate", 71)
            for n in range(4):
                cond, hf = n // 2, n % 2
                if n >= 2:
                    filled(dve, l, "gbc", n - 2)
                else:
                    dve.wait_ge(S("y_sum"), 48 * (l + 1))
                for q in range(4):
                    f = 16 + 4 * hf + q
                    ins = v.tensor_scalar(diag[:, n % 2, q, :], ident[:], modT[:, l % 2, f, cond:cond + 1], None, ALU.mult)
                ins.then_inc(S("diag"), 1)
            for n in range(4):
                cond, hf = n // 2, n % 2
                b = filled(dve, l, "gbc", n)
                v.tensor_copy(gateB[:, cond, hf * 512:hf * 512 + 512], PS[:, b, :]).then_inc(bank_free[b], 1)
            for n in range(4):
                read_out(dve, l, "gbc", n)
            for p in range(4):
                for t in range(TT):
                    n = p * TT + t
                    b = filled(dve, l, "out", n)
                    if n >= 2:
                        dve.wait_ge(S("rows_added"), 4 * TT * l + n - 1)
                    v.tensor_tensor(tmpw[:, n % 2, :], PS[:, b, 0:256], gateB[:, int(t == 8), p * 256:(p + 1) * 256],
                                    ALU.mult).then_inc(bank_free[b], 1)
            if l + 1 < DEPTH:
                for ch in range(NCH):
                    norm_dve(l + 1, ch)
            else:
                for ch in range(NCH):
                    norm_scale(DEPTH, ch, final=True)

    @block.tensor
    def _(pe):
        mm = nc.tensor.matmul

        def three_pass(out, wh, wl, xh, xl, first, last):
            mm(out, wh, xh, start=first, stop=False)
            mm(out, wh, xl, start=False, stop=False)
            return mm(out, wl, xh, start=False, stop=last)

        def mod_item(l, ph, n, layer, h):
            b = pe_takes(pe, ph[0], ph[1], n)
            for q in range(3):
                m = 3 * h + q
                arrived(pe, unit_at[("mod", layer, m)])
                for k in range(KF):
                    ins = mm(PS[:, b, 2 * q:2 * q + 2], raw[:, unit_at[("mod", layer, m)] % 4, k, :], silu_c[:, k, :],
                             start=(k == 0), stop=(k == KF - 1))
            ins.then_inc(bank_full[b], 1)

        def norm_turn(l, ch):
            pe.wait_ge(S("xhat"), 9 * l + CT * (ch + 1))
            for f in range(KF):
                b = pe_takes(pe, l, "norm", ch * KF + f)
                for tt in range(CT):
                    ins = nc.tensor.transpose(PS[:, b, tt * P:(tt + 1) * P], xhat[:, tt, f * P:(f + 1) * P], ident[:])
                ins.then_inc(bank_full[b], 1)

        pe.wait_ge(S("const_in"), 64)
        pe.wait_ge(S("ones"), 1)
        pe.wait_ge(S("vec_in"), 16 * 6)
        nc.tensor.transpose(PS[:, 6, 0:84], vec_rows[0:84, :], ident[0:84, 0:84]).then_inc(bank_full[6], 1)
        pe.wait_ge(S("silu_c"), 2)
        for h in range(8):
            mod_item(0, (0, "mod"), h, 0, h)
        for ch in range(NCH):
            norm_turn(0, ch)

        for l in range(DEPTH):
            for p in range(3):
                pe.wait_ge(S("split_low"), split_k[("tok", l, 2 * p + 1)] + 1)
                w = ws[:] if p == 0 else bs[:, 2 * (p - 1):2 * p]
                for t in range(TT):
                    if p == 0 and t % CT == 0:
                        pe.wait_ge(S("xn_low"), KF * (l * NCH + t // CT + 1))
                    b = pe_takes(pe, l, "tok", p * TT + t)
                    sl = slice(t * P, (t + 1) * P)
                    out = PS[:, b, 0:256]
                    for k in range(KF):
                        ins = three_pass(out, XH[:, k, sl], XL[:, k, sl], w[:, :, 0, k, :], w[:, :, 1, k, :],
                                         k == 0, k == KF - 1)
                    ins.then_inc(bank_full[b], 1)
            def columns(phase, l, u, ch, n):
                b = pe_takes(pe, l, phase, n)
                sl = slice(ch * CH, (ch + 1) * CH)
                for k in range(KF):
                    ins = three_pass(PS[:, b, 0:CH], ws[:, u % 2, 0, k, :], ws[:, u % 2, 1, k, :], XH[:, k, sl],
                                     XL[:, k, sl], k == 0, k == KF - 1)
                ins.then_inc(bank_full[b], 1)
            for u in range(10):
                pe.wait_ge(S("split_low"), split_k[("feat", l, u)] + 1)
                for ch in range(NCH):
                    columns("feat", l, u, ch, 3 * u + ch)
            pe.wait_ge(S("lat_ready"), l + 1)
            for n in range(6):
                kt, ch = n // 3, n % 3
                b = pe_takes(pe, l, "turn", n)
                for tt in range(CT):
                    ins = nc.tensor.transpose(PS[:, b, tt * P:(tt + 1) * P], qlat[:, ch * CT + tt, kt * P:(kt + 1) * P], ident[:])
                ins.then_inc(bank_full[b], 1)
            for kind in range(2):
                for n in range(4):
                    b = pe_takes(pe, l, "turn", 6 + 4 * kind + n)
                    for s in range(3 * n, min(3 * n + 3, KS)):
                        src = kvk[:, s, 0:P] if kind == 0 else kvk[:, s, KVW - P:KVW]
                        ins = nc.tensor.transpose(PS[:, b, (s - 3 * n) * P:(s - 3 * n + 1) * P], src, ident[:])
                    ins.then_inc(bank_full[b], 1)
            for n in range(4):
                read_out(pe, l, "turn", 6 + n)
            wv = wkv[:].rearrange("p (h c) -> p h c", c=P)[:, :, NOPE:P]
            for s in range(KS):
                b = pe_takes(pe, l, "val", s)
                mm(PS[:, b, :], ckvT[:, s * P:(s + 1) * P], wv, start=True, stop=True).then_inc(bank_full[b], 1)
            pe.wait_ge(S("small_in"), SMALL * (l + 1))
            for n in range(6):
                kt, ch = n // 3, n % 3
                pe.wait_ge(S("pooled"), 4 * l + 2 * kt + 2)
                b = pe_takes(pe, l, "pool", n)
                for cond, c0, c1 in cond_parts(ch):
                    o = SAMPLE0 + ch * CH if cond == 0 else PROMPT0 - c0
                    ins = mm(PS[:, b, c0:c1], pool_mat[:, kt, :], binp[:, kt, o + c0:o + c1], start=True, stop=True)
                ins.then_inc(bank_full[b], 1)
            pe.wait_ge(S("dft_in"), 32 * (l + 1))
            pe.wait_ge(S("dft8"), 8 * (l + 1))
            for n in range(12):
                r, kt = n // 2, n % 2
                ks = slice(kt * P, (kt + 1) * P)
                b = pe_takes(pe, l, "seq", n)
                out = PS[:, b, 0:256]
                if r in (0, 4):
                    ins = mm(out, U[:, r // 4, ks], seq_dft[:, 6 + r // 4, :], start=True, stop=True)
                elif r == 5:
                    ins = mm(out, atok[:, 8, ks], seq_dft[:, 8, :], start=True, stop=True)
                else:
                    mm(out, U[:, 2 * r, ks], seq_dft[:, r - 1, :], start=True, stop=False)
                    ins = mm(out, U[:, 2 * r + 1, ks], seq_dft[:, r + 2, :], start=False, stop=True)
                ins.then_inc(bank_full[b], 1)
            for n in range(10, 12):
                read_out(pe, l, "seq", n)
            cd, sd, nsd = chan_dft[:, 0, :], chan_dft[:, 1, :], chan_dft[:, 2, :]
            for n in range(6):
                kt, part = n // 3, n % 3
                b = pe_takes(pe, l, "chan", n)
                if part == 0:
                    mm(PS[:, b, :], cd, XR[:, kt, 0, 0:4, :], start=True, stop=False)
                    ins = mm(PS[:, b, :], sd, XR[:, kt, 1, 0:4, :], start=False, stop=True)
                elif part == 1:
                    for q in range(4):
                        out = PS[:, b, q * P:(q + 1) * P]
                        mm(out, cd, XR[:, kt, 0, 4 - q, :], start=True, stop=False)
                        ins = mm(out, nsd if q else sd, XR[:, kt, 1, 4 - q, :], start=False, stop=True)
                else:
                    mm(PS[:, b, 0:P], cd, XR[:, kt, 0, 5, :], start=True, stop=False)
                    ins = mm(PS[:, b, 0:P], sd, XR[:, kt, 1, 5, :], start=False, stop=True)
                ins.then_inc(bank_full[b], 1)
            for n in range(6):
                read_out(pe, l, "chan", n)
            def beside_pe(kind, h, i):
                it = attn[l][(kind, h, i)]
                if kind == "m":
                    mod_item(l, (l, "attn"), it, l + 1, h)
                    return
                b = pe_takes(pe, l, "attn", it)
                if kind == "q":
                    if i == 0:
                        pe.wait_ge(S("wq_ready"), l * HEADS + h + 1)
                    sl = slice(i * CH, (i + 1) * CH)
                    for k in range(2):
                        ins = mm(PS[:, b, 0:CH], wq[:, h % 2, k, :], qhatT[:, k, sl], start=(k == 0), stop=(k == 1))
                else:
                    c0, c1 = K_CHUNKS[i]
                    ins = mm(PS[0:NOPE, b, 0:c1 - c0], wkv[:, h * P:h * P + NOPE], ckvT[:, c0:c1], start=True, stop=True)
                ins.then_inc(bank_full[b], 1)

            def scores(m, c):
                h, j = divmod(m, TT)
                if j == 0 and c == 0:
                    pe.wait_ge(S("q_low"), (l * HEADS + h + 1) * 3)
                    for i in range(3):
                        read_out(pe, l, "attn", attn[l][("k", h, i)])
                u = h % 2
                qs = slice(j * P, (j + 1) * P)
                ks = slice(9 * P, 10 * P) if j == 8 else slice(c * CH, (c + 1) * CH)
                b = pe_takes(pe, l, "score", score_item(m, c))
                three_pass(PS[:, b, 0:P if j == 8 else CH], qT[:, u, 0, qs], qT[:, u, 1, qs], kT[:, u, 0, ks],
                           kT[:, u, 1, ks], True, True).then_inc(bank_full[b], 1)

            def turn(m, gg):
                read_out(pe, l, "score", score_item(m, gg))
                b = pe_takes(pe, l, "attn", attn[l][("t", m, gg)])
                for q in range(parts(m)):
                    ins = nc.tensor.transpose(PS[:, b, q * P:(q + 1) * P],
                                              (P0, P1)[m % 2][:, (3 * gg + q) * P:(3 * gg + q + 1) * P], ident[:])
                if gg == parts(m) - 1:
                    pe.wait_ge(S("sum_inv"), l * TILES + m + 1)
                    ins = nc.tensor.transpose(PS[:, b, CH:CH + P], sum_inv[:, m % 2:m % 2 + 1].broadcast_to([P, P]), ident[:])
                ins.then_inc(bank_full[b], 1)

            def mix(hh, gr, kts):
                G = hh * GROUPS + gr
                if kts[0] == 0:
                    pe_takes(pe, l, "mixed", G)
                    if gr == 0:
                        pe.wait_ge(S("v_ready"), l * 4 + hh // 2 + 1)
                w = 2 * P if gr < 4 else P
                b = item(l, "mixed", G)[0]
                for kt in kts:
                    if kt % 3 == 0:
                        for j in ((2 * gr, 2 * gr + 1) if gr < 4 else (8,)):
                            read_out(pe, l, "attn", attn[l][("t", hh * TT + j, kt // 3)])
                    if gr < 4:
                        sl, xh, xl = kt, PT[:, gr % 2, 0, kt, :], PT[:, gr % 2, 1, kt, :]
                    else:
                        sl, xh, xl = 9, PTp[:, 0, :], PTp[:, 1, :]
                    last = kt == 8 or gr == 4
                    ins = three_pass(PS[:, b, 0:w], vh[:, 0, sl, :], vh[:, 1, sl, :], xh, xl, kt == 0, last)
                if last:
                    ins.then_inc(bank_full[b], 1)

            for kind in "qk":
                for i in range(3):
                    beside_pe(kind, 0, i)
            for c in range(3):
                scores(0, c)
            for s in range(STEPS):
                for c in range(3):
                    if s + 1 < TILES and c < parts(s + 1):
                        scores(s + 1, c)
                    if 1 <= s <= TILES and c < parts(s - 1):
                        turn(s - 1, c)
                    if mix_slots(s)[c]:
                        mix(*mix_slots(s)[c])
                for it in beside(l, s):
                    beside_pe(*it)
            for j in range(KF):
                for b3 in range(3):
                    u = 3 * j + b3
                    pe.wait_ge(S("split_low"), split_k[("gate", l, u)] + 1)
                    for ch in range(NCH):
                        if u == 0:
                            pe.wait_ge(S(f"xn_back{ch}"), 32 * (l + 1))
                        columns("gate", l, u, ch, 3 * u + ch)
                    nu = unit_at[("branch", l, j)]
                    arrived(pe, nu)
                    k0, k1 = ((0, 2), (2, 4), (4, 8))[b3]
                    if j == 0 and b3 == 2:
                        pe.wait_ge(S("gated"), HEADS * GROUPS * (l + 1))
                    for ch in range(NCH):
                        b = pe_takes(pe, l, "branch", 3 * u + ch)
                        for k in range(k0, k1):
                            ins = mm(PS[:, b, 0:CH], raw[:, nu % 4, k, :], BR[:, k, ch * CH:(ch + 1) * CH],
                                     start=(k == k0), stop=(k == k1 - 1))
                        ins.then_inc(bank_full[b], 1)
            for n in range(4):
                pe.wait_ge(S("diag"), 4 * l + n + 1)
                b = pe_takes(pe, l, "gbc", n)
                mm(PS[:, b, :], ones[:], diag[:, n % 2].rearrange("p q m -> p (q m)"), start=True, stop=True)\
                    .then_inc(bank_full[b], 1)
            for p in range(4):
                pe.wait_ge(S("split_low"), split_k[("out", l, 2 * p + 1)] + 1)
                w = bs[:, 2 * (p % 2):2 * (p % 2) + 2]
                for t in range(TT):
                    if p == 0 and t % CT == 0:
                        pe.wait_ge(S("y_low"), KF * (l * NCH + t // CT + 1))
                    b = pe_takes(pe, l, "out", p * TT + t)
                    sl = slice(t * P, (t + 1) * P)
                    for k in range(KF):
                        ins = three_pass(PS[:, b, 0:256], XH[:, k, sl], XL[:, k, sl], w[:, :, 0, k, :], w[:, :, 1, k, :],
                                         k == 0, k == KF - 1)
                    ins.then_inc(bank_full[b], 1)
            if l + 1 < DEPTH:
                for ch in range(NCH):
                    norm_turn(l + 1, ch)

    block_cm.__exit__(None, None, None)


_INS = ["x_prompt", "x_sample", "cache_ckv", "cache_krope", "c", "c_ctx", "norm_g", "w_mod", "b_mod", "w_in",
        "pool_w", "pool_scale", "q_norm_g", "w_q_up", "kv_norm_g", "w_kv_up", "w_br_a", "w_br_b", "w_br_c",
        "w_out", "final_norm_g"]
_OUTS = [(1, SEQ, D), (1, LAT, D), (1, DEPTH, SEQ, KVR), (1, DEPTH, SEQ, ROPE)]


def kernel(**inputs):
    import numpy as _np
    import concourse.bacc as _bacc
    from concourse import mybir as _mybir
    from concourse.bass_utils import run_bass_kernel_spmd as _run

    nc = _bacc.Bacc("TRN2", target_bir_lowering=False, num_devices=1)
    arrays, args, tab = {}, [], {}
    for name in _INS:
        a = _np.ascontiguousarray(inputs[name])
        arrays[f"in_{name}"] = a
        args.append(nc.dram_tensor(f"in_{name}", a.shape, _mybir.dt.from_np(a.dtype), kind="ExternalInput").ap())
    for name, a in make_tables().items():
        a = _np.ascontiguousarray(a, dtype=_np.float32)
        arrays[f"tab_{name}"] = a
        tab[name] = nc.dram_tensor(f"tab_{name}", a.shape, _mybir.dt.float32, kind="ExternalInput").ap()
    outs = [nc.dram_tensor(f"out_{i}", s, _mybir.dt.float32, kind="ExternalOutput").ap() for i, s in enumerate(_OUTS)]
    park = [nc.dram_tensor(n, s, _mybir.dt.float32).ap()
            for n, s in (("park_high", (P, KF, TOK)), ("park_low", (P, KF, TOK)), ("rows_mid", (P, TT, D)))]
    hybrid_step(nc, *args, tab, *outs, *park)
    r = _run(nc, [arrays], core_ids=[0])
    return tuple(r.results[0][f"out_{i}"] for i in range(len(_OUTS)))
```

```python
import numpy as np

from concourse import mybir
from concourse.alu_op_type import AluOpType as ALU

F32 = mybir.dt.float32
F32R = mybir.dt.float32r
ACT = mybir.ActivationFunctionType
AX = mybir.AxisListType

P = 128
D = 1024
DEPTH = 2
SEQ = 128
LAT = 1024
PAST = 128
TOK = LAT + SEQ
TT = TOK // P
KF = D // P
CH = 384
NCH = TOK // CH
CT = CH // P
HEADS = 8
NOPE, ROPE, VDIM = 64, 32, 64
QR, KVR = 256, 128
KEYS = LAT + PAST + SEQ
KS = KEYS // P
EPS = 1e-6
GRID_W = 64
WINDOWS = (2, 4, 8, 16)
COL_AIN, COL_AZ, COL_BIN, COL_BZ, COL_Q, COL_KV, COL_CZ, COL_G = 0, 256, 512, 768, 1024, 1280, 1440, 1952
TOK_COLS = (COL_AIN, COL_Q, COL_CZ - 256)
FEAT_COLS = tuple(COL_BIN + P * i for i in range(2)) + tuple(COL_AZ + P * i for i in range(2)) \
    + tuple(COL_BZ + P * i for i in range(2)) + tuple(COL_CZ + P * i for i in range(4))
PAD = 8
SAMPLE0, PROMPT0, POOLW = PAD, PAD + LAT + 2 * PAD, LAT + SEQ + 4 * PAD
KVW = 224


def make_tables():
    n = np.arange(P)
    def cs(r, length, scale):
        ang = 2 * np.pi * ((n[:, None] * (8 * n[None, :] + r)) % length) / length if length == LAT \
            else 2 * np.pi * ((n[:, None] * n[None, :]) % length) / length
        return np.cos(ang) * scale, np.sin(ang) * scale
    big, small = 1 / np.sqrt(LAT * 64.0), 1 / np.sqrt(SEQ * 64.0)
    dft = []
    for r in (1, 2, 3):
        c, s = cs(r, LAT, big)
        dft.append(np.concatenate([c, -s], 1))
    for r in (1, 2, 3):
        c, s = cs(r, LAT, big)
        dft.append(np.concatenate([s, c], 1))
    for r in (0, 4):
        c, s = cs(r, LAT, big)
        dft.append(np.concatenate([c, -s], 1))
    c, s = cs(0, SEQ, small)
    dft.append(np.concatenate([c, -s], 1))
    seq_dft = np.stack(dft, 1)
    m = np.arange(64)
    ang = 2 * np.pi * ((m[:, None] * m[None, :]) % 64) / 64
    chan = np.zeros((P, 3, P))
    for g in (0, 64):
        chan[g:g + 64, 0, g:g + 64] = np.cos(ang)
        chan[g:g + 64, 1, g:g + 64] = np.sin(ang)
        chan[g:g + 64, 2, g:g + 64] = -np.sin(ang)
    half = ROPE // 2
    freqs = (10000.0 ** (-np.arange(0, half, 2, dtype=np.float32) / half)).astype(np.float32)
    t = np.arange(LAT)
    ar = (t // GRID_W).astype(np.float32)[:, None] * freqs
    ac = (t % GRID_W).astype(np.float32)[:, None] * freqs
    cos = np.concatenate([np.cos(ar), np.cos(ar), np.cos(ac), np.cos(ac)], 1)
    sin = np.concatenate([np.sin(ar), np.sin(ar), np.sin(ac), np.sin(ac)], 1)
    sign = np.tile(np.r_[-np.ones(8), np.ones(8)], 2)
    rope_rows = np.stack([cos.reshape(8, P, ROPE), (sin * sign).reshape(8, P, ROPE)]).transpose(2, 0, 1, 3)
    q_scale = np.zeros((P, TOK))
    q_scale[:NOPE + ROPE] = 1.0
    q_scale[NOPE:NOPE + ROPE, :LAT] = cos.T
    q_scale[NOPE + ROPE:, :LAT] = sin.T
    q_scale *= (NOPE + ROPE) ** -0.5
    edge = np.ones((P, 2, 4, PAD))
    for g, w in enumerate(WINDOWS):
        rows = slice(64 * (g % 2), 64 * (g % 2) + 64)
        for e, (start, length) in enumerate(((0, LAT), (LAT - PAD, LAT), (0, SEQ), (SEQ - PAD, SEQ))):
            pos = start + np.arange(PAD)
            lo = np.clip(pos - w // 2, 0, length - 1)
            hi = np.clip(pos + w - 1 - w // 2, 0, length - 1)
            edge[rows, g // 2, e] = w / (hi - lo + 1.0)
    return {"seq_dft": seq_dft, "chan_dft": chan, "rope_rows": rope_rows, "q_scale": q_scale,
            "edge": edge, "ident": np.eye(P), "vec_zero": np.zeros((P, 2, P))}


def bank_plan():
    phases = []
    def add(layer, name, first, banks, count):
        phases.append(((layer, name), first, banks, count))
    add(0, "vec", 6, 1, 1)
    add(0, "mod", 0, 6, 16)
    add(0, "modt", 6, 1, 1)
    add(0, "norm", 6, 2, NCH * KF)
    for l in range(DEPTH):
        add(l, "tok", 0, 3, 3 * TT)
        add(l, "feat", 0, 6, 3 * len(FEAT_COLS))
        add(l, "turn", 0, 6, 14)
        add(l, "val", 6, 2, KS)
        add(l, "seq", 6, 2, 12)
        add(l, "chan", 0, 6, 6)
        add(l, "pool", 0, 6, 6)
        add(l, "attn", 6, 2, len(attention_items()))
        add(l, "score", 0, 5, HEADS * (3 * TT - 2))
        add(l, "mixed", 5, 1, HEADS * GROUPS)
        add(l, "gate", 0, 3, 3 * 3 * KF)
        add(l, "branch", 3, 3, 3 * 3 * KF)
        if l == 0:
            add(l, "later", 6, 2, later(3 * KF - 2)[0])
        add(l, "gbc", 6, 2, 4)
        if l == 0:
            add(l, "last", 6, 2, len(LATER) - later(3 * KF - 2)[0])
        add(l, "out", 0, 6, 4 * TT)
        if l + 1 < DEPTH:
            add(l + 1, "norm", 6, 2, NCH * KF)
    used = [0] * 8
    plan = {}
    for key, first, banks, count in phases:
        plan[key] = (first, banks, [used[first + i] for i in range(banks)])
        for i in range(banks):
            used[first + i] += len(range(i, count, banks))
    return plan


LATER = [(0, m) for m in range(16, 24)] + [(l, m) for l in range(1, DEPTH) for m in range(24)]


NORM_IN_OUT = {5: (0, 0, 3), 6: (0, 3, 6), 7: (0, 6, 8)}
NORM_IN_ROWS = {2: 1, 5: 2}


def later(u):
    return range(len(LATER) * u // (3 * KF), len(LATER) * (u + 1) // (3 * KF))


def later_item(n):
    n0 = later(3 * KF - 2)[0]
    return ("later", n) if n < n0 else ("last", n - n0)


TILES = HEADS * TT
GROUPS = 5
K_CHUNKS = ((0, 512), (512, 1024), (1024, 1280))


def parts(m):
    return 1 if m % TT == 8 else 3


def score_item(m, c):
    h, j = divmod(m, TT)
    return h * (3 * TT - 2) + 3 * j + c


STEPS = TILES + 3
PE_STEP = (("turn", 0), ("score", 0), ("mix", 0), ("turn", 1), ("score", 1), ("mix", 1),
           ("turn", 2), ("score", 2), ("mix", 2))
DVE_STEP = (("beside", 0), ("unmix", 0), ("low", 0), ("sum", 0), ("max", 0), ("low", 1),
            ("max", 1), ("low", 2))
BESIDE_STEPS = (1, 2, 3, 4, 5, 6)


def mix_slots(s):
    slots = [None, None, None]
    h, j = divmod(s, TT)
    if j in (3, 5, 7) and h < HEADS:
        slots[1], slots[2] = (h, (j - 3) // 2, (0, 1)), (h, (j - 3) // 2, (2, 3, 4))
    if j in (4, 6, 8) and h < HEADS:
        slots = [(h, (j - 4) // 2, (5,)), (h, (j - 4) // 2, (6, 7)), (h, (j - 4) // 2, (8,))]
    if h and j == 0:
        slots[1], slots[2] = (h - 1, 3, (0, 1)), (h - 1, 3, (2, 3, 4))
    if h and j == 1:
        slots = [(h - 1, 3, (5,)), (h - 1, 3, (6, 7)), (h - 1, 3, (8,))]
    if h and j == 2:
        slots[1] = (h - 1, 4, (0,))
    return slots


VALUE_PARTS = ((0, 9), (9, 10))


def new_values(s):
    h, j = divmod(s, TT)
    return (h // 2, j - 1) if h % 2 == 0 and 0 < h < HEADS and j in (1, 2) else None


def turned(m, c):
    if not 0 <= m < TILES:
        return None
    if parts(m) == 3:
        return c
    return 0 if c == 2 else None


def mixed_in(s):
    for slot in mix_slots(s):
        if slot and (slot[2][-1] == 8 or slot[1] == 4):
            return slot[:2]
    return None


def beside(s):
    h, j = divmod(s, TT)
    if j in BESIDE_STEPS and h + 1 < HEADS:
        n = BESIDE_STEPS.index(j)
        return [("qk"[n // 3], h + 1, n % 3)]
    return []


def attention_items():
    order = [(kind, 0, i) for kind in "qk" for i in range(3)]
    for s in range(STEPS):
        if 1 <= s <= TILES:
            order += [("t", s - 1, g) for g in range(parts(s - 1))]
        order += beside(s)
    return {key: n for n, key in enumerate(order)}


def hybrid_step(nc, x_prompt, x_sample, cache_ckv, cache_krope, c, c_ctx, norm_g, w_mod, b_mod, w_in,
                pool_w, pool_scale, q_norm_g, w_q_up, kv_norm_g, w_kv_up, w_br_a, w_br_b, w_br_c,
                w_out, final_norm_g, tab, y_prompt, y_sample, new_ckv, new_krope, park_hi, park_lo, rows_mid):
    plan = bank_plan()

    base = 16512
    class Region:
        def __init__(self, start, size):
            self.at, self.end = start, start + size
        def put(self, name, shape, dt=F32):
            t = nc.alloc_sbuf_tensor_at(name, [P] + shape, dt, offset=self.at)
            self.at += (4 * int(np.prod(shape)) + 31) // 32 * 32
            assert self.at <= self.end, name
            return t

    SZ_BR, SZ_RAW, SZ_XY, SZ_R2, SZ_WS, SZ_S = 36864, 16384, 73728, 36864, 16384, 17408
    at = base
    starts = {}
    for name, size in (("br", SZ_BR), ("raw", SZ_RAW), ("xy", SZ_XY), ("r2", SZ_R2), ("ws", SZ_WS), ("s", SZ_S)):
        starts[name] = (at, size)
        at += size
    def region(name):
        return Region(*starts[name])
    const = Region(at, 229344 - at)

    ident = const.put("ident", [P])
    ones = const.put("ones", [P])
    q_scale = const.put("q_scale", [TOK])
    rope_at = const.at
    rope = const.put("rope", [2, 8, ROPE])
    rot_tmp = const.put("rot_tmp", [8, ROPE])
    r = Region(rope_at, 3072)
    rinvT = r.put("sum_inv_rows", [2, 2 * P])
    mixed_out = r.put("mixed_out", [2 * P])
    r = Region(rope_at, 3072)
    mod_sums = r.put("mod_sums", [2, 2, P])
    mod_pair = r.put("mod_pair", [2])
    rinvTp = const.put("sum_inv_prompt", [P])
    edge = const.put("edge", [2, 4, PAD])
    pool_mat = const.put("pool_mat", [2, P])
    modT = const.put("modT", [2, 24, 2])
    scaleT = const.put("scaleT", [KF, 2])
    vecT = const.put("vecT", [84])
    silu_c = const.put("silu_c", [KF, 2])
    ssq = const.put("ssq", [CT])
    root = const.put("root", [CT])
    rinv = const.put("rinv", [CT])
    lat_ssq = const.put("lat_ssq", [2 * TT])
    lat_root = const.put("lat_root", [2 * TT])
    lat_rinv = const.put("lat_rinv", [2 * TT])
    negmax = const.put("negmax", [2])
    partmax = const.put("partmax", [2, 4])
    partsum = const.put("partsum", [2, 4])
    rowsum = const.put("rowsum", [2])
    sum_inv = const.put("sum_inv", [2])
    qtmp_at = const.at
    qtmp = const.put("q_value", [2, CH])
    r = Region(qtmp_at, 1536)
    gq_rows = r.put("gq_rows", [QR])
    gkv_rows = r.put("gkv_rows", [KVR])

    BR = region("br").put("branch", [KF, TOK])
    bs = region("br").put("split_br", [4, 2, KF, P], F32R)
    raw = region("raw").put("raw", [4, KF, P])
    r = region("xy")
    XH = r.put("xn_high", [KF, TOK], F32R)
    XL = r.put("xn_low", [KF, TOK], F32R)
    r = region("xy")
    qhatT = r.put("qhatT", [2, TOK])
    V = r.put("values", [KS, HEADS * VDIM])
    kT = r.put("kT", [2, 2, KEYS], F32R)
    dft_at = r.at
    qT = r.put("qT", [2, 2, TOK], F32R)
    P0 = r.put("probs0", [TOK])
    r = Region(dft_at, starts["xy"][0] + SZ_XY - dft_at)
    seq_dft = r.put("seq_dft", [9, 2 * P])
    chan_dft = r.put("chan_dft", [3, P])
    XR = r.put("spectrum", [2, 2, 6, P])
    H = region("r2").put("rows", [TT, D])
    Y = region("r2").put("merged", [KF, TOK])
    r = region("r2")
    atok = r.put("fourier_in", [TT, 256])
    winA = Region(r.at, 4 * TT * QR).put("winA", [POOLW])
    qlat = r.put("qlat", [TT, QR])
    winB = Region(r.at, 4 * 9 * KVW).put("winB", [POOLW])
    kvk = r.put("kvk", [KS, KVW])
    binp = r.put("pool_in", [2, POOLW])
    r = region("r2")
    PT = r.put("probsT", [2, 2, 9, 2 * P], F32R)
    ws = region("ws").put("split_ws", [2, 2, KF, P], F32R)
    r = region("ws")
    dft_sd = r.put("dft_sd", [8, 256])
    U = r.put("dft_u", [8, 256])
    r = region("ws")
    P1 = r.put("probs1", [TOK])
    vh = r.put("head_values", [2, KS, P], F32R)
    PTp = r.put("probsT_prompt", [2, P], F32R)
    r = region("ws")
    gateB = r.put("gate_rows", [2, D])
    finalB = r.put("final_rows", [D])
    tmpw = r.put("tmpw", [2, 256])
    r = region("s")
    wq_raw = r.put("wq_raw", [2, HEADS * (NOPE + ROPE)])
    wkv = r.put("wkv", [HEADS * P])
    ckvT = r.put("ckvT", [KEYS])
    wq = r.put("wq_head", [2, 2, P])
    r = region("s")
    xhat = r.put("xhat", [CT, D])
    vtmp = r.put("xn_value", [3, CH])
    r = region("s")
    sig = r.put("sigmoids", [3, CH])
    prod = r.put("products", [2, CH])
    wbr = r.put("branch_weights", [2, KF, P])
    diag = Region(qtmp_at, 4 * 2 * CH).put("diag", [4, P])
    r = region("ws")
    vec_rows = r.put("vec_rows", [P])
    mod_flat = r.put("mod_flat", [16, P])

    PS = nc.alloc_psum_tensor("ps", [P, 8, 512], F32)

    sems = {}
    def S(name):
        if name not in sems:
            sems[name] = nc.alloc_semaphore(name)
        return sems[name]
    bank_full = [S(f"bank_full{b}") for b in range(8)]
    bank_free = [S(f"bank_free{b}") for b in range(8)]
    raw_in = [S(f"raw_in{s}") for s in range(4)]

    SMALL = 16 * 13
    attn = attention_items()

    def item(l, phase, n):
        first, banks, start = plan[(l, phase)]
        return first + n % banks, start[n % banks] + n // banks

    def pe_takes(pe, l, phase, n):
        b, use = item(l, phase, n)
        if use:
            pe.wait_ge(bank_free[b], use)
        return b

    def filled(eng, l, phase, n):
        b, use = item(l, phase, n)
        eng.wait_ge(bank_full[b], use + 1)
        return b

    def read_out(eng, l, phase, n):
        b, use = item(l, phase, n)
        eng.wait_ge(bank_free[b], use + 1)

    units = []
    unit_at = {}
    def unit(key, srcs, split, release):
        unit_at[key] = len(units)
        units.append((srcs, split, release))
    n_split = 0
    split_plan = []
    last_in = {}
    def split_unit(key, srcs, dest, release):
        nonlocal n_split
        unit(key, srcs, n_split, None)
        split_plan.append((unit_at[key], dest, last_in.get(dest)))
        last_in[dest] = release
        n_split += 1
    def wcols(w, l, c0):
        return w[l].rearrange("(k p) n -> p k n", p=P)[:, :, c0:c0 + P]
    for m in range(16):
        unit(("mod", 0, m), [(0, KF, wcols(w_mod, 0, m * P))], None, (0, "mod", m))
    for l in range(DEPTH):
        for p in range(3):
            for u in range(2):
                split_unit(("tok", l, 2 * p + u), [(0, KF, wcols(w_in, l, TOK_COLS[p] + u * P))],
                           2 + 2 * (p % 2) + u, (l, "tok", p * TT + TT - 1))
        for u, c0 in enumerate(FEAT_COLS):
            split_unit(("feat", l, u), [(0, KF, wcols(w_in, l, c0))], u % 2, (l, "feat", 3 * u + 2))
        for u in range(3 * KF):
            split_unit(("gate", l, u), [(0, KF, wcols(w_in, l, COL_G + (u % 3) * D + (u // 3) * P))],
                       u % 2, (l, "gate", 3 * u + 2))
            for n in (later(u) if l == 0 else ()):
                lm, m = LATER[n]
                unit(("later", n), [(0, KF, wcols(w_mod, lm, m * P))], None, (16 * (n + 1),))
        for u in range(8):
            split_unit(("out", l, u), [(0, KF, wcols(w_out, l, u * P))], 2 + u % 4,
                       (l, "out", (u // 2) * TT + TT - 1))
    arrivals = [0] * 4
    arrived_at = []
    for n, (srcs, _, _) in enumerate(units):
        arrivals[n % 4] += 16 * len(srcs)
        arrived_at.append(arrivals[n % 4])
    def split_dest(d):
        return ws[:, d] if d < 2 else bs[:, d - 2]
    split_no = {u: k for k, (u, _, _) in enumerate(split_plan)}
    split_k = {key: split_no[n] for key, n in unit_at.items() if n in split_no}

    def turned_place(m, gg, part):
        h, j = divmod(m, TT)
        if j == 8:
            return PTp[:, part:part + 1, :]
        return PT[:, (j // 2) % 2, part, 3 * gg:3 * gg + 3, (j % 2) * P:(j % 2) * P + P]

    def sums_place(m):
        j = m % TT
        return rinvTp[:] if j == 8 else rinvT[:, (j // 2) % 2, (j % 2) * P:(j % 2) * P + P]

    def arrived(eng, n):
        eng.wait_ge(raw_in[n % 4], arrived_at[n])

    def load_units(sp, lo, hi):
        for n in range(lo, hi):
            srcs = units[n][0]
            if n >= 4:
                _, k, release = units[n - 4]
                if k is not None:
                    sp.wait_ge(S("split_low"), k + 1)
                elif len(release) == 1:
                    sp.wait_ge(S("mod_sum"), release[0])
                else:
                    filled(sp, *release)
            for k0, k1, src in srcs:
                sp.dma_start(raw[:, n % 4, k0:k1, :], src).then_inc(raw_in[n % 4], 16)

    def load_branch(sp, l, j):
        for k0, k1, src in ((0, 2, w_br_a), (2, 4, w_br_b), (4, 8, w_br_c)):
            sp.dma_start(wbr[:, j % 2, k0:k1, :], wcols(src, l, j * P)).then_inc(S(f"branch_in{j % 2}"), 16)

    def rows_arrived(eng, ch, times):
        eng.wait_ge(S(f"rows_in{ch}"), 16 * CT * times)

    def low_done(eng, n):
        eng.wait_ge(S("xn_low_even"), (n + 1) // 2)
        if n // 2:
            eng.wait_ge(S("xn_low_odd"), n // 2)

    Y_PIECES = [(ch, j) for ch in range(NCH) for j in range(KF - 1)] + [(ch, KF - 1) for ch in range(NCH)]

    def y_low_done(eng, l, ch):
        eng.wait_ge(S("y_low_even"), 4 * (l * NCH + ch + 1))
        eng.wait_ge(S("y_low_odd"), 4 * NCH * l + 3 * NCH + ch + 1)

    def cond_parts(c):
        return [(0, 0, CH)] if (c + 1) * CH <= LAT else [(0, 0, LAT - c * CH), (1, LAT - c * CH, CH)]

    block_cm = nc.Block()
    block = block_cm.__enter__()

    @block.sync
    def _(sp):
        sp.dma_start(ident[:], tab["ident"]).then_inc(S("ident_in"), 16)
        for row, src in ((0, b_mod[0].rearrange("(r p) -> r p", p=P)), (24, b_mod[1].rearrange("(r p) -> r p", p=P)),
                         (48, norm_g.rearrange("l (r p) -> (l r) p", p=P)),
                         (64, pool_scale.rearrange("l (r p) -> (l r) p", p=P)),
                         (68, c.rearrange("a (r p) -> (a r) p", p=P)),
                         (76, c_ctx.rearrange("(r p) -> r p", p=P))):
            sp.dma_start(vec_rows[row:row + src.shape[0], :], src).then_inc(S("vec_in"), 16)
        xs = x_sample[0].rearrange("(t p) d -> p t d", p=P)

        def load_rows(t):
            sp.dma_start(H[:, t, :], xs[:, t, :] if t < 8 else x_prompt[0]).then_inc(S(f"rows_in{t // CT}"), 16)

        load_units(sp, 0, 6)
        for t in range(CT):
            load_rows(t)
            load_units(sp, 6 + 3 * t, 9 + 3 * t)
        load_units(sp, 15, unit_at[("tok", 0, 2)])
        for dst, src in ((q_scale, "q_scale"), (edge, "edge"), (pool_mat, "vec_zero")):
            sp.dma_start(dst[:], tab[src]).then_inc(S("const_in"), 16)
        for t in range(CT, 2 * CT):
            load_rows(t)
        load_units(sp, unit_at[("tok", 0, 2)], unit_at[("tok", 0, 4)])
        for t in range(2 * CT, TT):
            load_rows(t)
        for l in range(DEPTH):
            for ch in range(NCH):
                low_done(sp, KF * ((l * NCH) + ch + 1))
                sl = slice(ch * CH, (ch + 1) * CH)
                sp.dma_start(park_hi[:, :, sl], XH[:, :, sl].bitcast(F32)).then_inc(S("parked"), 16)
                sp.dma_start(park_lo[:, :, sl], XL[:, :, sl].bitcast(F32)).then_inc(S("parked"), 16)
                if ch == 0:
                    load_units(sp, unit_at[("tok", l, 4)], unit_at[("tok", l, 5)] + 1)
            sp.dma_start(gq_rows[:], q_norm_g[l:l + 1, :].broadcast_to([P, QR])).then_inc(S("small_in"), 16)
            sp.dma_start(gkv_rows[:], kv_norm_g[l:l + 1, :].broadcast_to([P, KVR])).then_inc(S("small_in"), 16)
            sp.dma_start(wq_raw[:], w_q_up[l].rearrange("(k p) n -> p k n", p=P)).then_inc(S("small_in"), 16)
            sp.dma_start(wkv[:], w_kv_up[l]).then_inc(S("small_in"), 16)
            sp.dma_start(rope[:], tab["rope_rows"]).then_inc(S("small_in"), 16)
            sp.dma_start(kvk[:, 8, 0:KVR], cache_ckv[0, l]).then_inc(S("small_in"), 16)
            for off in (128, 160, 192):
                sp.dma_start(kvk[:, 8, off:off + ROPE], cache_krope[0, l]).then_inc(S("small_in"), 16)
            if l:
                filled(sp, l - 1, "pool", 5)
            else:
                sp.wait_ge(S("const_in"), 48)
            for g in range(4):
                o = 64 * (g % 2)
                sp.dma_start(pool_mat[o:o + 64, g // 2, o:o + 64], pool_w[l, g]).then_inc(S("small_in"), 16)
            load_units(sp, unit_at[("feat", l, 0)], unit_at[("feat", l, 9)] + 1)
            sp.wait_ge(S("lat_ready"), l + 1)
            sp.dma_start(new_ckv[0, l], kvk[:, 9, 0:KVR]).then_inc(S("stored"), 16)
            sp.dma_start(new_krope[0, l], kvk[:, 9, KVR:KVR + ROPE]).then_inc(S("stored"), 16)
            sp.wait_ge(S("parked"), 16 * 6 * (l + 1))
            filled(sp, l, "feat", 29)
            sp.dma_start(seq_dft[:], tab["seq_dft"]).then_inc(S("dft_in"), 16)
            sp.dma_start(chan_dft[:], tab["chan_dft"]).then_inc(S("dft_in"), 16)
            load_units(sp, unit_at[("gate", l, 0)], unit_at[("gate", l, 0)] + 4)
            filled(sp, l, "attn", attn[("k", HEADS - 1, 2)])
            for j in range(2):
                load_branch(sp, l, j)
            def back(full, parked, k0, k1, name, ch=None):
                sl = slice(0, TOK) if ch is None else slice(ch * CH, (ch + 1) * CH)
                sp.dma_start(full[:, k0:k1, sl].bitcast(F32), parked[:, k0:k1, sl]).then_inc(S(name), 16)
            filled(sp, l, "score", (HEADS - 1) * (3 * TT - 2) - 1)
            sp.wait_ge(S("v_ready"), HEADS * (l + 1))
            back(XH, park_hi, 0, KF, "xn_back")
            back(XL, park_lo, 3, 4, "xn_back")
            filled(sp, l, "score", HEADS * (3 * TT - 2) - 1)
            back(XL, park_lo, 0, 3, "xn_back")
            back(XL, park_lo, 4, 6, "xn_back")
            filled(sp, l, "attn", attn[("t", TILES - 2, 2)])
            for ch in range(NCH):
                back(XL, park_lo, 6, KF, f"xn_back{ch}", ch)
            at_unit = unit_at[("gate", l, 0)] + 4
            for j in range(2, KF):
                load_units(sp, at_unit, unit_at[("gate", l, 3 * j)])
                at_unit = unit_at[("gate", l, 3 * j)]
                filled(sp, l, "branch", 9 * (j - 1) - 1)
                load_branch(sp, l, j)
            load_units(sp, at_unit, unit_at[("out", l, 3)] + 1)
            y_low_done(sp, l, NCH - 1)
            for t in range(TT):
                if l == 0:
                    src = xs[:, t, :] if t < 8 else x_prompt[0]
                else:
                    src = rows_mid[:, t, :]
                sp.dma_start(H[:, t, :], src).then_inc(S(f"rows_in{t // CT}"), 16)
            if l + 1 == DEPTH:
                sp.dma_start(finalB[:], final_norm_g.rearrange("(a d) -> a d", a=1).broadcast_to([P, D])).then_inc(S("final_in"), 16)
            hi = unit_at[("tok", l + 1, 3)] + 1 if l + 1 < DEPTH else len(units)
            load_units(sp, unit_at[("out", l, 4)], hi)
            if l + 1 < DEPTH:
                for t in range(TT):
                    sp.wait_ge(S("rows_added"), 4 * TT * l + 3 * TT + t + 1)
                    sp.dma_start(rows_mid[:, t, :], H[:, t, :]).then_inc(S(f"mid_out{t // CT}"), 16)
            else:
                ys = y_sample[0].rearrange("(t p) d -> p t d", p=P)
                for t in range(TT):
                    sp.wait_ge(S("y_rows"), t + 1)
                    sp.dma_start(ys[:, t, :] if t < 8 else y_prompt[0], H[:, t, :]).then_inc(S("y_out"), 16)
        sp.wait_ge(S("stored"), 16 * 2 * DEPTH)
        sp.wait_ge(S("y_out"), 16 * TT)

    @block.scalar
    def _(act):
        a = nc.scalar

        def split_high(key):
            k = split_k[key]
            n, dest, free_after = split_plan[k]
            arrived(act, n)
            if free_after:
                filled(act, *free_after)
            a.activation(split_dest(dest)[:, 0], raw[:, n % 4], ACT.Copy).then_inc(S("split_high"), 1)

        def squares(l, ch):
            for tt in range(CT):
                t = ch * CT + tt
                if l == 0:
                    rows_arrived(act, ch, 1)
                else:
                    act.wait_ge(S("rows_added"), 4 * TT * (l - 1) + 3 * TT + t + 1)
                a.activation(xhat[:, tt, :], H[:, t, :], ACT.Square, accum_out=ssq[:, tt:tt + 1])\
                    .then_inc(S("squares"), 1)

        def norm_roots(l, ch):
            if ch:
                filled(act, l, "norm", ch * KF - 1)
            squares(l, ch)
            act.wait_ge(S("mean_sq"), l * NCH + ch + 1)
            a.activation(root[:], ssq[:], ACT.Sqrt).then_inc(S("roots"), 1)

        def norm_values(l, ch, f0, f1):
            for f in range(f0, f1):
                n = ch * KF + f
                b = filled(act, l, "norm", n)
                if n + l * NCH * KF >= 3:
                    low_done(act, l * NCH * KF + n - 2)
                if f == 0:
                    act.wait_ge(S("scale_ready"), l + 1)
                parts = cond_parts(ch)
                for i, (cond, c0, c1) in enumerate(parts):
                    ins = a.activation(vtmp[:, n % 3, c0:c1], PS[:, b, c0:c1], ACT.Identity,
                                       bias=modT[:, l % 2, f, cond:cond + 1], scale=scaleT[:, f, cond:cond + 1])
                    if i == len(parts) - 1:
                        ins.then_inc(bank_free[b], 1)

        read_out(act, 0, "vec", 0)
        for cond in range(2):
            a.activation(silu_c[:, :, cond], vecT[:, 68 + 8 * cond:76 + 8 * cond], ACT.Silu).then_inc(S("silu_c"), 1)
        norm_roots(0, 0)
        split_high(("tok", 0, 0))
        norm_values(0, 0, 0, 4)
        split_high(("tok", 0, 1))
        norm_values(0, 0, 4, KF)

        for l in range(DEPTH):
            norm_roots(l, 1)
            for p in range(3):
                for t in range(TT):
                    b = filled(act, l, "tok", p * TT + t)
                    if t == 0:
                        act.wait_ge(S("xhat"), 9 * l + 3 * (p + 1))
                        if l:
                            act.wait_ge(S(f"mid_out{p}"), 16 * CT)
                    if p == 0:
                        ins = a.activation(atok[:, t, :], PS[:, b, 0:256], ACT.Copy)
                    elif p == 1:
                        ins = a.activation(qlat[:, t, :], PS[:, b, 0:256], ACT.Copy)
                    else:
                        s = t if t < 8 else 9
                        ins = a.activation(kvk[:, s, 0:160], PS[:, b, 96:256], ACT.Copy)
                    ins.then_inc(bank_free[b], 1)
                    if p == 0 and t + 1 in NORM_IN_ROWS:
                        norm_values(l, NORM_IN_ROWS[t + 1], 0, KF)
                    if p == 0 and t == 2:
                        norm_roots(l, 2)
                    if p == 0 and t == 5:
                        for u in (2, 3):
                            split_high(("tok", l, u))
                    if p == 1 and t == 0:
                        for u in (4, 5):
                            split_high(("tok", l, u))
                if p == 1:
                    if l:
                        act.wait_ge(S("rows_added"), 4 * TT * l)
                    split_high(("feat", l, 0))
                    split_high(("feat", l, 1))
            for u in range(10):
                if u == 1:
                    act.wait_ge(S("lat_mean"), l + 1)
                    a.activation(lat_root[:], lat_ssq[:], ACT.Sqrt).then_inc(S("lat_root"), 1)
                if 1 <= u < 9:
                    split_high(("feat", l, u + 1))
                for ch in range(NCH):
                    b = filled(act, l, "feat", 3 * u + ch)
                    if u < 2:
                        if ch == 0:
                            act.wait_ge(S("pads"), l + 1)
                        for cond, c0, c1 in cond_parts(ch):
                            o = SAMPLE0 + ch * CH if cond == 0 else PROMPT0 - c0
                            ins = a.activation(binp[:, u, o + c0:o + c1], PS[:, b, c0:c1], ACT.Copy)
                    else:
                        i = u - 2
                        ins = a.activation(BR[:, i, ch * CH:(ch + 1) * CH], PS[:, b, 0:CH], ACT.Silu)
                    ins.then_inc(bank_free[b], 1)
            act.wait_ge(S("parked"), 16 * 6 * (l + 1))
            for n in range(6):
                b = filled(act, l, "turn", n)
                kt, ch = n // 3, n % 3
                a.activation(qhatT[:, kt, ch * CH:(ch + 1) * CH], PS[:, b, 0:CH], ACT.Copy).then_inc(bank_free[b], 1)
            for s in range(KS):
                b = filled(act, l, "val", s)
                a.activation(V[:, s, :], PS[:, b, :], ACT.Copy).then_inc(bank_free[b], 1)
            for n in range(12):
                b = filled(act, l, "seq", n)
                a.activation(XR[:, n % 2, :, n // 2, :], PS[:, b, 0:256].rearrange("p (c m) -> p c m", c=2),
                             ACT.Copy).then_inc(bank_free[b], 1)
            def exps(m, c):
                if c == 0:
                    act.wait_ge(S("negmax"), l * TILES + m + 1)
                    if m >= 2:
                        filled(act, l, "attn", attn[("t", m - 2, parts(m - 2) - 1)])
                n = score_item(m, c)
                b = filled(act, l, "score", n)
                w = CH if parts(m) == 3 else P
                a.activation((P0, P1)[m % 2][:, c * CH:c * CH + w], PS[:, b, 0:w], ACT.Exp,
                             bias=negmax[:, m % 2:m % 2 + 1], accum_out=partsum[:, m % 2, c:c + 1])\
                    .then_inc(bank_free[b], 1)

            def turned_high(m, gg):
                h, j = divmod(m, TT)
                b = filled(act, l, "attn", attn[("t", m, gg)])
                if m == 0 and gg == 0:
                    act.wait_ge(S("stored"), 32 * (l + 1))
                if gg == 0:
                    if j < 8 and h * 4 + j // 2 >= 2:
                        hh, gr = divmod(h * 4 + j // 2 - 2, 4)
                        filled(act, l, "mixed", hh * GROUPS + gr)
                    if j == 8 and h:
                        filled(act, l, "mixed", h * GROUPS - 1)
                n = parts(m)
                ins = a.activation(turned_place(m, gg, 0), PS[:, b, 0:n * P].rearrange("p (k c) -> p k c", k=n), ACT.Copy)
                if gg == n - 1:
                    ins = a.activation(sums_place(m), PS[:, b, CH:CH + P], ACT.Copy)
                ins.then_inc(S("pt_high"), 1)

            def beside_high(kind, h, i):
                if kind == "q":
                    sl = slice(i * CH, (i + 1) * CH)
                    read_out(act, l, "attn", attn[(kind, h, i)])
                    if h >= 2 and i == 0:
                        filled(act, l, "score", (h - 1) * (3 * TT - 2) - 1)
                    a.activation(qT[:, h % 2, 0, sl], qtmp[:, i % 2, :], ACT.Copy).then_inc(S("q_high"), 1)
                elif kind == "k":
                    b = filled(act, l, "attn", attn[(kind, h, i)])
                    c0, c1 = K_CHUNKS[i]
                    a.activation(kT[0:NOPE, h % 2, 0, c0:c1], PS[0:NOPE, b, 0:c1 - c0], ACT.Copy)\
                        .then_inc(S("k_high"), 1)

            def values_high(pair, part):
                k0, k1 = VALUE_PARTS[part]
                if pair:
                    filled(act, l, "mixed", 2 * pair * GROUPS - 2 + part)
                else:
                    for n in (KS - 2, KS - 1):
                        read_out(act, l, "val", n)
                    filled(act, l, "seq", 11)
                a.activation(vh[:, 0, k0:k1], V[:, k0:k1, pair * P:(pair + 1) * P], ACT.Copy).then_inc(S("v_high"), 1)

            values_high(0, 0)
            values_high(0, 1)
            for kind in "qk":
                for i in range(3):
                    beside_high(kind, 0, i)
            for s in range(STEPS):
                for c in range(3):
                    if turned(s - 1, c) is not None:
                        turned_high(s - 1, turned(s - 1, c))
                    if s < TILES and c < parts(s):
                        exps(s, c)
                    if c == 0 and s:
                        for it in beside(s - 1):
                            if it[0] == "q":
                                beside_high(*it)
                for it in beside(s):
                    if it[0] == "k":
                        beside_high(*it)
                if new_values(s):
                    values_high(*new_values(s))
            filled(act, l, "mixed", HEADS * GROUPS - 1)
            split_high(("gate", l, 0))
            split_high(("gate", l, 1))
            def y_high(ch, j):
                sl = slice(ch * CH, (ch + 1) * CH)
                if ch == 0 and j == 0:
                    act.wait_ge(S("y_sum"), 48 * l + 42)
                if j == KF - 1:
                    act.wait_ge(S("y_sum"), 48 * l + 45 + ch + 1)
                a.activation(XH[:, j, sl], Y[:, j, sl], ACT.Copy).then_inc(S("y_high"), 1)

            for n in range(24):
                for ch in range(NCH):
                    b = filled(act, l, "gate", 3 * n + ch)
                    if 3 * n + ch >= 3:
                        read_out(act, l, "branch", 3 * n + ch - 3)
                    a.activation(sig[:, ch, :], PS[:, b, 0:CH], ACT.Sigmoid).then_inc(bank_free[b], 1)
                    if n == 23:
                        if ch == 0:
                            filled(act, l, "branch", 68)
                            split_high(("out", l, 0))
                            split_high(("out", l, 1))
                        for j in range(KF - 1):
                            y_high(ch, j)
                if n + 2 < 24:
                    split_high(("gate", l, n + 2))
            for ch in range(NCH):
                y_high(ch, KF - 1)
            filled(act, l, "branch", 71)
            for u in (2, 3):
                split_high(("out", l, u))
            for u in range(4, 8):
                split_high(("out", l, u))
            if l + 1 < DEPTH:
                split_high(("tok", l + 1, 0))
                split_high(("tok", l + 1, 1))
                norm_roots(l + 1, 0)
                norm_values(l + 1, 0, 0, KF)
            else:
                for ch in range(NCH):
                    act.wait_ge(S("roots"), DEPTH * NCH + ch)
                    squares(DEPTH, ch)
                    act.wait_ge(S("mean_sq"), DEPTH * NCH + ch + 1)
                    a.activation(root[:], ssq[:], ACT.Sqrt).then_inc(S("roots"), 1)

    @block.gpsimd
    def _(pool):
        g = nc.gpsimd

        def split_low(key):
            k = split_k[key]
            n, dest, _ = split_plan[k]
            pool.wait_ge(S("split_high"), k + 1)
            d = split_dest(dest)
            g.tensor_tensor(d[:, 1], raw[:, n % 4], d[:, 0].bitcast(F32), ALU.subtract).then_inc(S("split_low"), 1)

        def norm_low(l, ch, f0=0, f1=KF):
            for f in range(f0 + f0 % 2, f1, 2):
                n = l * NCH * KF + ch * KF + f
                pool.wait_ge(S("xn_high"), n + 1)
                sl = slice(ch * CH, (ch + 1) * CH)
                g.tensor_tensor(XL[:, f, sl], vtmp[:, (ch * KF + f) % 3, :], XH[:, f, sl].bitcast(F32),
                                ALU.subtract).then_inc(S("xn_low_even"), 1)

        g.memset(ones[:], 1.0).then_inc(S("ones"), 1)
        split_low(("tok", 0, 0))
        norm_low(0, 0, 0, 4)
        split_low(("tok", 0, 1))
        norm_low(0, 0, 4, KF)
        for l in range(DEPTH):
            for u in range(2, 6):
                if u == 2:
                    norm_low(l, 1)
                    norm_low(l, 2)
                split_low(("tok", l, u))
            split_low(("feat", l, 0))
            split_low(("feat", l, 1))
            for i, (o, w) in enumerate(((0, PAD), (SAMPLE0 + LAT, 2 * PAD), (PROMPT0 + SEQ, PAD))):
                ins = g.memset(binp[:, :, o:o + w], 0.0)
            ins.then_inc(S("pads"), 1)
            for u in range(2, 10):
                split_low(("feat", l, u))
            filled(pool, l, "turn", 13)
            for kt in range(2):
                read_out(pool, l, "feat", 3 * kt + 2)
                if kt:
                    pool.wait_ge(S("pooled"), 4 * l + 2)
                w = POOLW
                x = binp[:, kt, :]
                nw = l * 6 + (0 if kt == 0 else 2)
                g.tensor_tensor(winA[:, 1:w], x[:, 0:w - 1], x[:, 1:w], ALU.add).then_inc(S("window"), 1)
                pool.wait_ge(S("window"), nw + 1)
                lo = 64 if kt == 0 else 0
                g.tensor_tensor(winB[lo:, 2:w - 1], winA[lo:, 1:w - 2], winA[lo:, 3:w], ALU.add).then_inc(S("window"), 1)
                if kt:
                    pool.wait_ge(S("window"), nw + 2)
                    g.tensor_tensor(winA[:, 4:w - 3], winB[:, 2:w - 5], winB[:, 6:w - 1], ALU.add).then_inc(S("window"), 1)
                    pool.wait_ge(S("window"), nw + 3)
                    g.tensor_tensor(winB[64:, 8:w - 7], winA[64:, 4:w - 11], winA[64:, 12:w - 3], ALU.add)\
                        .then_inc(S("window"), 1)
            done = {"window": 6 * (l + 1), "q_low": l * HEADS * 3, "v_ready": l * HEADS, "gated": l * HEADS * GROUPS}

            def own_done():
                for name, value in done.items():
                    if value:
                        pool.wait_ge(S(name), value)

            def values_low(pair, part):
                own_done()
                done["v_ready"] += 1
                pool.wait_ge(S("v_high"), l * HEADS + 2 * pair + part + 1)
                k0, k1 = VALUE_PARTS[part]
                g.tensor_tensor(vh[:, 1, k0:k1], V[:, k0:k1, pair * P:(pair + 1) * P], vh[:, 0, k0:k1].bitcast(F32),
                                ALU.subtract).then_inc(S("v_ready"), 1)

            def q_low(h, i):
                own_done()
                done["q_low"] += 1
                pool.wait_ge(S("q_high"), (l * HEADS + h) * 3 + i + 1)
                sl = slice(i * CH, (i + 1) * CH)
                g.tensor_tensor(qT[:, h % 2, 1, sl], qtmp[:, i % 2, :], qT[:, h % 2, 0, sl].bitcast(F32), ALU.subtract)\
                    .then_inc(S("q_low"), 1)

            def gated(hh, gr):
                own_done()
                done["gated"] += 1
                G = hh * GROUPS + gr
                w = 2 * P if gr < 4 else P
                read_out(pool, l, "mixed", G)
                rows = slice(VDIM * (hh % 2), VDIM * (hh % 2) + VDIM)
                x = BR[rows, 4 + hh // 2, gr * 2 * P:gr * 2 * P + w]
                g.tensor_tensor(x, mixed_out[rows, 0:w], x, ALU.mult).then_inc(S("gated"), 1)

            read_out(pool, l, "feat", 29)
            values_low(0, 0)
            values_low(0, 1)
            for i in range(3):
                q_low(0, i)
            for s in range(STEPS):
                group = mixed_in(s)
                new = new_values(s)
                if new:
                    values_low(*new)
                if group:
                    gated(*group)
                for kind, hh, i in beside(s):
                    if kind == "q":
                        q_low(hh, i)
            own_done()
            split_low(("gate", l, 0))
            split_low(("gate", l, 1))
            for j in range(KF):
                for b in range(3):
                    if 3 * j + b == 23:
                        split_low(("out", l, 0))
                        split_low(("out", l, 1))
                        for ch in range(NCH):
                            for jj in range(0, KF, 2):
                                sl = slice(ch * CH, (ch + 1) * CH)
                                pool.wait_ge(S("y_high"), l * NCH * KF + Y_PIECES.index((ch, jj)) + 1)
                                g.tensor_tensor(XL[:, jj, sl], Y[:, jj, sl], XH[:, jj, sl].bitcast(F32), ALU.subtract)\
                                    .then_inc(S("y_low_even"), 1)
                    if b:
                        for ch in range(NCH):
                            q = 6 * j + (b - 1) * 3 + ch
                            sl = slice(ch * CH, (ch + 1) * CH)
                            read_out(pool, l, "branch", (3 * j + b) * 3 + ch)
                            if b == 1:
                                read_out(pool, l, "branch", 3 * j * 3 + ch)
                            else:
                                pool.wait_ge(S("y_sum"), 48 * l + q - 2)
                            g.tensor_tensor(Y[:, j, sl], Y[:, j, sl], prod[:, q % 2, :], ALU.add)\
                                .then_inc(S("y_sum"), 1)
                    n = 3 * j + b
                    if n + 2 < 24:
                        split_low(("gate", l, n + 2))
            for u in (2, 3):
                split_low(("out", l, u))
            for p in range(4):
                for t in range(TT):
                    n = p * TT + t
                    if l + 1 < DEPTH and p == 3 and t in (1, 2):
                        split_low(("tok", l + 1, t - 1))
                    if t == 5 and p in (0, 1):
                        split_low(("out", l, 4 + 2 * p))
                        split_low(("out", l, 5 + 2 * p))
                    read_out(pool, l, "out", n)
                    if p == 0:
                        rows_arrived(pool, t // CT, l + 2)
                    dst = H[:, t, p * 256:(p + 1) * 256]
                    g.tensor_tensor(dst, dst, tmpw[:, n % 2, :], ALU.add).then_inc(S("rows_added"), 1)
                    if l + 1 < DEPTH and p == 3 and t in NORM_IN_OUT:
                        norm_low(l + 1, *NORM_IN_OUT[t])

    @block.vector
    def _(dve):
        v = nc.vector

        def norm_scale(l, ch, final=False):
            gch = l * NCH + ch
            dve.wait_ge(S("squares"), CT * (gch + 1))
            v.tensor_scalar(ssq[:], ssq[:], 1.0 / D, EPS, ALU.mult, ALU.add).then_inc(S("mean_sq"), 1)
            dve.wait_ge(S("roots"), gch + 1)
            v.reciprocal(rinv[:], root[:]).then_inc(S("rinv"), 1)
            dve.wait_ge(S("rinv"), gch + 1)
            if final and ch == 0:
                dve.wait_ge(S("final_in"), 16)
            for tt in range(CT):
                t = ch * CT + tt
                if final:
                    v.scalar_tensor_tensor(H[:, t, :], H[:, t, :], rinv[:, tt:tt + 1], finalB[:], ALU.mult,
                                           ALU.mult).then_inc(S("y_rows"), 1)
                else:
                    v.tensor_scalar(xhat[:, tt, :], H[:, t, :], rinv[:, tt:tt + 1], None, ALU.mult)\
                        .then_inc(S("xhat"), 1)

        def norm_dve(l, ch, f0=0, f1=KF):
            for f in range(f0, f1):
                n = ch * KF + f
                read_out(dve, l, "norm", n)
                if l and f == 0:
                    filled(dve, l - 1, "out", 3 * TT + ch * CT + CT - 1)
                sl = slice(ch * CH, (ch + 1) * CH)
                v.tensor_copy(XH[:, f, sl], vtmp[:, n % 3, :]).then_inc(S("xn_high"), 1)
                if f % 2:
                    dve.wait_ge(S("xn_high"), l * NCH * KF + n + 1)
                    v.tensor_tensor(XL[:, f, sl], vtmp[:, n % 3, :], XH[:, f, sl].bitcast(F32), ALU.subtract)\
                        .then_inc(S("xn_low_odd"), 1)

        def later_modulation(n):
            l, m = LATER[n]
            b = filled(dve, 0, *later_item(n))
            if n:
                dve.wait_ge(S("mod_ready"), n)
            v.tensor_reduce(mod_pair[:], PS[:, b, 0:2 * P].rearrange("p (c m) -> p c m", c=2), AX.X, ALU.add)\
                .then_inc(bank_free[b], 1)
            read_out(dve, 0, *later_item(n))
            v.tensor_tensor(modT[:, l % 2, m, :], mod_pair[:], vecT[:, 24 * l + m:24 * l + m + 1].broadcast_to([P, 2]),
                            ALU.add).then_inc(S("mod_ready"), 1)

        def mod_products(n):
            nu = unit_at[("later", n)]
            arrived(dve, nu)
            for k in range(KF):
                for cond in range(2):
                    acc = mod_sums[:, n % 2, cond, :]
                    w = raw[:, nu % 4, k, :]
                    if k == 0:
                        v.tensor_scalar(acc, w, silu_c[:, k, cond:cond + 1], None, ALU.mult).then_inc(S("mod_sum"), 1)
                    else:
                        dve.wait_ge(S("mod_sum"), 16 * n + 2 * k + cond - 1)
                        v.scalar_tensor_tensor(acc, w, silu_c[:, k, cond:cond + 1], acc, ALU.mult, ALU.add)\
                            .then_inc(S("mod_sum"), 1)

        def scales(l):
            for cond in range(2):
                ins = v.scalar_tensor_tensor(scaleT[:, :, cond], modT[:, l % 2, 8:16, cond], 1.0,
                                             vecT[:, 48 + 8 * l:56 + 8 * l], ALU.add, ALU.mult)
            ins.then_inc(S("scale_ready"), 1)

        filled(dve, 0, "vec", 0)
        v.tensor_copy(vecT[:], PS[:, 6, 0:84]).then_inc(bank_free[6], 1)
        read_out(dve, 0, "vec", 0)
        for m in range(16):
            if m == 10:
                norm_scale(0, 0)
            b = filled(dve, 0, "mod", m)
            v.tensor_copy(mod_flat[0:2, m, :], PS[0:2, b, 0:P]).then_inc(bank_free[b], 1)
        b = filled(dve, 0, "modt", 0)
        v.tensor_tensor(modT[:, 0, 0:16, :], PS[:, b, 0:32].rearrange("p (m c) -> p m c", c=2),
                        vecT[:, 0:16].unsqueeze(2).broadcast_to([P, 16, 2]), ALU.add).then_inc(bank_free[b], 1)
        read_out(dve, 0, "modt", 0)
        scales(0)
        norm_dve(0, 0)

        for l in range(DEPTH):
            for ch in (1, 2):
                norm_scale(l, ch)
                norm_dve(l, ch)
            dve.wait_ge(S("small_in"), SMALL * (l + 1))
            if l == 0:
                dve.wait_ge(S("const_in"), 48)
            for t in range(TT):
                read_out(dve, l, "tok", TT + t)
                v.tensor_tensor_reduce(rot_tmp[:].rearrange("p a b -> p (a b)"), qlat[:, t, :], qlat[:, t, :], 1.0, 0.0, ALU.mult, ALU.add,
                                       lat_ssq[:, t:t + 1]).then_inc(S("lat_ssq"), 1)
                dve.wait_ge(S("lat_ssq"), 18 * l + t + 1)
            for t in range(TT):
                s = t if t < 8 else 9
                read_out(dve, l, "tok", 2 * TT + t)
                v.tensor_tensor_reduce(rot_tmp[:].rearrange("p a b -> p (a b)")[:, 0:KVR], kvk[:, s, 0:KVR],
                                       kvk[:, s, 0:KVR], 1.0, 0.0, ALU.mult, ALU.add,
                                       lat_ssq[:, TT + t:TT + t + 1]).then_inc(S("lat_ssq"), 1)
                dve.wait_ge(S("lat_ssq"), 18 * l + TT + t + 1)
            v.tensor_scalar(lat_ssq[:, 0:TT], lat_ssq[:, 0:TT], 1.0 / QR, EPS, ALU.mult, ALU.add)
            v.tensor_scalar(lat_ssq[:, TT:2 * TT], lat_ssq[:, TT:2 * TT], 1.0 / KVR, EPS, ALU.mult, ALU.add)\
                .then_inc(S("lat_mean"), 1)
            kr = kvk[:, 0:8, KVR:KVR + ROPE]
            kr1 = kvk[:, 0:8, KVR + ROPE:KVR + 2 * ROPE]
            for hf in range(2):
                for a2 in range(2):
                    o = 16 * a2 + 8 * hf
                    oo = 16 * a2 + 8 * (1 - hf)
                    v.tensor_tensor(rot_tmp[:, :, o:o + 8], kr[:, :, oo:oo + 8], rope[:, 1, :, o:o + 8], ALU.mult)\
                        .then_inc(S("rope_rot"), 1)
            v.tensor_tensor(kr1, kr, rope[:, 0], ALU.mult).then_inc(S("rope_rot"), 1)
            dve.wait_ge(S("rope_rot"), 6 * l + 5)
            v.tensor_tensor(kr1, kr1, rot_tmp[:], ALU.add).then_inc(S("rope_rot"), 1)
            dve.wait_ge(S("rope_rot"), 6 * l + 6)
            v.tensor_copy(kvk[:, 0:8, KVR + 2 * ROPE:KVW], kr1)
            for o in (160, 192):
                v.tensor_copy(kvk[:, 9, o:o + ROPE], kvk[:, 9, KVR:KVR + ROPE])
            dve.wait_ge(S("lat_root"), l + 1)
            v.reciprocal(lat_rinv[:], lat_root[:]).then_inc(S("lat_rinv"), 1)
            dve.wait_ge(S("lat_rinv"), l + 1)
            for t in range(TT):
                v.scalar_tensor_tensor(qlat[:, t, :], qlat[:, t, :], lat_rinv[:, t:t + 1], gq_rows[:], ALU.mult, ALU.mult)
            for t in range(TT):
                s = t if t < 8 else 9
                ins = v.scalar_tensor_tensor(kvk[:, s, 0:KVR], kvk[:, s, 0:KVR], lat_rinv[:, TT + t:TT + t + 1],
                                             gkv_rows[:], ALU.mult, ALU.mult)
            ins.then_inc(S("lat_ready"), 1)
            filled(dve, l, "feat", 29)
            dve.wait_ge(S("parked"), 16 * 6 * (l + 1))
            for n in range(4):
                b = filled(dve, l, "turn", 6 + n)
                w = min(CH, KEYS - CH * n)
                v.tensor_copy(ckvT[:, CH * n:CH * n + w], PS[:, b, 0:w]).then_inc(bank_free[b], 1)
            ss, dd = dft_sd[:, 0:4, :], dft_sd[:, 4:8, :]
            half = 0.5 ** 0.5
            v.tensor_tensor(ss, atok[:, 0:4, :], atok[:, 4:8, :], ALU.add).then_inc(S("dft8"), 1)
            v.tensor_tensor(dd, atok[:, 0:4, :], atok[:, 4:8, :], ALU.subtract).then_inc(S("dft8"), 1)
            dve.wait_ge(S("dft8"), 8 * l + 2)
            v.tensor_tensor(atok[:, 0:2, :], ss[:, 0:2], ss[:, 2:4], ALU.add).then_inc(S("dft8"), 1)
            v.tensor_tensor(U[:, 4], ss[:, 0], ss[:, 2], ALU.subtract)
            v.tensor_tensor(U[:, 5], ss[:, 3], ss[:, 1], ALU.subtract)
            v.tensor_tensor(atok[:, 2], dd[:, 1], dd[:, 3], ALU.subtract).then_inc(S("dft8"), 1)
            v.tensor_tensor(atok[:, 3], dd[:, 1], dd[:, 3], ALU.add).then_inc(S("dft8"), 1)
            dve.wait_ge(S("dft8"), 8 * l + 5)
            v.tensor_tensor(U[:, 0], atok[:, 0], atok[:, 1], ALU.add)
            v.tensor_tensor(U[:, 1], atok[:, 0], atok[:, 1], ALU.subtract)
            v.scalar_tensor_tensor(U[:, 2], atok[:, 2], half, dd[:, 0], ALU.mult, ALU.add)
            v.scalar_tensor_tensor(U[:, 6], atok[:, 2], -half, dd[:, 0], ALU.mult, ALU.add).then_inc(S("dft8"), 1)
            v.scalar_tensor_tensor(U[:, 3], atok[:, 3], -half, dd[:, 2], ALU.mult, ALU.subtract).then_inc(S("dft8"), 1)
            v.scalar_tensor_tensor(U[:, 7], atok[:, 3], -half, dd[:, 2], ALU.mult, ALU.add).then_inc(S("dft8"), 1)
            for n in range(4):
                b = filled(dve, l, "turn", 10 + n)
                w = min(CH, KEYS - CH * n)
                sl = slice(CH * n, CH * n + w)
                v.tensor_copy(kT[NOPE:, 0, 0, sl], PS[NOPE:, b, 0:w])
                v.tensor_copy(kT[NOPE:, 1, 0, sl], PS[NOPE:, b, 0:w]).then_inc(S("kr_high"), 1)
                dve.wait_ge(S("kr_high"), 4 * l + n + 1)
                for u in range(2):
                    ins = v.tensor_tensor(kT[NOPE:, u, 1, sl], PS[NOPE:, b, 0:w], kT[NOPE:, u, 0, sl].bitcast(F32),
                                          ALU.subtract)
                ins.then_inc(bank_free[b], 1)
            def head_weights(h):
                u = h % 2
                if h >= 2:
                    filled(dve, l, "attn", attn[("q", h - 2, 2)])
                c0 = h * (NOPE + ROPE)
                v.tensor_copy(wq[:, u, :, 0:96], wq_raw[:, :, c0:c0 + 96])
                for a2 in range(2):
                    for hf in range(2):
                        dst = wq[:, u, :, 96 + 16 * a2 + 8 * hf:104 + 16 * a2 + 8 * hf]
                        so = c0 + NOPE + 16 * a2 + 8 * (1 - hf)
                        ins = v.tensor_scalar(dst, wq_raw[:, :, so:so + 8], 1.0 if hf else -1.0, None, ALU.mult)
                ins.then_inc(S("wq_ready"), 1)

            def beside_dve(kind, h, i):
                b = filled(dve, l, "attn", attn[(kind, h, i)])
                if kind == "q":
                    n = (l * HEADS + h) * 3 + i
                    if n >= 2:
                        dve.wait_ge(S("q_low"), n - 1)
                    sl = slice(i * CH, (i + 1) * CH)
                    v.tensor_tensor(qtmp[:, i % 2, :], PS[:, b, 0:CH], q_scale[:, sl], ALU.mult).then_inc(bank_free[b], 1)
                elif kind == "k":
                    c0, c1 = K_CHUNKS[i]
                    dve.wait_ge(S("k_high"), (l * HEADS + h) * 3 + i + 1)
                    v.tensor_tensor(kT[0:NOPE, h % 2, 1, c0:c1], PS[0:NOPE, b, 0:c1 - c0],
                                    kT[0:NOPE, h % 2, 0, c0:c1].bitcast(F32), ALU.subtract).then_inc(bank_free[b], 1)

            def pool_edges(kt):
                dve.wait_ge(S("window"), 6 * l + (2 if kt == 0 else 6))
                for hf, wn in ((0, winA), (1, winB)):
                    rows = slice(64 * hf, 64 * hf + 64)
                    for e, o in enumerate((SAMPLE0, SAMPLE0 + LAT - PAD, PROMPT0, PROMPT0 + SEQ - PAD)):
                        ins = v.tensor_tensor(wn[rows, o:o + PAD], wn[rows, o:o + PAD], edge[rows, kt, e, :], ALU.mult)
                    ins.then_inc(S("edges"), 1)
                dve.wait_ge(S("edges"), 4 * l + 2 * kt + 2)
                for hf, wn in ((0, winA), (1, winB)):
                    rows = slice(64 * hf, 64 * hf + 64)
                    x = binp[rows, kt, PAD:POOLW - PAD]
                    v.scalar_tensor_tensor(x, wn[rows, PAD:POOLW - PAD], 1.0 / WINDOWS[2 * kt + hf], x, ALU.mult,
                                           ALU.subtract).then_inc(S("pooled"), 1)
            pool_edges(0)
            for n in range(6):
                kt, part = n // 3, n % 3
                b = filled(dve, l, "chan", n)
                z = BR[:, kt, 0:LAT].rearrange("p (m r) -> p r m", r=8)
                pb = PS[:, b, :].rearrange("p (r m) -> p r m", r=4)
                if part == 0:
                    ins = v.tensor_tensor(z[:, 0:4, :], pb, z[:, 0:4, :], ALU.mult)
                elif part == 1:
                    v.tensor_tensor(z[:, 4, :], pb[:, 0, :], z[:, 4, :], ALU.mult)
                    for r3 in range(3):
                        ins = v.tensor_tensor(z[:, 5 + r3, :], pb[:, 1 + r3, ::-1], z[:, 5 + r3, :], ALU.mult)
                else:
                    zp = BR[:, kt, LAT:TOK]
                    ins = v.tensor_tensor(zp, PS[:, b, 0:P], zp, ALU.mult)
                ins.then_inc(bank_free[b], 1)

            pool_edges(1)
            for n in range(6):
                kt, ch = n // 3, n % 3
                b = filled(dve, l, "pool", n)
                if n == 0:
                    read_out(dve, l, "feat", 6 * 3 - 1)
                x = BR[:, 2 + kt, ch * CH:(ch + 1) * CH]
                v.scalar_tensor_tensor(x, PS[:, b, 0:CH], vecT[:, 64 + 2 * l + kt:65 + 2 * l + kt], x, ALU.mult, ALU.mult)\
                    .then_inc(bank_free[b], 1)
            head_weights(0)
            head_weights(1)
            for kind in "qk":
                for i in range(3):
                    beside_dve(kind, 0, i)
            def maxes(m, c):
                b = filled(dve, l, "score", score_item(m, c))
                w = CH if parts(m) == 3 else P
                v.tensor_reduce(partmax[:, m % 2, c:c + 1], PS[:, b, 0:w], AX.X, ALU.max).then_inc(S("partmax"), 1)

            def negmaxes(m):
                dve.wait_ge(S("partmax"), l * HEADS * (3 * TT - 2) + score_item(m, parts(m) - 1) + 1)
                if m >= 2:
                    read_out(dve, l, "score", score_item(m - 2, parts(m - 2) - 1))
                v.tensor_reduce(negmax[:, m % 2:m % 2 + 1], partmax[:, m % 2, 0:parts(m)], AX.X, ALU.max, negate=True)\
                    .then_inc(S("negmax"), 1)

            def turned_low(m, gg):
                b = filled(dve, l, "attn", attn[("t", m, gg)])
                dve.wait_ge(S("pt_high"), l * HEADS * (3 * TT - 2) + score_item(m, gg) + 1)
                n = parts(m)
                v.tensor_tensor(turned_place(m, gg, 1), PS[:, b, 0:n * P].rearrange("p (k c) -> p k c", k=n),
                                turned_place(m, gg, 0).bitcast(F32), ALU.subtract).then_inc(bank_free[b], 1)

            def sum_inverses(m):
                read_out(dve, l, "score", score_item(m, parts(m) - 1))
                g = l * TILES + m
                v.tensor_reduce(rowsum[:, m % 2:m % 2 + 1], partsum[:, m % 2, 0:parts(m)], AX.X, ALU.add)\
                    .then_inc(S("rowsum"), 1)
                dve.wait_ge(S("rowsum"), g + 1)
                if m >= 2:
                    filled(dve, l, "attn", attn[("t", m - 2, parts(m - 2) - 1)])
                v.reciprocal(sum_inv[:, m % 2:m % 2 + 1], rowsum[:, m % 2:m % 2 + 1]).then_inc(S("sum_inv"), 1)

            def unmix(hh, gr):
                G = hh * GROUPS + gr
                g = l * HEADS * GROUPS + G
                w = 2 * P if gr < 4 else P
                b = filled(dve, l, "mixed", G)
                if g:
                    dve.wait_ge(S("gated"), g)
                rows = slice(VDIM * (hh % 2), VDIM * (hh % 2) + VDIM)
                sums = rinvT[rows, gr % 2, :] if gr < 4 else rinvTp[rows, :]
                v.tensor_tensor(mixed_out[rows, 0:w], PS[rows, b, 0:w], sums, ALU.mult).then_inc(bank_free[b], 1)

            maxes(0, 0)
            maxes(0, 1)
            for s in range(STEPS):
                if s < TILES:
                    maxes(s, parts(s) - 1)
                    negmaxes(s)
                for what, c in DVE_STEP:
                    if what == "sum" and 1 <= s <= TILES:
                        sum_inverses(s - 1)
                    if what == "unmix" and s and mixed_in(s - 1):
                        unmix(*mixed_in(s - 1))
                    if what == "beside" and s:
                        for it in beside(s - 1):
                            beside_dve(*it)
                    if what == "max" and s + 1 < TILES and c < parts(s + 1) - 1:
                        maxes(s + 1, c)
                    if what == "low" and turned(s - 1, c) is not None:
                        turned_low(s - 1, turned(s - 1, c))
                h, j = divmod(s, TT)
                if j == 7 and h + 2 < HEADS:
                    head_weights(h + 2)
            unmix(*mixed_in(STEPS - 1))
            def gate_diag(n):
                cond, hf = n // 2, n % 2
                if n:
                    filled(dve, l, "gbc", n - 1)
                for q in range(4):
                    f = 16 + 4 * hf + q
                    ins = v.tensor_scalar(diag[:, q, :], ident[:], modT[:, l % 2, f, cond:cond + 1], None, ALU.mult)
                ins.then_inc(S("diag"), 1)

            def y_low_odd(ch, j):
                sl = slice(ch * CH, (ch + 1) * CH)
                dve.wait_ge(S("y_high"), l * NCH * KF + Y_PIECES.index((ch, j)) + 1)
                v.tensor_tensor(XL[:, j, sl], Y[:, j, sl], XH[:, j, sl].bitcast(F32), ALU.subtract)\
                    .then_inc(S("y_low_odd"), 1)

            for j in range(KF):
                for b3 in range(3):
                    u = 3 * j + b3
                    if u == 3 * KF - 1:
                        if l == 0:
                            dve.wait_ge(S("mod_ready"), 8)
                        gate_diag(0)
                        for n in range(4):
                            if n < 3:
                                gate_diag(n + 1)
                            if n == 0:
                                filled(dve, l, "gate", 3 * u - 1)
                            b = filled(dve, l, "gbc", n)
                            v.tensor_copy(gateB[:, n // 2, (n % 2) * 512:(n % 2) * 512 + 512], PS[:, b, :])\
                                .then_inc(bank_free[b], 1)
                            if n < NCH:
                                for jj in (1, 3, 5):
                                    y_low_odd(n, jj)
                    for ch in range(NCH):
                        n = u * 3 + ch
                        read_out(dve, l, "gate", n)
                        b = filled(dve, l, "branch", n)
                        sl = slice(ch * CH, (ch + 1) * CH)
                        if b3 == 0:
                            dst = Y[:, j, sl]
                        else:
                            q = 6 * j + (b3 - 1) * 3 + ch
                            if q >= 2:
                                dve.wait_ge(S("y_sum"), 48 * l + q - 1)
                            dst = prod[:, q % 2, :]
                        v.tensor_tensor(dst, PS[:, b, 0:CH], sig[:, ch, :], ALU.mult).then_inc(bank_free[b], 1)
                    if u == 3 * KF - 1:
                        for ch in range(NCH):
                            y_low_odd(ch, KF - 1)
                    if l == 0:
                        for n in (later(u - 1) if u else ()):
                            later_modulation(n)
                        for n in later(u):
                            mod_products(n)
            for n in range(4):
                read_out(dve, l, "gbc", n)
            for p in range(4):
                for t in range(TT):
                    n = p * TT + t
                    b = filled(dve, l, "out", n)
                    if n >= 2:
                        dve.wait_ge(S("rows_added"), 4 * TT * l + n - 1)
                    v.tensor_tensor(tmpw[:, n % 2, :], PS[:, b, 0:256], gateB[:, int(t == 8), p * 256:(p + 1) * 256],
                                    ALU.mult).then_inc(bank_free[b], 1)
                    if l + 1 < DEPTH and p == 3:
                        if t == 4:
                            norm_scale(l + 1, 0)
                        if t in NORM_IN_OUT:
                            norm_dve(l + 1, *NORM_IN_OUT[t])
                    if l + 1 == DEPTH and p == 3 and t in (4, 7):
                        norm_scale(DEPTH, (t - 4) // 3, final=True)
                if l == 0 and p == 0:
                    for n in later(3 * KF - 1):
                        later_modulation(n)
                    dve.wait_ge(S("mod_ready"), len(LATER))
                    scales(1)
            if l + 1 == DEPTH:
                norm_scale(DEPTH, 2, final=True)

    @block.tensor
    def _(pe):
        mm = nc.tensor.matmul

        def three_pass(out, wh, wl, xh, xl, first, last):
            mm(out, wh, xh, start=first, stop=False)
            mm(out, wh, xl, start=False, stop=False)
            return mm(out, wl, xh, start=False, stop=last)

        def mod_item(m):
            b = pe_takes(pe, 0, "mod", m)
            nu = unit_at[("mod", 0, m)]
            arrived(pe, nu)
            for k in range(KF):
                ins = mm(PS[0:2, b, 0:P], silu_c[:, k, :], raw[:, nu % 4, k, :], start=(k == 0), stop=(k == KF - 1))
            ins.then_inc(bank_full[b], 1)

        def mod_rows(n):
            b = pe_takes(pe, 0, *later_item(n))
            pe.wait_ge(S("mod_sum"), 16 * (n + 1))
            for cond in range(2):
                ins = nc.tensor.transpose(PS[:, b, cond * P:(cond + 1) * P], mod_sums[:, n % 2, cond, :], ident[:])
            ins.then_inc(bank_full[b], 1)

        def norm_turn(l, ch, f0, f1):
            if f0 == 0:
                pe.wait_ge(S("xhat"), 9 * l + CT * (ch + 1))
            for f in range(f0, f1):
                b = pe_takes(pe, l, "norm", ch * KF + f)
                for tt in range(CT):
                    ins = nc.tensor.transpose(PS[:, b, tt * P:(tt + 1) * P], xhat[:, tt, f * P:(f + 1) * P], ident[:])
                ins.then_inc(bank_full[b], 1)

        pe.wait_ge(S("ident_in"), 16)
        pe.wait_ge(S("ones"), 1)
        pe.wait_ge(S("vec_in"), 16 * 6)
        nc.tensor.transpose(PS[:, 6, 0:84], vec_rows[0:84, :], ident[0:84, 0:84]).then_inc(bank_full[6], 1)
        pe.wait_ge(S("silu_c"), 2)
        for m in range(16):
            mod_item(m)
        for m in range(10, 16):
            read_out(pe, 0, "mod", m)
        for m in range(16):
            ins = nc.tensor.transpose(PS[:, 6, 2 * m:2 * m + 2], mod_flat[0:2, m, :], ident[0:2, 0:2])
        ins.then_inc(bank_full[6], 1)
        norm_turn(0, 0, 0, KF)

        for l in range(DEPTH):
            for p in range(3):
                pe.wait_ge(S("split_low"), split_k[("tok", l, 2 * p + 1)] + 1)
                w = bs[:, 2 * (p % 2):2 * (p % 2) + 2]
                for t in range(TT):
                    if p == 0 and t % CT == 0:
                        low_done(pe, KF * (l * NCH + t // CT + 1))
                    b = pe_takes(pe, l, "tok", p * TT + t)
                    sl = slice(t * P, (t + 1) * P)
                    out = PS[:, b, 0:256]
                    for k in range(KF):
                        if p == 0 and t in NORM_IN_ROWS:
                            norm_turn(l, NORM_IN_ROWS[t], k, k + 1)
                        ins = three_pass(out, XH[:, k, sl], XL[:, k, sl], w[:, :, 0, k, :], w[:, :, 1, k, :],
                                         k == 0, k == KF - 1)
                    ins.then_inc(bank_full[b], 1)
            def columns(phase, l, u, ch, n):
                b = pe_takes(pe, l, phase, n)
                sl = slice(ch * CH, (ch + 1) * CH)
                for k in range(KF):
                    ins = three_pass(PS[:, b, 0:CH], ws[:, u % 2, 0, k, :], ws[:, u % 2, 1, k, :], XH[:, k, sl],
                                     XL[:, k, sl], k == 0, k == KF - 1)
                ins.then_inc(bank_full[b], 1)
            for u in range(10):
                pe.wait_ge(S("split_low"), split_k[("feat", l, u)] + 1)
                for ch in range(NCH):
                    columns("feat", l, u, ch, 3 * u + ch)
            pe.wait_ge(S("lat_ready"), l + 1)
            for n in range(6):
                kt, ch = n // 3, n % 3
                b = pe_takes(pe, l, "turn", n)
                for tt in range(CT):
                    ins = nc.tensor.transpose(PS[:, b, tt * P:(tt + 1) * P], qlat[:, ch * CT + tt, kt * P:(kt + 1) * P], ident[:])
                ins.then_inc(bank_full[b], 1)
            for kind in range(2):
                for n in range(4):
                    b = pe_takes(pe, l, "turn", 6 + 4 * kind + n)
                    for s in range(3 * n, min(3 * n + 3, KS)):
                        src = kvk[:, s, 0:P] if kind == 0 else kvk[:, s, KVW - P:KVW]
                        ins = nc.tensor.transpose(PS[:, b, (s - 3 * n) * P:(s - 3 * n + 1) * P], src, ident[:])
                    ins.then_inc(bank_full[b], 1)
            for n in range(4):
                read_out(pe, l, "turn", 6 + n)
            wv = wkv[:].rearrange("p (h c) -> p h c", c=P)[:, :, NOPE:P]
            for s in range(KS):
                b = pe_takes(pe, l, "val", s)
                mm(PS[:, b, :], ckvT[:, s * P:(s + 1) * P], wv, start=True, stop=True).then_inc(bank_full[b], 1)
            pe.wait_ge(S("dft_in"), 32 * (l + 1))
            pe.wait_ge(S("dft8"), 8 * (l + 1))
            for n in range(12):
                r, kt = n // 2, n % 2
                ks = slice(kt * P, (kt + 1) * P)
                b = pe_takes(pe, l, "seq", n)
                out = PS[:, b, 0:256]
                if r in (0, 4):
                    ins = mm(out, U[:, r // 4, ks], seq_dft[:, 6 + r // 4, :], start=True, stop=True)
                elif r == 5:
                    ins = mm(out, atok[:, 8, ks], seq_dft[:, 8, :], start=True, stop=True)
                else:
                    mm(out, U[:, 2 * r, ks], seq_dft[:, r - 1, :], start=True, stop=False)
                    ins = mm(out, U[:, 2 * r + 1, ks], seq_dft[:, r + 2, :], start=False, stop=True)
                ins.then_inc(bank_full[b], 1)
            for n in range(10, 12):
                read_out(pe, l, "seq", n)
            cd, sd, nsd = chan_dft[:, 0, :], chan_dft[:, 1, :], chan_dft[:, 2, :]
            for n in range(6):
                kt, part = n // 3, n % 3
                b = pe_takes(pe, l, "chan", n)
                if part == 0:
                    mm(PS[:, b, :], cd, XR[:, kt, 0, 0:4, :], start=True, stop=False)
                    ins = mm(PS[:, b, :], sd, XR[:, kt, 1, 0:4, :], start=False, stop=True)
                elif part == 1:
                    for q in range(4):
                        out = PS[:, b, q * P:(q + 1) * P]
                        mm(out, cd, XR[:, kt, 0, 4 - q, :], start=True, stop=False)
                        ins = mm(out, nsd if q else sd, XR[:, kt, 1, 4 - q, :], start=False, stop=True)
                else:
                    mm(PS[:, b, 0:P], cd, XR[:, kt, 0, 5, :], start=True, stop=False)
                    ins = mm(PS[:, b, 0:P], sd, XR[:, kt, 1, 5, :], start=False, stop=True)
                ins.then_inc(bank_full[b], 1)
            def beside_pe(kind, h, i):
                it = attn[(kind, h, i)]
                b = pe_takes(pe, l, "attn", it)
                if kind == "q":
                    if i == 0:
                        pe.wait_ge(S("wq_ready"), l * HEADS + h + 1)
                    sl = slice(i * CH, (i + 1) * CH)
                    for k in range(2):
                        ins = mm(PS[:, b, 0:CH], wq[:, h % 2, k, :], qhatT[:, k, sl], start=(k == 0), stop=(k == 1))
                else:
                    c0, c1 = K_CHUNKS[i]
                    ins = mm(PS[0:NOPE, b, 0:c1 - c0], wkv[:, h * P:h * P + NOPE], ckvT[:, c0:c1], start=True, stop=True)
                ins.then_inc(bank_full[b], 1)

            def scores(m, c):
                h, j = divmod(m, TT)
                if j == 0 and c == 0:
                    pe.wait_ge(S("q_low"), (l * HEADS + h + 1) * 3)
                    for i in range(3):
                        read_out(pe, l, "attn", attn[("k", h, i)])
                u = h % 2
                qs = slice(j * P, (j + 1) * P)
                ks = slice(9 * P, 10 * P) if j == 8 else slice(c * CH, (c + 1) * CH)
                b = pe_takes(pe, l, "score", score_item(m, c))
                three_pass(PS[:, b, 0:P if j == 8 else CH], qT[:, u, 0, qs], qT[:, u, 1, qs], kT[:, u, 0, ks],
                           kT[:, u, 1, ks], True, True).then_inc(bank_full[b], 1)

            def turn(m, gg):
                read_out(pe, l, "score", score_item(m, gg))
                b = pe_takes(pe, l, "attn", attn[("t", m, gg)])
                for q in range(parts(m)):
                    ins = nc.tensor.transpose(PS[:, b, q * P:(q + 1) * P],
                                              (P0, P1)[m % 2][:, (3 * gg + q) * P:(3 * gg + q + 1) * P], ident[:])
                if gg == parts(m) - 1:
                    pe.wait_ge(S("sum_inv"), l * TILES + m + 1)
                    ins = nc.tensor.transpose(PS[:, b, CH:CH + P], sum_inv[:, m % 2:m % 2 + 1].broadcast_to([P, P]), ident[:])
                ins.then_inc(bank_full[b], 1)

            def mix(hh, gr, kts):
                G = hh * GROUPS + gr
                if kts[0] == 0:
                    pe_takes(pe, l, "mixed", G)
                    if gr in (0, 4):
                        pe.wait_ge(S("v_ready"), l * HEADS + 2 * (hh // 2) + (1 if gr == 0 else 2))
                w = 2 * P if gr < 4 else P
                b = item(l, "mixed", G)[0]
                for kt in kts:
                    if kt % 3 == 0:
                        for j in ((2 * gr, 2 * gr + 1) if gr < 4 else (8,)):
                            read_out(pe, l, "attn", attn[("t", hh * TT + j, kt // 3)])
                    if gr < 4:
                        sl, xh, xl = kt, PT[:, gr % 2, 0, kt, :], PT[:, gr % 2, 1, kt, :]
                    else:
                        sl, xh, xl = 9, PTp[:, 0, :], PTp[:, 1, :]
                    last = kt == 8 or gr == 4
                    ins = three_pass(PS[:, b, 0:w], vh[:, 0, sl, :], vh[:, 1, sl, :], xh, xl, kt == 0, last)
                if last:
                    ins.then_inc(bank_full[b], 1)

            for n in range(6):
                read_out(pe, l, "chan", n)
            pe.wait_ge(S("small_in"), SMALL * (l + 1))
            for n in range(6):
                kt, ch = n // 3, n % 3
                pe.wait_ge(S("pooled"), 4 * l + 2 * kt + 2)
                b = pe_takes(pe, l, "pool", n)
                for cond, c0, c1 in cond_parts(ch):
                    o = SAMPLE0 + ch * CH if cond == 0 else PROMPT0 - c0
                    ins = mm(PS[:, b, c0:c1], pool_mat[:, kt, :], binp[:, kt, o + c0:o + c1], start=True, stop=True)
                ins.then_inc(bank_full[b], 1)
            for kind in "qk":
                for i in range(3):
                    beside_pe(kind, 0, i)
            for c in range(3):
                scores(0, c)
            for s in range(STEPS):
                for what, c in PE_STEP:
                    if what == "score" and s + 1 < TILES and c < parts(s + 1):
                        scores(s + 1, c)
                    if what == "turn" and turned(s - 1, c) is not None:
                        turn(s - 1, turned(s - 1, c))
                    if what == "mix" and mix_slots(s)[c]:
                        mix(*mix_slots(s)[c])
                for it in beside(s):
                    beside_pe(*it)
            def gate_rows(n):
                pe.wait_ge(S("diag"), 4 * l + n + 1)
                b = pe_takes(pe, l, "gbc", n)
                mm(PS[:, b, :], ones[:], diag[:].rearrange("p q m -> p (q m)"), start=True, stop=True)\
                    .then_inc(bank_full[b], 1)

            for j in range(KF):
                for b3 in range(3):
                    u = 3 * j + b3
                    pe.wait_ge(S("split_low"), split_k[("gate", l, u)] + 1)
                    for ch in range(NCH):
                        if u == 0:
                            if ch == 0:
                                pe.wait_ge(S("xn_back"), 64 * (l + 1))
                            pe.wait_ge(S(f"xn_back{ch}"), 16 * (l + 1))
                        columns("gate", l, u, ch, 3 * u + ch)
                        if u == 3 * KF - 1:
                            gate_rows(ch)
                    if u == 3 * KF - 1:
                        gate_rows(3)
                    for n in (later(u - 1) if l == 0 and u else ()):
                        mod_rows(n)
                    pe.wait_ge(S(f"branch_in{j % 2}"), 48 * (l * KF // 2 + j // 2 + 1))
                    k0, k1 = ((0, 2), (2, 4), (4, 8))[b3]
                    if j == 0 and b3 == 2:
                        pe.wait_ge(S("gated"), HEADS * GROUPS * (l + 1))
                    for ch in range(NCH):
                        b = pe_takes(pe, l, "branch", 3 * u + ch)
                        for k in range(k0, k1):
                            ins = mm(PS[:, b, 0:CH], wbr[:, j % 2, k, :], BR[:, k, ch * CH:(ch + 1) * CH],
                                     start=(k == k0), stop=(k == k1 - 1))
                        ins.then_inc(bank_full[b], 1)
            for p in range(4):
                pe.wait_ge(S("split_low"), split_k[("out", l, 2 * p + 1)] + 1)
                w = bs[:, 2 * (p % 2):2 * (p % 2) + 2]
                for t in range(TT):
                    if p == 0 and t % CT == 0:
                        y_low_done(pe, l, t // CT)
                    b = pe_takes(pe, l, "out", p * TT + t)
                    sl = slice(t * P, (t + 1) * P)
                    for k in range(KF):
                        ins = three_pass(PS[:, b, 0:256], XH[:, k, sl], XL[:, k, sl], w[:, :, 0, k, :], w[:, :, 1, k, :],
                                         k == 0, k == KF - 1)
                    ins.then_inc(bank_full[b], 1)
                    if l == 0 and p == 0 and t == 2:
                        for n in later(3 * KF - 1):
                            mod_rows(n)
                    if l + 1 < DEPTH and p == 3 and t in NORM_IN_OUT:
                        norm_turn(l + 1, *NORM_IN_OUT[t])

    block_cm.__exit__(None, None, None)


_INS = ["x_prompt", "x_sample", "cache_ckv", "cache_krope", "c", "c_ctx", "norm_g", "w_mod", "b_mod", "w_in",
        "pool_w", "pool_scale", "q_norm_g", "w_q_up", "kv_norm_g", "w_kv_up", "w_br_a", "w_br_b", "w_br_c",
        "w_out", "final_norm_g"]
_OUTS = [(1, SEQ, D), (1, LAT, D), (1, DEPTH, SEQ, KVR), (1, DEPTH, SEQ, ROPE)]


def kernel(**inputs):
    import numpy as _np
    import concourse.bacc as _bacc
    from concourse import mybir as _mybir
    from concourse.bass_utils import run_bass_kernel_spmd as _run

    nc = _bacc.Bacc("TRN2", target_bir_lowering=False, num_devices=1)
    arrays, args, tab = {}, [], {}
    for name in _INS:
        a = _np.ascontiguousarray(inputs[name])
        arrays[f"in_{name}"] = a
        args.append(nc.dram_tensor(f"in_{name}", a.shape, _mybir.dt.from_np(a.dtype), kind="ExternalInput").ap())
    for name, a in make_tables().items():
        a = _np.ascontiguousarray(a, dtype=_np.float32)
        arrays[f"tab_{name}"] = a
        tab[name] = nc.dram_tensor(f"tab_{name}", a.shape, _mybir.dt.float32, kind="ExternalInput").ap()
    outs = [nc.dram_tensor(f"out_{i}", s, _mybir.dt.float32, kind="ExternalOutput").ap() for i, s in enumerate(_OUTS)]
    park = [nc.dram_tensor(n, s, _mybir.dt.float32).ap()
            for n, s in (("park_high", (P, KF, TOK)), ("park_low", (P, KF, TOK)), ("rows_mid", (P, TT, D)))]
    hybrid_step(nc, *args, tab, *outs, *park)
    r = _run(nc, [arrays], core_ids=[0])
    return tuple(r.results[0][f"out_{i}"] for i in range(len(_OUTS)))
```
